# Optimizing a Trainium2 kernel written in Bass

```python
import jax, jax.numpy as jnp
from jax import lax
import numpy as np
import math

D_MODEL = 1024
BATCH = 1
SEQ = 256
DEPTH = 1

CHUNK = 64
N_MEM = 256
HEAD_DIM = 64
D_MIX = D_MODEL
FOX_HEADS = D_MIX // 2 // HEAD_DIM
CHK_HEADS = D_MIX // 2 // HEAD_DIM
D_FOX = FOX_HEADS * HEAD_DIM
D_CHK = CHK_HEADS * HEAD_DIM
LEFT_CHUNKS = 8
BAND = (LEFT_CHUNKS + 1) * CHUNK
MAX_REL = 128
N_REL = 2 * MAX_REL + 1
Q_BLOCK = 128
MEM_HEADS = 4
MEM_HEAD_DIM = D_MODEL // MEM_HEADS
D_FF = 4 * D_MODEL
EPS = 1e-6
D_IN = 3 * D_FOX + FOX_HEADS + 3 * D_CHK


def rmsnorm(x, g):
    xf = x.astype(jnp.float32)
    y = xf * lax.rsqrt(jnp.mean(xf * xf, axis=-1, keepdims=True) + EPS) * g.astype(jnp.float32)
    return y.astype(x.dtype)

def forgetting_attention(q, k, v, f_logit):
    S = q.shape[1]
    Dh = q.shape[-1]
    scale = Dh ** -0.5
    logf = jax.nn.log_sigmoid(f_logit.astype(jnp.float32))
    c = jnp.cumsum(logf, axis=1).transpose(0, 2, 1)
    pos = jnp.arange(S)
    outs = []
    for i in range(S // Q_BLOCK):
        q0, q1 = i * Q_BLOCK, (i + 1) * Q_BLOCK
        qb = q[:, q0:q1]
        kb = k[:, :q1]
        vb = v[:, :q1]
        logits = jnp.einsum('bqhd,bkhd->bhqk', qb, kb).astype(jnp.float32) * scale
        logits = logits + c[:, :, q0:q1, None] - c[:, :, None, :q1]
        causal = pos[q0:q1, None] >= pos[None, :q1]
        logits = jnp.where(causal[None, None], logits, -jnp.inf)
        p = jax.nn.softmax(logits, axis=-1).astype(v.dtype)
        outs.append(jnp.einsum('bhqk,bkhd->bqhd', p, vb))
    return jnp.concatenate(outs, axis=1)

def _rel_index():
    i = np.arange(CHUNK)[:, None]
    m = np.arange(BAND)[None, :]
    rel = i + LEFT_CHUNKS * CHUNK - m
    return np.clip(rel, -MAX_REL, MAX_REL) + MAX_REL

def chunked_relpos_attention(q, k, v, rel_table):
    B, S, H, Dh = q.shape
    NC = S // CHUNK
    scale = Dh ** -0.5
    qc = q.reshape(B, NC, CHUNK, H, Dh)
    pad = ((0, 0), (LEFT_CHUNKS * CHUNK, 0), (0, 0), (0, 0))
    kp = jnp.pad(k, pad).reshape(B, NC + LEFT_CHUNKS, CHUNK, H, Dh)
    vp = jnp.pad(v, pad).reshape(B, NC + LEFT_CHUNKS, CHUNK, H, Dh)
    kband = jnp.concatenate([kp[:, j:j + NC] for j in range(LEFT_CHUNKS + 1)], axis=2)
    vband = jnp.concatenate([vp[:, j:j + NC] for j in range(LEFT_CHUNKS + 1)], axis=2)
    bias = rel_table.astype(jnp.float32)[:, _rel_index()]
    key_pos = jnp.arange(NC)[:, None] * CHUNK + jnp.arange(BAND)[None, :] - LEFT_CHUNKS * CHUNK
    valid = key_pos >= 0
    logits = jnp.einsum('bcqhd,bckhd->bhcqk', qc, kband).astype(jnp.float32) * scale
    logits = logits + bias[None, :, None]
    logits = jnp.where(valid[None, None, :, None, :], logits, -jnp.inf)
    p = jax.nn.softmax(logits, axis=-1).astype(v.dtype)
    out = jnp.einsum('bhcqk,bckhd->bcqhd', p, vband)
    return out.reshape(B, S, H, Dh)

def memory_cross_attention(h, mem_n, w_mq, w_mk, w_mv, w_mo):
    B, S, _ = h.shape
    M = mem_n.shape[1]
    q = (h @ w_mq).reshape(B, S, MEM_HEADS, MEM_HEAD_DIM)
    k = (mem_n @ w_mk).reshape(B, M, MEM_HEADS, MEM_HEAD_DIM)
    v = (mem_n @ w_mv).reshape(B, M, MEM_HEADS, MEM_HEAD_DIM)
    logits = jnp.einsum('bshd,bmhd->bhsm', q, k).astype(jnp.float32) * (MEM_HEAD_DIM ** -0.5)
    p = jax.nn.softmax(logits, axis=-1).astype(v.dtype)
    o = jnp.einsum('bhsm,bmhd->bshd', p, v).reshape(B, S, D_MODEL)
    return o @ w_mo

def first_inputs(seed: int = 0) -> dict:
    key = jax.random.key(seed)
    ks = jax.random.split(key, 24)
    f32 = jnp.float32

    def w(k, shape, fan_in):
        return jax.random.normal(k, shape, f32) * fan_in ** -0.5

    def gain(k, n):
        return 1.0 + 0.05 * jax.random.normal(k, (DEPTH, n), f32)

    return {
        'x': jax.random.normal(ks[0], (BATCH, SEQ, D_MODEL), f32),
        'mem': jax.random.normal(ks[1], (BATCH, N_MEM, D_MODEL), f32),
        'w_in': w(ks[2], (DEPTH, D_MODEL, D_IN), D_MODEL),
        'b_fgt': 3.0 + 0.1 * jax.random.normal(ks[3], (DEPTH, FOX_HEADS), f32),
        'rel_bias': 0.2 * jax.random.normal(ks[4], (DEPTH, CHK_HEADS, N_REL), f32),
        'g_fox_out': gain(ks[5], D_FOX),
        'g_chk_out': gain(ks[6], D_CHK),
        'w_out': w(ks[7], (DEPTH, D_MIX, D_MODEL), D_MIX),
        'g_mix_pre': gain(ks[8], D_MODEL),
        'g_mix_post': gain(ks[9], D_MODEL),
        'g_mem_kv': gain(ks[10], D_MODEL),
        'w_mq': w(ks[11], (DEPTH, D_MODEL, D_MODEL), D_MODEL),
        'w_mk': w(ks[12], (DEPTH, D_MODEL, D_MODEL), D_MODEL),
        'w_mv': w(ks[13], (DEPTH, D_MODEL, D_MODEL), D_MODEL),
        'w_mo': w(ks[14], (DEPTH, D_MODEL, D_MODEL), D_MODEL),
        'g_mem_pre': gain(ks[15], D_MODEL),
        'g_mem_post': gain(ks[16], D_MODEL),
        'w_ff1': w(ks[17], (DEPTH, D_MODEL, D_FF), D_MODEL),
        'w_ff2': w(ks[18], (DEPTH, D_FF, D_MODEL), D_FF),
        'g_ff_pre': gain(ks[19], D_MODEL),
        'g_ff_post': gain(ks[20], D_MODEL),
    }

def first_block(x, mem, w_in, b_fgt, rel_bias, g_fox_out, g_chk_out, w_out, g_mix_pre, g_mix_post,
              g_mem_kv, w_mq, w_mk, w_mv, w_mo, g_mem_pre, g_mem_post,
              w_ff1, w_ff2, g_ff_pre, g_ff_post):
    B, S, _ = x.shape
    for l in range(DEPTH):
        h = rmsnorm(x, g_mix_pre[l])
        proj = h @ w_in[l]
        o0 = 0
        fq = proj[..., o0:o0 + D_FOX]; o0 += D_FOX
        fk = proj[..., o0:o0 + D_FOX]; o0 += D_FOX
        fv = proj[..., o0:o0 + D_FOX]; o0 += D_FOX
        f_logit = proj[..., o0:o0 + FOX_HEADS] + b_fgt[l]; o0 += FOX_HEADS
        cq = proj[..., o0:o0 + D_CHK]; o0 += D_CHK
        ck = proj[..., o0:o0 + D_CHK]; o0 += D_CHK
        cv = proj[..., o0:o0 + D_CHK]
        shp_f = (B, S, FOX_HEADS, HEAD_DIM)
        shp_c = (B, S, CHK_HEADS, HEAD_DIM)
        y_fox = forgetting_attention(fq.reshape(shp_f), fk.reshape(shp_f), fv.reshape(shp_f), f_logit)
        y_chk = chunked_relpos_attention(cq.reshape(shp_c), ck.reshape(shp_c), cv.reshape(shp_c), rel_bias[l])
        y = jnp.concatenate([rmsnorm(y_fox.reshape(B, S, D_FOX), g_fox_out[l]),
                             rmsnorm(y_chk.reshape(B, S, D_CHK), g_chk_out[l])], axis=-1)
        x = x + rmsnorm(y @ w_out[l], g_mix_post[l])
        h = rmsnorm(x, g_mem_pre[l])
        mem_n = rmsnorm(mem, g_mem_kv[l])
        y = memory_cross_attention(h, mem_n, w_mq[l], w_mk[l], w_mv[l], w_mo[l])
        x = x + rmsnorm(y, g_mem_post[l])
        h = rmsnorm(x, g_ff_pre[l])
        y = jnp.square(jax.nn.relu(h @ w_ff1[l])) @ w_ff2[l]
        x = x + rmsnorm(y, g_ff_post[l])
    return x


GDN_HEAD_K = 128
GDN_HEAD_V = 128
GDN_HEADS = D_MODEL // GDN_HEAD_V
GDN_CONV = 4
GDN_CHUNK = 64
GDN_QK_DIM = GDN_HEADS * GDN_HEAD_K
GDN_V_DIM = GDN_HEADS * GDN_HEAD_V
GDN_CONV_DIM = 2 * GDN_QK_DIM + GDN_V_DIM

ATT_HEAD_DIM = 128
ATT_HEADS = D_MODEL // ATT_HEAD_DIM
ATT_KV_HEADS = 2
ATT_Q_DIM = ATT_HEADS * ATT_HEAD_DIM
ATT_KV_DIM = ATT_KV_HEADS * ATT_HEAD_DIM
IDX_HEADS = 8
IDX_DIM = 64
TOPK_MAX = 256

ROPE_THETA = 500000.0
ROPE_FRACTION = 4
D_FF_2 = 4 * D_MODEL

IN_SPLITS = (GDN_CONV_DIM, GDN_V_DIM, GDN_HEADS, GDN_HEADS,
             ATT_Q_DIM, ATT_KV_DIM, ATT_KV_DIM,
             IDX_HEADS * IDX_DIM, IDX_DIM, IDX_HEADS,
             D_MODEL, D_MODEL)
IN_PROJ_DIM = (GDN_CONV_DIM + GDN_V_DIM + 2 * GDN_HEADS + ATT_Q_DIM + 2 * ATT_KV_DIM
               + IDX_HEADS * IDX_DIM + IDX_DIM + IDX_HEADS + 2 * D_MODEL)


def rms_norm(x, g):
    xf = x.astype(jnp.float32)
    y = xf * lax.rsqrt(jnp.mean(xf * xf, axis=-1, keepdims=True) + EPS)
    return (y * g.astype(jnp.float32)).astype(x.dtype)

def l2_normalize(x):
    xf = x.astype(jnp.float32)
    return xf * lax.rsqrt(jnp.sum(xf * xf, axis=-1, keepdims=True) + EPS)

def rope_tables(seq, rot_dim):
    inv_freq = ROPE_THETA ** (-jnp.arange(0, rot_dim, 2, dtype=jnp.float32) / rot_dim)
    ang = jnp.arange(seq, dtype=jnp.float32)[:, None] * inv_freq[None, :]
    return jnp.cos(ang), jnp.sin(ang)

def apply_partial_rope(t, cos, sin):
    half = cos.shape[-1]
    shape = (t.shape[1],) + (1,) * (t.ndim - 3) + (half,)
    c, s = cos.reshape(shape), sin.reshape(shape)
    tf = t.astype(jnp.float32)
    x1, x2 = tf[..., :half], tf[..., half:2 * half]
    out = jnp.concatenate([x1 * c - x2 * s, x2 * c + x1 * s, tf[..., 2 * half:]], axis=-1)
    return out.astype(t.dtype)

def causal_short_conv(u, w):
    k = w.shape[0]
    s = u.shape[1]
    up = jnp.pad(u, ((0, 0), (k - 1, 0), (0, 0)))
    y = up[:, 0:s] * w[0]
    for j in range(1, k):
        y = y + up[:, j:j + s] * w[j]
    return y

def gated_delta_rule_chunked(q, k, v, g, beta):
    B, S, H, dk = q.shape
    dv = v.shape[-1]
    C = GDN_CHUNK
    N = S // C
    f32 = jnp.float32

    def chunks(t):
        t = jnp.swapaxes(t.astype(f32), 1, 2)
        return t.reshape((B, H, N, C) + t.shape[3:])

    q, k, v, g, beta = chunks(q), chunks(k), chunks(v), chunks(g), chunks(beta)
    g_cum = jnp.cumsum(g, axis=-1)
    pos = jnp.arange(C)
    incl = pos[:, None] >= pos[None, :]
    strict = pos[:, None] > pos[None, :]
    diff = g_cum[..., :, None] - g_cum[..., None, :]
    decay = jnp.where(incl, jnp.exp(jnp.where(incl, diff, 0.0)), 0.0)
    k_beta = k * beta[..., None]
    a_mat = jnp.where(strict, jnp.einsum('bhnid,bhnjd->bhnij', k_beta, k) * decay, 0.0)
    lhs = a_mat + jnp.eye(C, dtype=f32)
    rhs = jnp.concatenate([v * beta[..., None], k_beta * jnp.exp(g_cum)[..., None]], axis=-1)
    sol = lax.linalg.triangular_solve(lhs, rhs, left_side=True, lower=True, unit_diagonal=True)
    u, w = sol[..., :dv], sol[..., dv:]
    qk = jnp.where(incl, jnp.einsum('bhnid,bhnjd->bhnij', q, k) * decay, 0.0)
    q_dec = q * jnp.exp(g_cum)[..., None]
    g_last = g_cum[..., -1]
    k_dec = k * jnp.exp(g_last[..., None] - g_cum)[..., None]

    def step(state, xs):
        u_n, w_n, qk_n, q_n, k_n, gl_n = xs
        v_new = u_n - jnp.einsum('bhcd,bhde->bhce', w_n, state)
        o_n = (jnp.einsum('bhcd,bhde->bhce', q_n, state)
               + jnp.einsum('bhij,bhje->bhie', qk_n, v_new))
        state = state * jnp.exp(gl_n)[..., None, None] + jnp.einsum('bhcd,bhce->bhde', k_n, v_new)
        return state, o_n

    xs = tuple(jnp.moveaxis(t, 2, 0) for t in (u, w, qk, q_dec, k_dec, g_last))
    state0 = jnp.zeros((B, H, dk, dv), f32)
    _, o = lax.scan(step, state0, xs)
    o = jnp.moveaxis(o, 0, 2).reshape(B, H, S, dv)
    return jnp.swapaxes(o, 1, 2)

def dsa_sparse_attention(q, k, v, q_idx, k_idx, w_idx):
    B, S, H, hd = q.shape
    kvh = k.shape[2]
    grp = H // kvh
    n_blk = S // Q_BLOCK
    k_sel = min(TOPK_MAX, S // 4)
    scale = hd ** -0.5
    key_pos = jnp.arange(S, dtype=jnp.int32)
    k_idx_f = k_idx.astype(jnp.float32)

    def to_blocks(t):
        return jnp.moveaxis(t.reshape((B, n_blk, Q_BLOCK) + t.shape[2:]), 1, 0)

    def block(args):
        blk, qb, qib, wb = args
        t = blk * Q_BLOCK + jnp.arange(Q_BLOCK, dtype=jnp.int32)
        logits = jnp.einsum('bqhd,bsd->bqhs', qib.astype(jnp.float32), k_idx_f)
        score = jnp.einsum('bqh,bqhs->bqs', wb.astype(jnp.float32), jax.nn.relu(logits))
        causal = key_pos[None, :] <= t[:, None]
        score = jnp.where(causal[None], score, -jnp.inf)
        _, sel = lax.top_k(score, k_sel)
        valid = sel <= t[None, :, None]
        k_g = jax.vmap(lambda kb, ib: kb[ib])(k, sel)
        v_g = jax.vmap(lambda vb, ib: vb[ib])(v, sel)
        qg = qb.reshape(B, Q_BLOCK, kvh, grp, hd)
        s = jnp.einsum('bqcgd,bqncd->bqcgn', qg, k_g).astype(jnp.float32) * scale
        s = jnp.where(valid[:, :, None, None, :], s, -jnp.inf)
        p = jax.nn.softmax(s, axis=-1).astype(v_g.dtype)
        o = jnp.einsum('bqcgn,bqncd->bqcgd', p, v_g)
        return o.reshape(B, Q_BLOCK, H * hd)

    o = lax.map(block, (jnp.arange(n_blk, dtype=jnp.int32), to_blocks(q),
                        to_blocks(q_idx), to_blocks(w_idx)))
    return jnp.moveaxis(o, 0, 1).reshape(B, S, H * hd)

def hybrid_layer(x, norm_mix_g, w_in, conv_w, a_log, dt_bias, gdn_norm_g,
                 q_norm_g, k_norm_g, w_out, norm_mlp_g, w_mlp_up, w_mlp_down):
    B, S, _ = x.shape
    h = rms_norm(x, norm_mix_g)
    proj = h @ w_in
    points = np.cumsum(np.array(IN_SPLITS))[:-1].tolist()
    (g_qkv, g_z, g_a, g_b, a_q, a_k, a_v,
     i_q, i_k, i_w, gate_a, gate_b) = jnp.split(proj, points, axis=-1)

    qkv = jax.nn.silu(causal_short_conv(g_qkv, conv_w))
    gq, gk, gv = jnp.split(qkv, [GDN_QK_DIM, 2 * GDN_QK_DIM], axis=-1)
    gq = l2_normalize(gq.reshape(B, S, GDN_HEADS, GDN_HEAD_K)) * (GDN_HEAD_K ** -0.5)
    gk = l2_normalize(gk.reshape(B, S, GDN_HEADS, GDN_HEAD_K))
    gv = gv.reshape(B, S, GDN_HEADS, GDN_HEAD_V)
    beta = jax.nn.sigmoid(g_b.astype(jnp.float32))
    g = -jnp.exp(a_log.astype(jnp.float32)) * jax.nn.softplus(
        g_a.astype(jnp.float32) + dt_bias.astype(jnp.float32))
    o_gdn = gated_delta_rule_chunked(gq, gk, gv, g, beta)
    z = jax.nn.silu(g_z.reshape(B, S, GDN_HEADS, GDN_HEAD_V).astype(jnp.float32))
    o_gdn = (rms_norm(o_gdn, gdn_norm_g) * z).reshape(B, S, GDN_V_DIM).astype(x.dtype)

    cos, sin = rope_tables(S, ATT_HEAD_DIM // ROPE_FRACTION)
    a_q = apply_partial_rope(rms_norm(a_q.reshape(B, S, ATT_HEADS, ATT_HEAD_DIM), q_norm_g), cos, sin)
    a_k = apply_partial_rope(rms_norm(a_k.reshape(B, S, ATT_KV_HEADS, ATT_HEAD_DIM), k_norm_g), cos, sin)
    a_v = a_v.reshape(B, S, ATT_KV_HEADS, ATT_HEAD_DIM)
    cos_i, sin_i = rope_tables(S, IDX_DIM // ROPE_FRACTION)
    i_q = apply_partial_rope(i_q.reshape(B, S, IDX_HEADS, IDX_DIM), cos_i, sin_i)
    i_k = apply_partial_rope(i_k, cos_i, sin_i)
    i_w = i_w * (IDX_HEADS ** -0.5 * IDX_DIM ** -0.5)
    o_att = dsa_sparse_attention(a_q, a_k, a_v, i_q, i_k, i_w).astype(x.dtype)

    merged = jax.nn.sigmoid(gate_a) * o_gdn + jax.nn.sigmoid(gate_b) * o_att
    x = x + merged @ w_out

    h2 = rms_norm(x, norm_mlp_g)
    x = x + jnp.square(jax.nn.relu(h2 @ w_mlp_up)) @ w_mlp_down
    return x

def second_inputs(seed: int = 0) -> dict:
    key = jax.random.key(seed)
    ks = jax.random.split(key, 14)
    f32 = jnp.float32

    def gain(k, n):
        return 1.0 + 0.02 * jax.random.normal(k, (DEPTH, n), f32)

    x = jax.random.normal(ks[0], (BATCH, SEQ, D_MODEL), f32)
    norm_mix_g = gain(ks[1], D_MODEL)
    w_in = jax.random.normal(ks[2], (DEPTH, D_MODEL, IN_PROJ_DIM), f32) * D_MODEL ** -0.5
    conv_w = jax.random.normal(ks[3], (DEPTH, GDN_CONV, GDN_CONV_DIM), f32) * GDN_CONV ** -0.5
    a_log = jnp.log(jax.random.uniform(ks[4], (DEPTH, GDN_HEADS), f32, 1.0, 16.0))
    dt = jnp.exp(jax.random.uniform(ks[5], (DEPTH, GDN_HEADS), f32, math.log(1e-3), math.log(1e-1)))
    dt_bias = dt + jnp.log(-jnp.expm1(-dt))
    gdn_norm_g = gain(ks[6], GDN_HEAD_V)
    q_norm_g = gain(ks[7], ATT_HEAD_DIM)
    k_norm_g = gain(ks[8], ATT_HEAD_DIM)
    w_out = jax.random.normal(ks[9], (DEPTH, D_MODEL, D_MODEL), f32) * D_MODEL ** -0.5
    norm_mlp_g = gain(ks[10], D_MODEL)
    w_mlp_up = jax.random.normal(ks[11], (DEPTH, D_MODEL, D_FF_2), f32) * D_MODEL ** -0.5
    w_mlp_down = jax.random.normal(ks[12], (DEPTH, D_FF_2, D_MODEL), f32) * D_FF_2 ** -0.5
    return {"x": x, "norm_mix_g": norm_mix_g, "w_in": w_in, "conv_w": conv_w,
            "a_log": a_log, "dt_bias": dt_bias, "gdn_norm_g": gdn_norm_g,
            "q_norm_g": q_norm_g, "k_norm_g": k_norm_g, "w_out": w_out,
            "norm_mlp_g": norm_mlp_g, "w_mlp_up": w_mlp_up, "w_mlp_down": w_mlp_down}

def second_block(x, norm_mix_g, w_in, conv_w, a_log, dt_bias, gdn_norm_g, q_norm_g, k_norm_g,
              w_out, norm_mlp_g, w_mlp_up, w_mlp_down):
    for layer in range(DEPTH):
        x = hybrid_layer(x, norm_mix_g[layer], w_in[layer], conv_w[layer], a_log[layer],
                         dt_bias[layer], gdn_norm_g[layer], q_norm_g[layer], k_norm_g[layer],
                         w_out[layer], norm_mlp_g[layer], w_mlp_up[layer], w_mlp_down[layer])
    return x


def setup_inputs(seed=0):
    out = dict(first_inputs(seed))
    for name, value in second_inputs(seed + 1).items():
        if name != "x":
            out[name + "_2"] = value
    return out


def reference(
    x, mem, w_in, b_fgt, rel_bias, g_fox_out, g_chk_out, w_out, g_mix_pre, g_mix_post, g_mem_kv,
    w_mq, w_mk, w_mv, w_mo, g_mem_pre, g_mem_post, w_ff1, w_ff2, g_ff_pre, g_ff_post,
    norm_mix_g_2, w_in_2, conv_w_2, a_log_2, dt_bias_2, gdn_norm_g_2, q_norm_g_2, k_norm_g_2,
    w_out_2, norm_mlp_g_2, w_mlp_up_2, w_mlp_down_2,
):
    x = first_block(
        x, mem, w_in, b_fgt, rel_bias, g_fox_out, g_chk_out, w_out, g_mix_pre, g_mix_post,
        g_mem_kv, w_mq, w_mk, w_mv, w_mo, g_mem_pre, g_mem_post, w_ff1, w_ff2, g_ff_pre,
        g_ff_post,
    )
    return second_block(
        x, norm_mix_g_2, w_in_2, conv_w_2, a_log_2, dt_bias_2, gdn_norm_g_2, q_norm_g_2,
        k_norm_g_2, w_out_2, norm_mlp_g_2, w_mlp_up_2, w_mlp_down_2,
    )


_drawn_inputs = setup_inputs


def setup_inputs(seed=0):
    import zlib

    import numpy as np

    out = dict(_drawn_inputs(seed))
    spreads = {}
    factors = {'norm_mix_g_2': 6.238,
     'gdn_norm_g_2': 8.0,
     'q_norm_g_2': 23.12,
     'k_norm_g_2': 22.991,
     'norm_mlp_g_2': 15.334}
    for name, (base, spread) in spreads.items():
        noise = np.random.default_rng([zlib.crc32(name.encode()), seed]).standard_normal(out[name].shape)
        drawn = base * np.exp(spread * noise) if base else spread * noise
        out[name] = __import__('jax').numpy.asarray(drawn.astype(out[name].dtype))
    for name, factor in factors.items():
        out[name] = (out[name] * factor).astype(out[name].dtype)
    return out
```

```python
from contextlib import ExitStack

import numpy as np
import concourse.bass as bass
from concourse import mybir

F32 = mybir.dt.float32
F32R = mybir.dt.float32r
ALU = mybir.AluOpType
ACT = mybir.ActivationFunctionType
AX_X = mybir.AxisListType.X

P = 128
S = 256
NT = S // P
D = 1024
KC = D // P
EPS = 1e-6
NEG = -1e30

FH, FD = 8, 64
DFOX = FH * FD
CHUNK, MAX_REL = 64, 128
MH, MD = 4, 256
FF = 4096
GH, GD = 8, 128
AH, AKV, AD = 8, 2, 128
IH, ID = 8, 64
TOPK = 64
ROPE_THETA = 500000.0
AR, IR = AD // 8, ID // 8

RAW_SLOTS = 3
SPLIT_SLOTS = 2
AHEAD = SPLIT_SLOTS - 1

C_ID, C_CAUSAL, C_ZERO, C_SEL, C_DMASK = 0, 128, 384, 640, 648
C_LEVEL = C_DMASK + P
LEVELS = 7
C_COS = C_LEVEL + LEVELS * P
C_SIN = C_COS + NT * AR
C_ICOS = C_SIN + NT * AR
C_ISIN = C_ICOS + NT * IR
N_CONST = C_ISIN + NT * IR

O_FQ, O_FK, O_FV, O_F, O_CQ, O_CK, O_CV = 0, 512, 1024, 1536, 1544, 2056, 2568
O_QKV, O_Z, O_GAB, O_AQ, O_AKV, O_IQ, O_IKW, O_GA, O_GB = 0, 3072, 4096, 4112, 5136, 5648, 6160, 6232, 7256


def constants():
    c = np.zeros((P, N_CONST), np.float32)
    r, f = np.arange(P)[:, None], np.arange(P)[None, :]
    c[:, C_ID:C_ID + P] = np.eye(P)
    c[:, C_CAUSAL + P:C_CAUSAL + 2 * P] = np.where(f > r, NEG, 0)
    for h in range(8):
        c[[h, 32 + h, 64 + h, 96 + h], C_SEL + h] = 1
    c[:, C_DMASK:C_DMASK + P] = np.where(f >= r, 0, NEG)
    for l in range(LEVELS):
        b = 1 << l
        c[:, C_LEVEL + l * P:C_LEVEL + (l + 1) * P] = (f // (2 * b) == r // (2 * b)) & (f % (2 * b) >= b) & (r % (2 * b) < b)
    for cc, cs, half in ((C_COS, C_SIN, AR), (C_ICOS, C_ISIN, IR)):
        inv = (np.float32(ROPE_THETA) ** (-np.arange(0, 2 * half, 2, dtype=np.float32) / np.float32(2 * half))).astype(np.float32)
        ang = np.arange(S, dtype=np.float32)[:, None] * inv[None, :]
        for t in range(NT):
            c[:, cc + t * half:cc + (t + 1) * half] = np.cos(ang[t * P:(t + 1) * P])
            c[:, cs + t * half:cs + (t + 1) * half] = np.sin(ang[t * P:(t + 1) * P])
    return c


def rel_rows(rel_bias):
    idx = np.clip(P + np.arange(P)[:, None] - np.arange(S)[None, :], -MAX_REL, MAX_REL) + MAX_REL
    return np.ascontiguousarray(np.transpose(rel_bias[0][:, idx], (1, 0, 2)))


V_GAIN, V_NARROW = 0, 8 * KC
V_BC8 = V_NARROW + KC * 96
V_HEAD = V_BC8 + 24
V_CONV = V_HEAD + 3 * P
N_SMALL = V_CONV + 24 * 4


def small_inputs(a):
    def chunks(g):
        return g.reshape(-1, P).T

    def rows(wgt, c0, n):
        return wgt[0][:, c0:c0 + n].reshape(KC, P, n).transpose(1, 0, 2)

    gains = [a["g_mem_kv"], a["g_mix_pre"], np.concatenate([a["g_fox_out"], a["g_chk_out"]], 1), a["g_mem_pre"],
             a["g_ff_pre"], a["norm_mix_g_2"], a["norm_mlp_g_2"], a["norm_mlp_g_2"]]
    narrow = np.concatenate([rows(a["w_in"], O_F, 8), rows(a["w_in_2"], O_GAB, 16), rows(a["w_in_2"], O_IKW, 72)], 2)
    vectors = [a["b_fgt"], a["a_log_2"], a["dt_bias_2"], a["q_norm_g_2"], a["k_norm_g_2"], a["gdn_norm_g_2"]]
    return np.ascontiguousarray(np.concatenate(
        [chunks(g) for g in gains] + [narrow.reshape(P, -1)] + [np.repeat(v, P, 0) for v in vectors]
        + [a["conv_w_2"][0].reshape(4, 24, P).transpose(2, 1, 0).reshape(P, -1)], 1))


def weight_units(w):
    units, of = [], {}

    def rows(name, c0, n, k0, kc):
        return w[name][0, k0 * P:(k0 + kc) * P, c0:c0 + n].rearrange("(c p) n -> p c n", p=P)

    def group(tag, form, name, c0, ncol, kchunks=KC):
        ids = []
        if form == "B":
            for c in range(c0, c0 + ncol, 256):
                ids.append(len(units))
                units.append(dict(form="B", src=rows(name, c, 256, 0, KC), banks=[None]))
        else:
            for c in range(c0, c0 + ncol, 512):
                for k in range(0, kchunks, 4):
                    ids.append(len(units))
                    units.append(dict(form="A", src=rows(name, c, 512, k, 4), k0=k, first=k == 0,
                                      last=k == kchunks - 4, banks=[None, None]))
        of[tag] = ids

    group("fq", "B", "w_in", O_FQ, 512)
    group("fk", "B", "w_in", O_FK, 512)
    group("fv", "A", "w_in", O_FV, 512)
    group("cq", "B", "w_in", O_CQ, 512)
    group("ck", "B", "w_in", O_CK, 512)
    group("cv", "A", "w_in", O_CV, 512)
    group("mk", "B", "w_mk", 0, D)
    group("mv", "A", "w_mv", 0, D)
    group("out", "A", "w_out", 0, D)
    group("mq", "B", "w_mq", 0, D)
    group("mo", "A", "w_mo", 0, D)
    group("ff1", "B", "w_ff1", 0, FF)
    group("ff2", "A", "w_ff2", 0, D, FF // P)
    group("akv", "A", "w_in_2", O_AKV, 512)
    group("iq", "A", "w_in_2", O_IQ, 512)
    group("aq", "A", "w_in_2", O_AQ, 1024)
    group("qkv", "B", "w_in_2", O_QKV, 3 * D)
    group("z", "A", "w_in_2", O_Z, D)
    group("ga", "A", "w_in_2", O_GA, D)
    group("gb", "A", "w_in_2", O_GB, D)
    group("out2", "A", "w_out_2", 0, D)
    group("up", "B", "w_mlp_up_2", 0, FF)
    group("down", "A", "w_mlp_down_2", 0, D, FF // P)
    bank, uses = 0, [0] * 4
    for u in units:
        if u["form"] == "B" or u["first"]:
            if u["form"] == "A" and bank % 2:
                raise ValueError("pairs of banks are aligned")
            u["banks"] = [(bank + i) % 4 for i in range(len(u["banks"]))]
            u["before"] = [uses[b] for b in u["banks"]]
            for b in u["banks"]:
                uses[b] += 1
            bank += len(u["banks"])
        else:
            u["banks"], u["before"] = units[units.index(u) - 1]["banks"], None
    return units, of


class Count:

    def __init__(self):
        self.seen = {}

    def wait(self, eng, sem, k=1):
        key = (id(eng), id(sem))
        self.seen[key] = self.seen.get(key, 0) + k
        eng.wait_ge(sem, self.seen[key])


def build_program(nc, w, consts, small, rel, out):
    units, of = weight_units(w)
    NU = len(units)
    ctx = ExitStack()
    with ctx:
        def sb(name, shape, dt=F32, at=ctx):
            return at.enter_context(nc.sbuf_tensor("s_" + name, shape, dt))

        def sem(name):
            return ctx.enter_context(nc.semaphore(name))

        w_raw = [sb(f"w_raw{i}", [P, 2048]) for i in range(RAW_SLOTS)]
        w_hi = [sb(f"w_hi{i}", [P, 2048], F32R) for i in range(SPLIT_SLOTS)]
        w_lo = [sb(f"w_lo{i}", [P, 2048], F32R) for i in range(SPLIT_SLOTS)]
        h_hi = sb("h_hi", [P, KC, S], F32R)
        h_lo = sb("h_lo", [P, KC, S], F32R)
        x = sb("x", [P, NT, D])
        xn = sb("xn", [P, NT, D])
        cst = sb("cst", [P, N_CONST])
        sm = sb("sm", [P, N_SMALL])
        gcol = sm[:, V_GAIN:V_NARROW].rearrange("p (j c) -> p j c", c=KC)
        ws_raw = sm[:, V_NARROW:V_BC8].rearrange("p (c n) -> p c n", c=KC)
        bc8 = sm[:, V_BC8:V_HEAD].rearrange("p (j h) -> p j h", h=8)
        ghead = sm[:, V_HEAD:V_CONV].rearrange("p (j d) -> p j d", d=P)
        gpost = sb("gpost", [P, D])
        ws_hi = sb("ws_hi", [P, KC, 96], F32R)
        ws_lo = sb("ws_lo", [P, KC, 96], F32R)
        stat = sb("stat", [P, 64])
        rstd = sb("rstd", [P, 64])
        nmax = sb("nmax", [P, 56])
        rsum = sb("rsum", [P, 56])
        rinv = sb("rinv", [P, 56])
        half = sb("half", [P, 32])
        junk = sb("junk", [P, 512])
        sel_l = sb("sel_l", [104, 8, S])
        sel_a = sb("sel_a", [104, S])
        sel_r = sb("sel_r", [104, S])
        cum = sb("cum", [8, S])
        gate8 = sb("gate8", [P, 8, 16])

        def softmax_buffers(at, tag):
            return (sb("L" + tag, [P, 2, S], at=at), sb("P" + tag, [P, 3, S], at=at), sb("PT" + tag, [P, 2, NT, P], at=at))

        conv_h = sb("conv_h", [P, 24, 4])
        hsum = sb("hsum", [P, 80])
        hrms = sb("hrms", [P, 80])
        gq4 = sb("gq4", [P, P])
        r1 = ExitStack()
        bufs1 = softmax_buffers(r1, "1")
        mqT = sb("mqT", [P, KC, S], at=r1)
        fqT, fkT = mqT[:, 0:4, :], mqT[:, 4:8, :]
        fv = sb("fv", [P, NT, 512], at=r1)
        cqT = sb("cqT", [P, 4, S], at=r1)
        ckT = sb("ckT", [P, 4, S], at=r1)
        cv = sb("cv", [P, NT, 512], at=r1)
        relb = sb("relb", [P, FH, S], at=r1)
        y = sb("y", [P, NT, D], at=r1)
        mem = y
        mkT = sb("mkT", [P, KC, S], at=r1)
        mv = sb("mv", [P, NT, D], at=r1)
        m_hi = sb("m_hi", [P, KC, S], F32R, at=r1)
        m_lo = sb("m_lo", [P, KC, S], F32R, at=r1)
        r1.close()
        r2 = ExitStack()
        hid_hi = sb("hid_hi", [P, FF // P, S], F32R, at=r2)
        hid_lo = sb("hid_lo", [P, FF // P, S], F32R, at=r2)
        hid_r = sb("hid_r", [P, 2, 512], at=r2)
        hid_v = sb("hid_v", [P, 2, 512], at=r2)
        r2.close()
        a0 = ExitStack()
        qkvT = sb("qkvT", [P, 24, S], at=a0)
        b0 = ExitStack()
        bufs2 = softmax_buffers(b0, "2")
        aqT = sb("aqT", [P, AH, S], at=b0)
        akT = sb("akT", [P, AKV, S], at=b0)
        av = sb("av", [P, NT, AKV * AD], at=b0)
        selb = sb("selb", [P, NT, S], at=b0)
        score = sb("score", [P, NT, S], at=b0)
        work = junk[:, 0:S]
        top8 = sb("top8", [P, 8], at=b0)
        relu_i = sb("relu_i", [P, 2, S], at=b0)
        aqk = sb("aqk", [P, NT, AH + AKV, AD], at=b0)
        iqk = sb("iqk", [P, NT, IH + 2, ID], at=b0)
        iw = sb("iw", [P, NT, IH], at=b0)
        iqkT = sb("iqkT", [P, IH // 2 + 1, S], at=b0)
        rope_t = sb("rope_t", [P, 4, (AH + AKV) * AR], at=b0)
        cin = sb("cin", [P, 2, 2, 3 + S], at=b0)
        conv_t = sb("conv_t", [P, S], at=b0)
        tanh_c = sb("tanh_c", [P, 2, 512], at=b0)
        b0.close()
        b1 = ExitStack()
        khat = sb("khat", [P, NT, GH, GD], at=b1)
        kb = sb("kb", [P, NT, GH, GD], at=b1)
        qh = sb("qh", [P, NT, GH, GD], at=b1)
        vb = sb("vb", [P, NT, GH, GD], at=b1)
        kbg = sb("kbg", [P, GH, GD], at=b1)
        kdec = sb("kdec", [P, GH, GD], at=b1)
        zg = sb("zg", [P, NT, D], at=b1)
        tanh_g = sb("tanh_g", [P, 2, 512], at=b1)
        sqb = sb("sqb", [P, 2, 512], at=b1)
        b1.close()
        b2 = ExitStack()
        APT = sb("APT", [P, NT, GH, 2, P], at=b2)
        DT = sb("DT", [P, NT, GH, P], at=b2)
        b2.close()
        b3 = ExitStack()
        sb("under_APT", [P, NT * GH * 2 * P], at=b3)
        vnew = sb("vnew", [P, GH, GD], at=b3)
        S1 = sb("S1", [P, GH, GD], at=b3)
        b3.close()
        a0.close()
        a1 = ExitStack()
        khT = sb("khT", [P, NT, GH, P], at=a1)
        kbqT = sb("kbqT", [P, 2, NT, GH, P], at=a1)
        a1.close()
        a2 = ExitStack()
        Tm = sb("Tm", [P, 2, 4, P], at=a2)
        Um = sb("Um", [P, 2, 4, P], at=a2)
        Bt = sb("Bt", [P, 2, 4, P], at=a2)
        Yb = sb("Yb", [P, 2, 4, P], at=a2)
        a2.close()

        acc = [ctx.enter_context(nc.psum_tensor(f"acc{i}", [P, 512], F32)) for i in range(4)]
        aux = [ctx.enter_context(nc.psum_tensor(f"aux{i}", [P, 512], F32)) for i in range(4)]

        w_loaded = [sem(f"w_loaded{i}") for i in range(RAW_SLOTS)]
        w_hi_done, w_lo_done, unit_done = sem("w_hi_done"), sem("w_lo_done"), sem("unit_done")
        acc_free = [sem(f"acc_free{i}") for i in range(4)]
        x_in, id_in, gain_in, mem_in, cst_in, small_in, rel_in, gpost_in = [sem(n) for n in (
            "x_in", "id_in", "gain_in", "mem_in", "cst_in", "small_in", "rel_in", "gpost_in")]
        ss_done, rstd_done, diag_done, nt_tr, nt_hi, nt_lo = [sem(n) for n in (
            "ss_done", "rstd_done", "diag_done", "nt_tr", "nt_hi", "nt_lo")]
        ws_hi_done, ws_lo_done, ws_mm = sem("ws_hi_done"), sem("ws_lo_done"), sem("ws_mm")
        set_done, rel_done = sem("set_done"), sem("rel_done")
        gate_v, gate_a, gate_tr, gate_ct, sel_done = [sem(n) for n in ("gate_v", "gate_a", "gate_tr", "gate_ct", "sel_done")]
        ev = sem("ev")
        sc_done, l_done, p_done, pt_done, ptc_done, pv_done, rinv_done, y_done = [sem(n) for n in (
            "sc_done", "l_done", "p_done", "pt_done", "ptc_done", "pv_done", "rinv_done", "y_done")]
        post_tmp, x_done, relu_done, hid_hi_done, hid_lo_done = [sem(n) for n in (
            "post_tmp", "x_done", "relu_done", "hid_hi_done", "hid_lo_done")]
        stored = sem("stored")
        g2_in, g2_a, g2_g, g2_tr, g2_ct, g2_sel, g2_tm, g2_eg = [sem("g2_" + n) for n in ("in", "a", "g", "tr", "ct", "sel", "tm", "eg")]
        set2_done, ik_done, rope_i, iqT_mm, iqT_copied = [sem(n) for n in (
            "set2_done", "ik_done", "rope_i", "iqT_mm", "iqT_copied")]
        idx_mm, idx_relu, idx_acc, aqk_ss, aqk_rms, aqk_done, aT_mm, aT_copied = [sem(n) for n in (
            "idx_mm", "idx_relu", "idx_acc", "aqk_ss", "aqk_rms", "aqk_done", "aT_mm", "aT_copied")]
        conv_done, conv2_done, tanh_done, qkv_done = [sem(n) for n in ("conv_done", "conv2_done", "tanh_done", "qkv_done")]
        gate_tanh, tok_mm, tok_copied, tok_sq, tok_ss, tok_rms, tok_done = [sem(n) for n in (
            "gate_tanh", "tok_mm", "tok_copied", "tok_sq", "tok_ss", "tok_rms", "tok_done")]
        back_mm, back_copied, dt_mm, dt_add, dt_done, kdec_done, ap_mm, ap_done = [sem(n) for n in (
            "back_mm", "back_copied", "dt_mm", "dt_add", "dt_done", "kdec_done", "ap_mm", "ap_done")]
        bt_done, u_done, t_done, t_init, y_mm, y_copied, ty_mm, yu_mm = [sem("inv_" + n) for n in (
            "bt", "u", "t", "t_init", "y_mm", "y_copied", "ty_mm", "yu_mm")]
        r_mm, r_copied, qs_mm, qs_done, o_mm, o_done, o_ss, o_rms, merged_done = [sem("out_" + n) for n in (
            "r_mm", "r_copied", "qs_mm", "qs_done", "o_mm", "o_done", "o_ss", "o_rms", "merged")]

        def ident():
            return cst[:, C_ID:C_ID + P]

        N = Count()
        SS_AFTER = {"p_out": 16, "p_mo": 24, "p_ff2": 32}
        GAIN = {"mem": 0, "mix": 1, "y": 2, "mpre": 3, "memo": None, "ff": 4, "mix2": 5, "merged": None, "mlp2": 6}
        def unit_hi(act, u):
            act.wait_ge(w_loaded[u % RAW_SLOTS], 16 * (u // RAW_SLOTS + 1))
            if u >= SPLIT_SLOTS:
                act.wait_ge(unit_done, u - SPLIT_SLOTS + 1)
            act.activation(w_hi[u % SPLIT_SLOTS][:], w_raw[u % RAW_SLOTS][:], ACT.Copy).then_inc(w_hi_done, 1)

        def unit_lo(dve, u):
            dve.wait_ge(w_hi_done, u + 1)
            dve.tensor_tensor(w_lo[u % SPLIT_SLOTS][:], w_raw[u % RAW_SLOTS][:], w_hi[u % SPLIT_SLOTS][:].bitcast(F32),
                              ALU.subtract).then_inc(w_lo_done, 1)

        def narrow_mm(pe, k, t, bank, c0, n):
            ts, cs, o = slice(t * P, (t + 1) * P), slice(c0, c0 + n), bank[:, t * n:(t + 1) * n]
            pe.matmul(o, h_hi[:, k, ts], ws_hi[:, k, cs], start=k == 0 and t == 0, stop=False, skip_group_check=True)
            pe.matmul(o, h_hi[:, k, ts], ws_lo[:, k, cs], start=False, stop=False, skip_group_check=True)
            return pe.matmul(o, h_lo[:, k, ts], ws_hi[:, k, cs], start=False, stop=k == KC - 1, skip_group_check=True)

        def unit_mm(pe, u, hi, lo, narrow=(), fresh=None):
            def chunk_ready(k):
                if fresh is not None:
                    pe.wait_ge(nt_lo, KC * fresh + k + 1)

            q = units[u]
            pe.wait_ge(w_lo_done, u + 1)
            if q["before"] is not None:
                for b, n in zip(q["banks"], q["before"]):
                    if n:
                        pe.wait_ge(acc_free[b], n)
            wh, wl = w_hi[u % SPLIT_SLOTS], w_lo[u % SPLIT_SLOTS]
            if q["form"] == "A":
                for kk in range(4):
                    k = q["k0"] + kk
                    cs = slice(kk * 512, (kk + 1) * 512)
                    chunk_ready(k)
                    for t in range(NT):
                        ts = slice(t * P, (t + 1) * P)
                        o = acc[q["banks"][t]][:]
                        pe.matmul(o, hi[:, k, ts], wh[:, cs], start=q["first"] and kk == 0, stop=False)
                        pe.matmul(o, hi[:, k, ts], wl[:, cs], start=False, stop=False)
                        for bank, c0, n in narrow:
                            i = narrow_mm(pe, k, t, bank, c0, n)
                            if k == KC - 1 and t == NT - 1:
                                i.then_inc(ws_mm, 1)
                        i = pe.matmul(o, lo[:, k, ts], wh[:, cs], start=False, stop=q["last"] and kk == 3)
            else:
                for m in range(2):
                    o = acc[q["banks"][0]][:, m * S:(m + 1) * S]
                    for k in range(KC):
                        cs = slice(k * 256 + m * P, k * 256 + (m + 1) * P)
                        if m == 0:
                            chunk_ready(k)
                        pe.matmul(o, wh[:, cs], hi[:, k, :], start=k == 0, stop=False)
                        pe.matmul(o, wh[:, cs], lo[:, k, :], start=False, stop=False)
                        i = pe.matmul(o, wl[:, cs], hi[:, k, :], start=False, stop=k == KC - 1)
            i.then_inc(unit_done, 1)

        def released(u):
            q, v = units[u], u
            while units[v]["before"] is None:
                v -= 1
            return [(b, n + 1) for b, n in zip(q["banks"], units[v]["before"])]

        def wait_copied(pe, tag):
            for u in of[tag]:
                for b, n in released(u):
                    pe.wait_ge(acc_free[b], n)

        def nt_act_stats(act, n, src, ready=None):
            for g in range(2):
                for t in range(NT):
                    if ready is not None:
                        ready(g, t)
                    square(act, n, g, t, src[:, t, g * 512:(g + 1) * 512])

        def square(act, n, g, t, piece):
            c = 4 * NCOL[n] + 2 * g + t
            act.activation(junk[:], piece, ACT.Square, accum_out=stat[:, c:c + 1]).then_inc(ss_done, 1)
            N.wait(act, ss_done)

        NCOL = {"mem": 0, "mix": 1, "y": 2, "mpre": 3, "ff": 4, "mix2": 5, "mlp2": 6, "p_out": 7, "p_mo": 8, "p_ff2": 9}
        GROUPS = {n: [(0, D)] for n in NCOL}
        GROUPS["y"] = [(0, 512), (512, D)]

        def rstd_pool(pool, n):
            c = 4 * NCOL[n]
            pool.wait_ge(set_done, 1)
            N.wait(pool, ss_done, 4)
            if len(GROUPS[n]) == 1:
                pool.tensor_tensor(stat[:, c:c + 2], stat[:, c:c + 2], stat[:, c + 2:c + 4], ALU.add)
                pool.drain()
            width = 2 if len(GROUPS[n]) == 1 else 4
            pool.tensor_scalar(stat[:, c:c + width], stat[:, c:c + width], 1.0 / (D if width == 2 else 512), EPS,
                               ALU.mult, ALU.add)
            pool.drain()
            pool.tensor_tensor(rstd[:, c:c + width], stat[:, c:c + width], half[:, 0:width], ALU.pow).then_inc(rstd_done, 1)

        def rstd_y_pool(pool, g):
            c = 4 * NCOL["y"] + 2 * g
            N.wait(pool, ss_done, 2)
            pool.tensor_scalar(stat[:, c:c + 2], stat[:, c:c + 2], 1.0 / 512, EPS, ALU.mult, ALU.add)
            pool.drain()
            pool.tensor_tensor(rstd[:, c:c + 2], stat[:, c:c + 2], half[:, 0:2], ALU.pow).then_inc(rstd_done, 1)

        diag = xn[:, 0, 0:512].rearrange("p (j s) -> p j s", j=4)

        def nt_dve_diag(dve, n, g=0):
            N.wait(dve, rstd_done)
            for t in range(NT):
                c = 4 * NCOL[n] + 2 * g + t
                dve.tensor_scalar(diag[:, 2 * g + t, :], ident(), rstd[:, c:c + 1], None, ALU.mult).then_inc(diag_done, 1)

        def nt_pe(pe, n, src, banks=range(4)):
            for j in banks:
                if GAIN[n] is not None and (j == 0 or len(GROUPS[n]) == 2 and j == 2):
                    N.wait(pe, diag_done, 2)
                for kk in range(2):
                    for t in range(NT):
                        k = 2 * j + kk
                        o, piece = aux[j][:, kk * S + t * P:kk * S + (t + 1) * P], src[:, t, k * P:(k + 1) * P]
                        if GAIN[n] is None:
                            i = pe.transpose(o, piece, ident())
                        else:
                            g = k // 4 if len(GROUPS[n]) == 2 else 0
                            i = pe.matmul(o, piece, diag[:, 2 * g + t, :], start=True, stop=True)
                i.then_inc(nt_tr, 1)

        def nt_act(act, n, hi):
            for j in range(4):
                N.wait(act, nt_tr)
                for kk in range(2):
                    k = 2 * j + kk
                    g = 1.0 if GAIN[n] is None else gcol[:, GAIN[n], k:k + 1]
                    act.activation(hi[:, k, :], aux[j][:, kk * S:(kk + 1) * S], ACT.Copy, scale=g).then_inc(nt_hi, 1)

        def nt_dve(dve, n, hi, lo):
            for j in range(4):
                for kk in range(2):
                    k = 2 * j + kk
                    if kk == 0:
                        N.wait(dve, nt_hi, 2)
                    g = 1.0 if GAIN[n] is None else gcol[:, GAIN[n], k:k + 1]
                    dve.scalar_tensor_tensor(lo[:, k, :], aux[j][:, kk * S:(kk + 1) * S], g, hi[:, k, :].bitcast(F32),
                                             ALU.mult, ALU.subtract).then_inc(nt_lo, 1)

        def evac_b(act, u, dst, scale=1.0):
            act.wait_ge(unit_done, u + 1)
            act.activation(dst, acc[units[u]["banks"][0]][:], ACT.Copy, scale=scale).then_inc(acc_free[units[u]["banks"][0]], 1)

        def evac_a(act, u, dsts, scale=1.0):
            act.wait_ge(unit_done, u + 1)
            for t in range(NT):
                b = units[u]["banks"][t]
                act.activation(dsts[t], acc[b][:], ACT.Copy, scale=scale).then_inc(acc_free[b], 1)

        def bufs(i):
            return bufs1 if i < I_DSA else bufs2

        def at_pe_scores(pe, i, it):
            if i >= 2:
                pe.wait_ge(l_done, i - 1)
            nk = it["nk"]
            o = aux[i % 2][:, 0:nk]
            for j, (a, b) in enumerate(it["qk"]):
                m = pe.matmul(o, a, b, start=j == 0, stop=j == len(it["qk"]) - 1)
            m.then_inc(sc_done, 1)

        def at_dve_mask(dve, i, it):
            N.wait(dve, sc_done)
            if i >= 2:
                dve.wait_ge(p_done, i - 1)
            nk = it["nk"]
            dve.tensor_tensor_reduce(out=bufs(i)[0][:, i % 2, 0:nk], in0=aux[i % 2][:, 0:nk], in1=it["bias"], scale=-it["scale"],
                                     scalar=3e38, op0=ALU.add, op1=ALU.min, accum_out=nmax[:, i:i + 1]).then_inc(l_done, 1)

        def at_act_exp(act, i, it):
            N.wait(act, l_done)
            if i >= 3:
                act.wait_ge(pt_done, i - 2)
            nk = it["nk"]
            act.activation(bufs(i)[1][:, i % 3, 0:nk], bufs(i)[0][:, i % 2, 0:nk], ACT.Exp, bias=nmax[:, i:i + 1], scale=-1.0,
                           accum_out=rsum[:, i:i + 1]).then_inc(p_done, 1)

        def at_pe_tr(pe, i, it):
            N.wait(pe, p_done)
            if i >= 2:
                pe.wait_ge(y_done, i - 1)
            for b in range(it["nk"] // P):
                m = pe.transpose(aux[2 + i % 2][:, b * P:(b + 1) * P], bufs(i)[1][:, i % 3, b * P:(b + 1) * P], ident())
            m.then_inc(pt_done, 1)

        def at_dve_copy(dve, i, it):
            N.wait(dve, pt_done)
            if i >= 2:
                dve.wait_ge(pv_done, i - 1)
            nb = it["nk"] // P
            dve.tensor_copy(bufs(i)[2][:, i % 2, 0:nb, :], aux[2 + i % 2][:, 0:nb * P]).then_inc(ptc_done, 1)
            dve.wait_ge(p_done, i + 1)
            dve.reciprocal(rinv[:, i:i + 1], rsum[:, i:i + 1]).then_inc(rinv_done, 1)

        def at_pe_pv(pe, i, it):
            N.wait(pe, ptc_done)
            nb = it["nk"] // P
            dv = it["dv"]
            for b in range(nb):
                m = pe.matmul(aux[2 + i % 2][:, S:S + dv], bufs(i)[2][:, i % 2, b, :], it["v"][b], start=b == 0, stop=b == nb - 1)
            m.then_inc(pv_done, 1)

        def at_act_out(act, i, it):
            N.wait(act, pv_done)
            act.wait_ge(rinv_done, i + 1)
            act.activation(it["out"], aux[2 + i % 2][:, S:S + it["dv"]], ACT.Copy, scale=rinv[:, i:i + 1]).then_inc(y_done, 1)

        def fox_items():
            items = []
            for h in range(FH):
                r, m = 64 * (h % 2), h // 2
                for t in range(NT):
                    ts, nk = slice(t * P, (t + 1) * P), (t + 1) * P
                    items.append(dict(nk=nk, scale=1.0, dv=FD,
                                      qk=[(fqT[r:r + 64, m, ts], fkT[r:r + 64, m, 0:nk]), (sel_l[r:r + 40, h, ts], sel_r[r:r + 40, 0:nk])],
                                      bias=cst[:, C_CAUSAL + 2 * P - nk:C_CAUSAL + 2 * P],
                                      v=[fv[:, b, h * FD:(h + 1) * FD] for b in range(t + 1)],
                                      out=y[:, t, h * FD:(h + 1) * FD]))
            for h in range(FH):
                r, m = 64 * (h % 2), h // 2
                for t in range(NT):
                    ts, nk = slice(t * P, (t + 1) * P), (t + 1) * P
                    items.append(dict(nk=nk, scale=1.0, dv=FD,
                                      qk=[(cqT[r:r + 64, m, ts], ckT[r:r + 64, m, 0:nk])],
                                      bias=relb[:, h, S - nk:S],
                                      v=[cv[:, b, h * FD:(h + 1) * FD] for b in range(t + 1)],
                                      out=y[:, t, DFOX + h * FD:DFOX + (h + 1) * FD]))
            return items

        def mem_items():
            items = []
            for h in range(MH):
                for t in range(NT):
                    ts = slice(t * P, (t + 1) * P)
                    items.append(dict(nk=S, scale=1.0, dv=MD,
                                      qk=[(mqT[:, 2 * h + c, ts], mkT[:, 2 * h + c, :]) for c in range(2)],
                                      bias=cst[:, C_ZERO:C_ZERO + S],
                                      v=[mv[:, b, h * MD:(h + 1) * MD] for b in range(NT)],
                                      out=y[:, t, h * MD:(h + 1) * MD]))
            return items

        FOX, MEM = fox_items(), mem_items()
        I_MEM = len(FOX)
        I_DSA = I_MEM + len(MEM)

        def dsa_items():
            items = []
            for h in range(AH):
                kv = h // (AH // AKV)
                for t in range(NT):
                    ts, nk = slice(t * P, (t + 1) * P), (t + 1) * P
                    items.append(dict(nk=nk, scale=float(AD) ** -0.5, dv=AD, qk=[(aqT[:, h, ts], akT[:, kv, 0:nk])],
                                      bias=selb[:, t, 0:nk],
                                      v=[av[:, b, kv * AD:(kv + 1) * AD] for b in range(t + 1)],
                                      out=xn[:, t, h * AD:(h + 1) * AD]))
            return items

        DSA = dsa_items()

        def post_stats(act, n, tag):
            for g in range(2):
                u = of[tag][(g + 1) * len(of[tag]) // 2 - 1]
                act.wait_ge(unit_done, u + 1)
                for t in range(NT):
                    square(act, n, g, t, acc[units[u]["banks"][t]][:])

        def post_add(dve, n, tag, n_load):
            dve.wait_ge(gpost_in, 16 * n_load)
            for g in range(2):
                u = of[tag][(g + 1) * len(of[tag]) // 2 - 1]
                dve.wait_ge(unit_done, u + 1)
                dve.wait_ge(ss_done, SS_AFTER[n] - 2 + 2 * g)
                for t in range(NT):
                    b = units[u]["banks"][t]
                    cs = slice(g * 512, (g + 1) * 512)
                    dve.tensor_tensor(xn[:, t, cs], acc[b][:], gpost[:, cs], ALU.mult).then_inc(acc_free[b], 1)
            N.wait(dve, rstd_done)
            dve.drain()
            for g in range(2):
                for t in range(NT):
                    c = 4 * NCOL[n] + t
                    cs = slice(g * 512, (g + 1) * 512)
                    dve.scalar_tensor_tensor(x[:, t, cs], xn[:, t, cs], rstd[:, c:c + 1], x[:, t, cs],
                                             ALU.mult, ALU.add).then_inc(x_done, 1)

        def wait_read(eng, u):
            for b, n in released(u):
                eng.wait_ge(acc_free[b], n)

        HB = {"ff1": 0, "up": 16}

        def hid_act_relu(act, tag, j):
            u = of[tag][j]
            act.wait_ge(unit_done, u + 1)
            if j >= 2:
                wait_read(act, u - 2)
            act.activation(hid_r[:, j % 2, :], acc[units[u]["banks"][0]][:], ACT.Relu).then_inc(relu_done, 1)

        def hid_dve_sq(dve, tag, j):
            u = of[tag][j]
            N.wait(dve, relu_done)
            if j >= 2:
                dve.wait_ge(hid_lo_done, HB[tag] + j - 1)
            b = units[u]["banks"][0]
            dve.scalar_tensor_tensor(hid_v[:, j % 2, :], acc[b][:], 0.0, hid_r[:, j % 2, :], ALU.max, ALU.mult).then_inc(acc_free[b], 1)

        def hid_act_hi(act, tag, j):
            wait_read(act, of[tag][j])
            act.activation(hid_hi[:, 2 * j:2 * j + 2, :], hid_v[:, j % 2, :], ACT.Copy).then_inc(hid_hi_done, 1)

        def hid_dve_lo(dve, tag, j):
            N.wait(dve, hid_hi_done)
            dve.tensor_tensor(hid_lo[:, 2 * j:2 * j + 2, :], hid_v[:, j % 2, :], hid_hi[:, 2 * j:2 * j + 2, :].bitcast(F32),
                              ALU.subtract).then_inc(hid_lo_done, 1)

        def advance_hi(act, u):
            if u + AHEAD < NU:
                unit_hi(act, u + AHEAD)

        def advance_lo(dve, u):
            if u + AHEAD < NU:
                unit_lo(dve, u + AHEAD)

        EVAC_B = {"fq": (fqT, 0.125), "fk": (fkT, 1.0), "cq": (cqT, 0.125), "ck": (ckT, 1.0), "mk": (mkT, 1.0), "mq": (mqT, 0.0625)}
        EVAC_A = {"fv": fv, "cv": cv}

        def act_unit(act, tag, j):
            u = of[tag][j]
            advance_hi(act, u)
            if tag in EVAC_B:
                dst, scale = EVAC_B[tag]
                evac_b(act, u, dst[:, 2 * j:2 * j + 2, :], scale)
            elif tag in EVAC_A and units[u]["last"]:
                evac_a(act, u, [EVAC_A[tag][:, t, :] for t in range(NT)])
            elif tag == "mv" and units[u]["last"]:
                g = j // 2
                evac_a(act, u, [mv[:, t, g * 512:(g + 1) * 512] for t in range(NT)])
            elif tag == "iq" and units[u]["last"]:
                evac_a(act, u, [iqk[:, t, 0:IH, :].rearrange("p h d -> p (h d)") for t in range(NT)])
            elif tag == "aq" and units[u]["last"]:
                g = j // 2
                evac_a(act, u, [aqk[:, t, 4 * g:4 * g + 4, :].rearrange("p h d -> p (h d)") for t in range(NT)])
            elif tag == "akv" and units[u]["last"]:
                act.wait_ge(unit_done, u + 1)
                for t in range(NT):
                    b = units[u]["banks"][t]
                    act.activation(aqk[:, t, AH:, :].rearrange("p h d -> p (h d)"), acc[b][:, 0:AKV * AD], ACT.Copy)
                    act.activation(av[:, t, :], acc[b][:, AKV * AD:], ACT.Copy).then_inc(acc_free[b], 1)

        def attention_pe(pe, items, i0, between):
            for i in range(len(items) + 3):
                if i < len(items):
                    at_pe_scores(pe, i0 + i, items[i])
                if 2 <= i <= len(items) + 1:
                    at_pe_tr(pe, i0 + i - 2, items[i - 2])
                if i >= 3:
                    at_pe_pv(pe, i0 + i - 3, items[i - 3])
                between(i)

        def attention_act(act, items, i0, between):
            for i in range(len(items) + 3):
                if i < len(items):
                    at_act_exp(act, i0 + i, items[i])
                if i >= 3:
                    at_act_out(act, i0 + i - 3, items[i - 3])
                between(i)

        def attention_dve(dve, items, i0, between):
            for i in range(len(items) + 2):
                if i < len(items):
                    at_dve_mask(dve, i0 + i, items[i])
                if i >= 2:
                    at_dve_copy(dve, i0 + i - 2, items[i - 2])
                between(i)

        MEMU = [("mk", j) for j in range(4)] + [("mv", j) for j in range(4)]

        def mem_unit_at(i):
            return MEMU[i // 4] if i % 4 == 3 and i // 4 < len(MEMU) else None

        def both(ap, n=NT):
            return ap.unsqueeze(1).broadcast_to([ap.shape[0], n] + list(ap.shape[1:]))

        g16 = [gate8[:, j, :].rearrange("p (t h) -> p t h", t=NT) for j in range(8)]
        BETA, EG, A_EXP = g16[7], g16[5], gate8[:, 3, 0:8]

        def gates2_act(act):
            N.wait(act, g2_in)
            act.activation(gate8[:, 2, :], gate8[:, 1, :], ACT.Exp).then_inc(g2_a, 1)
            act.activation(A_EXP, bc8[:, 1, :], ACT.Exp).then_inc(g2_a, 1)
            act.activation(g16[6], aux[0][:, 0:32].rearrange("p (t c) -> p t c", t=NT)[:, :, 8:16], ACT.Tanh, scale=0.5).then_inc(g2_a, 1)
            act.wait_ge(g2_a, 1)
            act.activation(gate8[:, 4, :], gate8[:, 2, :], ACT.Ln, bias=1.0).then_inc(g2_a, 1)

        def gates2_dve_in(dve):
            N.wait(dve, ws_mm)
            dve.tensor_tensor(g16[0], aux[0][:, 0:32].rearrange("p (t c) -> p t c", t=NT)[:, :, 0:8], both(bc8[:, 2, :]), ALU.add)
            dve.drain()
            dve.scalar_tensor_tensor(g16[1], g16[0], -1.0, g16[0], ALU.mult, ALU.min).then_inc(g2_in, 1)

        def gates2_dve(dve):
            dve.wait_ge(g2_a, 4)
            dve.tensor_scalar(BETA, g16[6], 0.5, 0.5, ALU.mult, ALU.add)
            dve.scalar_tensor_tensor(g16[1], g16[0], 0.0, g16[4], ALU.max, ALU.add)
            dve.drain()
            dve.scalar_tensor_tensor(g16[2], g16[1], -1.0, both(A_EXP), ALU.mult, ALU.mult).then_inc(g2_g, 1)

        def gates2_pe(pe):
            pe.wait_ge(g2_g, 1)
            for t in range(NT):
                i = pe.transpose(aux[3][0:8, t * P:(t + 1) * P], gate8[:, 2, t * 8:(t + 1) * 8], ident())
            i.then_inc(g2_tr, 1)

        def gates2_dve_sum(dve):
            dve.wait_ge(g2_tr, 1)
            for t in range(NT):
                ts = slice(t * P, (t + 1) * P)
                dve.tensor_tensor_scan(cum[:, ts], sel_a[0:8, ts], aux[3][0:8, ts], 0.0, ALU.mult, ALU.add)
            dve.drain()
            dve.tensor_copy(sel_r[0:8, :], cum[:]).then_inc(g2_ct, 1)
            dve.tensor_scalar(sel_a[32:40, :], cum[:], -1.0, None, ALU.mult).then_inc(g2_ct, 1)

        def gates2_pool(pool):
            pool.wait_ge(g2_ct, 2)
            pool.tensor_tensor(sel_l[0:40], both(sel_a[0:40, :], 8),
                               cst[0:40, C_SEL:C_SEL + 8].unsqueeze(2).broadcast_to([40, 8, S]), ALU.mult).then_inc(g2_sel, 1)

        def gates2_pe_tm(pe):
            pe.wait_ge(g2_ct, 2)
            for t in range(NT):
                i = pe.transpose(aux[3][:, t * 8:(t + 1) * 8], cum[:, t * P:(t + 1) * P], cst[0:8, C_ID:C_ID + 8])
            i.then_inc(g2_tm, 1)

        def gates2_act_eg(act):
            act.wait_ge(g2_tm, 1)
            act.activation(gate8[:, 5, :], aux[3][:, 0:16], ACT.Exp).then_inc(g2_eg, 1)

        def rope(dve, v, heads, n, c_cos, c_sin, t):
            cos, sin = [cst[:, c + t * n:c + (t + 1) * n].unsqueeze(1).broadcast_to([P, heads, n]) for c in (c_cos, c_sin)]
            tmp = [rope_t[:, j, 0:heads * n].rearrange("p (h d) -> p h d", h=heads) for j in range(4)]
            x1, x2 = v[:, :, 0:n], v[:, :, n:2 * n]
            dve.tensor_tensor(tmp[0], x1, cos, ALU.mult)
            dve.tensor_tensor(tmp[1], x2, sin, ALU.mult)
            dve.tensor_tensor(tmp[2], x2, cos, ALU.mult)
            dve.tensor_tensor(tmp[3], x1, sin, ALU.mult)
            dve.drain()
            dve.tensor_tensor(x1, tmp[0], tmp[1], ALU.subtract)
            return dve.tensor_tensor(x2, tmp[2], tmp[3], ALU.add)

        def ik_act(act):
            act.wait_ge(ws_mm, 3)
            for t in range(NT):
                c = t * 72
                act.activation(iqk[:, t, IH:IH + 2, :], both(aux[1][:, c:c + ID]), ACT.Copy).then_inc(ik_done, 1)
                act.activation(iw[:, t, :], aux[1][:, c + ID:c + ID + IH], ACT.Copy, scale=float(IH * ID) ** -0.5).then_inc(ik_done, 1)

        def idx_rope_dve(dve):
            wait_copied(dve, "iq")
            dve.wait_ge(ik_done, 2 * NT)
            for t in range(NT):
                if t:
                    dve.wait_ge(rope_i, t)
                rope(dve, iqk[:, t], IH + 2, IR, C_ICOS, C_ISIN, t).then_inc(rope_i, 1)

        def idx_tr_pe(pe):
            pe.wait_ge(rope_i, NT)
            pe.wait_ge(g2_in, 1)
            pe.wait_ge(g2_a, 4)
            pe.wait_ge(ik_done, 2 * NT)
            for j in range(IH // 2 + 1):
                for t in range(NT):
                    i = pe.transpose(aux[j // 2][:, (j % 2) * S + t * P:(j % 2) * S + (t + 1) * P],
                                     iqk[:, t, 2 * j:2 * j + 2, :].rearrange("p h d -> p (h d)"), ident())
                if j % 2 or j == IH // 2:
                    i.then_inc(iqT_mm, 1)

        def idx_tr_act(act):
            for b in range(3):
                act.wait_ge(iqT_mm, b + 1)
                n = 2 if b < 2 else 1
                act.activation(iqkT[:, 2 * b:2 * b + n, :], aux[b][:, 0:n * S], ACT.Copy).then_inc(iqT_copied, 1)

        def idx_scores(eng, which, t, tick):
            for h in range(IH):
                j, nk = t * IH + h, (t + 1) * P
                r = 64 * (h % 2)
                if which == "pe":
                    pe = eng
                    pe.wait_ge(iqT_copied, 3)
                    if j >= 2:
                        pe.wait_ge(idx_relu, j - 1)
                    pe.matmul(aux[h % 2][:, 0:nk], iqkT[r:r + 64, h // 2, t * P:(t + 1) * P], iqkT[r:r + 64, IH // 2, 0:nk],
                              start=True, stop=True).then_inc(idx_mm, 1)
                elif which == "act":
                    act = eng
                    act.wait_ge(idx_mm, j + 1)
                    if j >= 2:
                        act.wait_ge(idx_acc, j - 1)
                    act.activation(relu_i[:, h % 2, 0:nk], aux[h % 2][:, 0:nk], ACT.Relu).then_inc(idx_relu, 1)
                else:
                    dve = eng
                    dve.wait_ge(idx_relu, j + 1)
                    if h == 0:
                        dve.tensor_scalar(score[:, t, 0:nk], relu_i[:, 0, 0:nk], iw[:, t, 0:1], None, ALU.mult).then_inc(idx_acc, 1)
                    else:
                        dve.wait_ge(idx_acc, j)
                        dve.scalar_tensor_tensor(score[:, t, 0:nk], relu_i[:, h % 2, 0:nk], iw[:, t, h:h + 1], score[:, t, 0:nk],
                                                 ALU.mult, ALU.add).then_inc(idx_acc, 1)

        def topk_dve(dve, t, tick):
            nk = (t + 1) * P
            sc, wk = score[:, t, 0:nk], work[:, 0:nk]
            dve.wait_ge(idx_acc, IH * (t + 1))
            dve.tensor_tensor(sc, sc, cst[:, C_CAUSAL + 2 * P - nk:C_CAUSAL + 2 * P], ALU.add)
            for r in range(TOPK // 8):
                dve.drain()
                src = sc if r == 0 else wk
                dve.max(top8[:], src)
                dve.drain()
                dve.match_replace(wk, top8[:], src, NEG)
                if r == 3:
                    tick()
            dve.drain()
            dve.tensor_tensor(wk, wk, sc, ALU.is_equal)
            dve.drain()
            dve.tensor_scalar(selb[:, t, 0:nk], wk, NEG, None, ALU.mult)
            dve.drain()

        XF = xn[:].rearrange("p t d -> p (t d)")

        def aqk_dve(dve, tick):
            wait_copied(dve, "akv")
            wait_copied(dve, "aq")
            n = (AH + AKV) * AD
            for t in range(NT):
                dve.tensor_tensor(XF[:, 0:n], aqk[:, t].rearrange("p h d -> p (h d)"), aqk[:, t].rearrange("p h d -> p (h d)"), ALU.mult)
                dve.drain()
                dve.tensor_reduce(hsum[:, 10 * t:10 * t + 10], XF[:, 0:n].rearrange("p (h d) -> p h d", d=AD), AX_X, ALU.add).then_inc(aqk_ss, 1)
                dve.drain()
                tick()
            for t in range(NT):
                dve.wait_ge(aqk_rms, 1)
                dve.tensor_tensor(aqk[:, t], aqk[:, t], hrms[:, 10 * t:10 * t + 10].unsqueeze(2).broadcast_to([P, AH + AKV, AD]), ALU.mult)
                dve.drain()
                dve.tensor_tensor(aqk[:, t, 0:AH], aqk[:, t, 0:AH], both(ghead[:, 0, :], AH), ALU.mult)
                dve.tensor_tensor(aqk[:, t, AH:], aqk[:, t, AH:], both(ghead[:, 1, :], AKV), ALU.mult)
                dve.drain()
                rope(dve, aqk[:, t], AH + AKV, AR, C_COS, C_SIN, t).then_inc(aqk_done, 1)
                dve.drain()
                tick()

        def aqk_pool(pool):
            pool.wait_ge(aqk_ss, NT)
            pool.tensor_scalar(hsum[:, 0:20], hsum[:, 0:20], 1.0 / AD, EPS, ALU.mult, ALU.add)
            pool.drain()
            pool.tensor_tensor(hrms[:, 0:20], hsum[:, 0:20], half[:, 0:20], ALU.pow).then_inc(aqk_rms, 1)

        def aqk_pe(pe, tick):
            for j in range(5):
                if j == 0:
                    pe.wait_ge(aqk_done, NT)
                    pe.wait_ge(idx_relu, NT * IH)
                    pe.wait_ge(g2_eg, 1)
                if j == 4:
                    pe.wait_ge(aT_copied, 1)
                for hh in range(2):
                    for t in range(NT):
                        i = pe.transpose(aux[j % 4][:, hh * S + t * P:hh * S + (t + 1) * P], aqk[:, t, 2 * j + hh, :], ident())
                i.then_inc(aT_mm, 1)

        def aqk_act(act):
            for j in range(5):
                act.wait_ge(aT_mm, j + 1)
                dst = aqT[:, 2 * j:2 * j + 2, :] if j < 4 else akT[:, 0:2, :]
                act.activation(dst, aux[j % 4][:], ACT.Copy).then_inc(aT_copied, 1)

        def qkv_act_in(act, j):
            u = of["qkv"][j]
            act.wait_ge(unit_done, u + 1)
            act.wait_ge(set2_done, 1)
            if j >= 2:
                act.wait_ge(conv_done, j - 1)
                act.wait_ge(conv2_done, j - 1)
            b = units[u]["banks"][0]
            act.activation(cin[:, j % 2, :, 3:3 + S], acc[b][:].rearrange("p (m s) -> p m s", m=2), ACT.Copy).then_inc(acc_free[b], 1)

        def conv_pool(pool, j):
            wait_read(pool, of["qkv"][j])
            pool.wait_ge(set2_done, 1)
            c = 2 * j + 1
            for tap in range(4):
                tw, src, dst = conv_h[:, c, tap:tap + 1], cin[:, j % 2, 1, tap:tap + S], qkvT[:, c, :]
                if tap:
                    pool.drain()
                pool.tensor_scalar(conv_t[:] if tap else dst, src, tw, None, ALU.mult)
                if tap:
                    pool.drain()
                    i = pool.tensor_tensor(dst, dst, conv_t[:], ALU.add)
            i.then_inc(conv_done, 1)

        def conv_dve(dve, j):
            wait_read(dve, of["qkv"][j])
            c = 2 * j
            for tap in range(4):
                tw, src, dst = conv_h[:, c, tap:tap + 1], cin[:, j % 2, 0, tap:tap + S], qkvT[:, c, :]
                if tap == 0:
                    i = dve.tensor_scalar(dst, src, tw, None, ALU.mult)
                else:
                    dve.drain()
                    i = dve.scalar_tensor_tensor(dst, src, tw, dst, ALU.mult, ALU.add)
            i.then_inc(conv2_done, 1)

        def qkv_act_tanh(act, j):
            act.wait_ge(conv_done, j + 1)
            act.wait_ge(conv2_done, j + 1)
            if j >= 2:
                act.wait_ge(qkv_done, j - 1)
            act.activation(tanh_c[:, j % 2, :], qkvT[:, 2 * j:2 * j + 2, :].rearrange("p m s -> p (m s)"), ACT.Tanh).then_inc(tanh_done, 1)

        def qkv_dve(dve, j):
            dve.wait_ge(tanh_done, j + 1)
            v = qkvT[:, 2 * j:2 * j + 2, :].rearrange("p m s -> p (m s)")
            dve.scalar_tensor_tensor(v, tanh_c[:, j % 2, :], 1.0, v, ALU.add, ALU.mult).then_inc(qkv_done, 1)

        def gate_act(act, tag, j):
            u = of[tag][j]
            act.wait_ge(unit_done, u + 1)
            base = {"z": 0, "ga": 4, "gb": 8}[tag] + (j // 2) * 2
            for t in range(NT):
                n = base + t
                if n >= 2:
                    wait_read(act, u - 2)
                act.activation(tanh_g[:, n % 2, :], acc[units[u]["banks"][t]][:], ACT.Tanh, scale=0.5).then_inc(gate_tanh, 1)

        def gate_dve(dve, tag, j):
            u = of[tag][j]
            g = j // 2
            cs = slice(g * 512, (g + 1) * 512)
            base = {"z": 0, "ga": 4, "gb": 8}[tag] + 2 * g
            for t in range(NT):
                n, b = base + t, units[u]["banks"][t]
                dve.wait_ge(gate_tanh, n + 1)
                th = tanh_g[:, n % 2, :]
                if tag == "z":
                    i = dve.scalar_tensor_tensor(zg[:, t, cs], th, 1.0, acc[b][:], ALU.add, ALU.mult)
                elif tag == "ga":
                    i = dve.scalar_tensor_tensor(zg[:, t, cs], th, 1.0, zg[:, t, cs], ALU.add, ALU.mult)
                else:
                    i = dve.scalar_tensor_tensor(xn[:, t, cs], th, 1.0, xn[:, t, cs], ALU.add, ALU.mult)
                i.then_inc(acc_free[b], 1)

        def gate_norm_dve(dve):
            for t in range(NT):
                v = zg[:, t, :].rearrange("p (h d) -> p h d", d=GD)
                dve.tensor_tensor(v, v, both(gq4[:], GH), ALU.mult)

        TOK = [(kind, n, g) for kind in (1, 0, 2) for n in range(NT) for g in range(2)]

        def tok_pe(pe, b):
            kind, n, g = TOK[b]
            if b >= 4:
                pe.wait_ge(tok_copied, b - 3)
            for hh in range(4):
                i = pe.transpose(aux[b % 4][:, hh * P:(hh + 1) * P], qkvT[:, kind * 8 + 4 * g + hh, n * P:(n + 1) * P], ident())
            i.then_inc(tok_mm, 1)

        def tok_act(act, b):
            kind, n, g = TOK[b]
            act.wait_ge(tok_mm, b + 1)
            if kind < 2:
                if b >= 2:
                    act.wait_ge(tok_ss, b - 1)
                act.activation(sqb[:, b % 2, :], aux[b % 4][:], ACT.Square).then_inc(tok_sq, 1)
            dst = {1: khat, 0: qh, 2: vb}[kind][:, n, 4 * g:4 * g + 4, :]
            act.activation(dst, aux[b % 4][:].rearrange("p (h d) -> p h d", h=4), ACT.Copy).then_inc(tok_copied, 1)

        def tok_dve(dve, b):
            kind, n, g = TOK[b]
            if kind < 2:
                dve.wait_ge(tok_sq, b + 1)
                c = 20 + (0 if kind == 1 else 16) + 8 * n + 4 * g
                dve.tensor_reduce(hsum[:, c:c + 4], sqb[:, b % 2, :].rearrange("p (h d) -> p h d", d=GD), AX_X, ALU.add).then_inc(tok_ss, 1)

        def tok_rms_pool(pool):
            pool.wait_ge(tok_ss, 8)
            pool.tensor_scalar(hsum[:, 20:52], hsum[:, 20:52], EPS, None, ALU.add)
            pool.drain()
            pool.tensor_tensor(hrms[:, 20:52], hsum[:, 20:52], half[:], ALU.pow)
            pool.drain()
            pool.tensor_scalar(hrms[:, 36:52], hrms[:, 36:52], float(GD) ** -0.5, None, ALU.mult).then_inc(tok_rms, 1)

        def per_head(ap):
            return ap.unsqueeze(2).broadcast_to([P, GH, GD])

        def tok_scale_dve(dve, tick):
            dve.wait_ge(tok_rms, 1)
            dve.wait_ge(tok_copied, 12)
            dve.wait_ge(g2_eg, 1)
            for n in range(NT):
                dve.tensor_tensor(khat[:, n], khat[:, n], per_head(hrms[:, 20 + 8 * n:28 + 8 * n]), ALU.mult).then_inc(tok_done, 1)
                dve.tensor_tensor(qh[:, n], qh[:, n], per_head(hrms[:, 36 + 8 * n:44 + 8 * n]), ALU.mult).then_inc(tok_done, 1)
                dve.wait_ge(tok_done, 5 * n + 1)
                dve.tensor_tensor(kb[:, n], khat[:, n], per_head(BETA[:, n, :]), ALU.mult).then_inc(tok_done, 1)
                tick()
                dve.tensor_tensor(vb[:, n], vb[:, n], per_head(BETA[:, n, :]), ALU.mult).then_inc(tok_done, 1)
                dve.wait_ge(tok_done, 5 * n + 3)
                if n:
                    dve.tensor_tensor(kbg[:], kb[:, n], per_head(EG[:, n, :]), ALU.mult).then_inc(tok_done, 1)
                else:
                    dve.engine_nop().then_inc(tok_done, 1)
                    tick()

        BACK = [(kind, n, g) for kind in range(3) for n in range(NT) for g in range(2)]

        def back_pe(pe, b):
            kind, n, g = BACK[b]
            if b == 0:
                pe.wait_ge(tok_done, 10)
            if b >= 4:
                pe.wait_ge(back_copied, b - 3)
            src = (khat, kb, qh)[kind]
            for hh in range(4):
                i = pe.transpose(aux[b % 4][:, hh * P:(hh + 1) * P], src[:, n, 4 * g + hh, :], ident())
            i.then_inc(back_mm, 1)

        def back_act(act, b):
            kind, n, g = BACK[b]
            act.wait_ge(back_mm, b + 1)
            dst = khT[:, n, 4 * g:4 * g + 4, :] if kind == 0 else kbqT[:, kind - 1, n, 4 * g:4 * g + 4, :]
            act.activation(dst, aux[b % 4][:].rearrange("p (h s) -> p h s", h=4), ACT.Copy).then_inc(back_copied, 1)

        def dt_pe(pe, b):
            n, g = b // 2, b % 2
            if b == 0:
                pe.wait_ge(back_copied, 12)
                pe.wait_ge(g2_sel, 1)
            for hh in range(4):
                ts = slice(n * P, (n + 1) * P)
                i = pe.matmul(aux[b][:, hh * P:(hh + 1) * P], sel_l[0:40, 4 * g + hh, ts], sel_r[0:40, ts], start=True, stop=True)
            i.then_inc(dt_mm, 1)

        def dt_dve(dve, b):
            n, g = b // 2, b % 2
            dve.wait_ge(dt_mm, b + 1)
            dve.tensor_tensor(DT[:, n, 4 * g:4 * g + 4, :], aux[b][:].rearrange("p (h s) -> p h s", h=4),
                              both(cst[:, C_DMASK:C_DMASK + P], 4), ALU.add).then_inc(dt_add, 1)

        def dt_act(act, b):
            n, g = b // 2, b % 2
            act.wait_ge(dt_add, b + 1)
            v = DT[:, n, 4 * g:4 * g + 4, :]
            act.activation(v, v, ACT.Exp).then_inc(dt_done, 1)

        def kdec_dve(dve):
            dve.wait_ge(dt_done, 2)
            dve.tensor_tensor(kdec[:], khat[:, 0], DT[:, 0, :, P - 1:P].broadcast_to([P, GH, GD]), ALU.mult).then_inc(kdec_done, 1)
            dve.wait_ge(kdec_done, 1)

        def ap_pe(pe, b):
            n, h = b // 4, 2 * (b % 4)
            if b < 4:
                pe.wait_ge(dt_add, b + 1)
            else:
                pe.wait_ge(ap_done, b - 3)
            for hh in range(2):
                i = pe.matmul(aux[b % 4][:, hh * S:(hh + 1) * S], khT[:, n, h + hh, :], kbqT[:, :, n, h + hh, :], start=True, stop=True)
            i.then_inc(ap_mm, 1)

        def ap_dve(dve, b):
            n, h = b // 4, 2 * (b % 4)
            dve.wait_ge(ap_mm, b + 1)
            dve.wait_ge(dt_done, 2 * n + 1 + (b % 4) // 2)
            for hh in range(2):
                i = dve.tensor_tensor(APT[:, n, h + hh], aux[b % 4][:, hh * S:(hh + 1) * S].rearrange("p (k s) -> p k s", k=2),
                                      both(DT[:, n, h + hh, :]), ALU.mult)
            i.then_inc(ap_done, 1)

        def level(l):
            return both(cst[:, C_LEVEL + l * P:C_LEVEL + (l + 1) * P], 4)

        def inv_pool(pool, n):
            for l in range(LEVELS):
                for g in range(2):
                    if l == 0:
                        pool.wait_ge(ap_done, 8)
                        if n:
                            pool.wait_ge(y_mm, (LEVELS * n - 1) * 2 + g + 1)
                    elif l == 1:
                        pool.wait_ge(u_done, 2 * LEVELS * n + g + 1)
                    else:
                        pool.wait_ge(y_mm, 2 * (LEVELS * n + l - 1) + g + 1)
                    pool.tensor_tensor(Bt[:, g], APT[:, n, 4 * g:4 * g + 4, 0, :], level(l), ALU.mult).then_inc(bt_done, 1)

        def inv_pe(pe, n):
            for l in range(LEVELS):
                e = LEVELS * n + l
                for g in range(2):
                    if l == 0:
                        pe.wait_ge(u_done, 2 * e + g + 1)
                        if n:
                            pe.wait_ge(r_copied, 6)
                        for hh in range(4):
                            i = pe.transpose(aux[g][:, hh * P:(hh + 1) * P], Um[:, g, hh, :], ident())
                    else:
                        pe.wait_ge(bt_done, 2 * e + g + 1)
                        if l == 1:
                            pe.wait_ge(y_copied, 2 * (e - 1) + g + 1)
                        else:
                            pe.wait_ge(t_done, 2 * ((LEVELS - 2) * n + l - 2) + g + 1)
                        for hh in range(4):
                            i = pe.matmul(aux[g][:, hh * P:(hh + 1) * P], Bt[:, g, hh, :], Tm[:, g, hh, :], start=True, stop=True)
                    i.then_inc(y_mm, 1)
                if l == 0:
                    continue
                for g in range(2):
                    pe.wait_ge(y_copied, 2 * e + g + 1)
                    pe.wait_ge(u_done, 2 * e + g)
                    if l < LEVELS - 1:
                        for hh in range(4):
                            i = pe.matmul(aux[2][:, hh * P:(hh + 1) * P], Um[:, g, hh, :], Yb[:, g, hh, :], start=True, stop=True)
                        i.then_inc(ty_mm, 1)
                    for hh in range(4):
                        i = pe.matmul(aux[3][:, hh * P:(hh + 1) * P], Yb[:, g, hh, :], Um[:, g, hh, :], start=True, stop=True)
                    i.then_inc(yu_mm, 1)

        def inv_act(act, n):
            for l in range(LEVELS):
                e = LEVELS * n + l
                for g in range(2):
                    act.wait_ge(y_mm, 2 * e + g + 1)
                    dst = Tm if l == 0 else Yb
                    act.activation(dst[:, g], aux[g][:].rearrange("p (h s) -> p h s", h=4), ACT.Copy).then_inc(y_copied, 1)

        def inv_dve(dve, n):
            for l in range(LEVELS):
                e = LEVELS * n + l
                for g in range(2):
                    if l == 0:
                        dve.wait_ge(bt_done, 2 * e + g + 1)
                        if n:
                            dve.wait_ge(r_copied, 2)
                        dve.tensor_tensor(Um[:, g], both(cst[:, C_ID:C_ID + P], 4), Bt[:, g], ALU.subtract).then_inc(u_done, 1)
                        continue
                    if l < LEVELS - 1:
                        dve.wait_ge(ty_mm, 2 * ((LEVELS - 2) * n + l - 1) + g + 1)
                        dve.tensor_tensor(Tm[:, g], Tm[:, g], aux[2][:].rearrange("p (h s) -> p h s", h=4), ALU.subtract).then_inc(t_done, 1)
                    dve.wait_ge(yu_mm, 2 * ((LEVELS - 1) * n + l - 1) + g + 1)
                    dve.tensor_tensor(Um[:, g], Um[:, g], aux[3][:].rearrange("p (h s) -> p h s", h=4), ALU.subtract).then_inc(u_done, 1)

        wTn = kbqT[:, 1, 0]

        def heads(pe, bank, g, f):
            for hh in range(4):
                parts = f(4 * g + hh, hh)
                for j, (a, b) in enumerate(parts):
                    i = pe.matmul(bank[:, hh * P:(hh + 1) * P], a, b, start=j == 0, stop=j == len(parts) - 1)
            return i

        def res_pe(pe, n):
            base = 6 * n
            pe.wait_ge(u_done, 2 * LEVELS * (n + 1))
            if n == 0:
                pe.wait_ge(kdec_done, 1)
                for g in range(2):
                    heads(pe, aux[g], g, lambda h, hh: [(Um[:, g, hh, :], vb[:, 0, h, :])]).then_inc(r_mm, 1)
                for g in range(2):
                    pe.wait_ge(r_copied, g + 1)
                    heads(pe, aux[2 + g], g, lambda h, hh: [(APT[:, 0, h, 1, :], vnew[:, h, :])]).then_inc(r_mm, 1)
                for g in range(2):
                    heads(pe, aux[g], g, lambda h, hh: [(kdec[:, h, :], vnew[:, h, :])]).then_inc(r_mm, 1)
            else:
                for g in range(2):
                    heads(pe, aux[g], g, lambda h, hh: [(kbg[:, h, :], Um[:, g, hh, :])]).then_inc(r_mm, 1)
                for g in range(2):
                    heads(pe, aux[2 + g], g, lambda h, hh: [(kbqT[:, 1, 1, h, :], S1[:, h, :])]).then_inc(qs_mm, 1)
                for g in range(2):
                    pe.wait_ge(r_copied, base + g + 1)
                    heads(pe, aux[g], g, lambda h, hh: [(Um[:, g, hh, :], vb[:, 1, h, :]), (wTn[:, h, :], S1[:, h, :])]).then_inc(r_mm, 1)
                for g in range(2):
                    pe.wait_ge(r_copied, base + 2 + g + 1)
                    pe.wait_ge(qs_done, g + 1)
                    heads(pe, aux[2 + g], g, lambda h, hh: [(APT[:, 1, h, 1, :], vnew[:, h, :])]).then_inc(o_mm, 1)

        def res_act(act, n):
            dst = [(vnew, 1.0), (vb[:, 0], 1.0), (S1, 1.0)] if n == 0 else [(wTn, -1.0), (vnew, 1.0)]
            base = 6 * n
            for k, (d, s) in enumerate(dst):
                for g in range(2):
                    act.wait_ge(r_mm, base + 2 * k + g + 1)
                    bank = aux[g] if n or k != 1 else aux[2 + g]
                    act.activation(d[:, 4 * g:4 * g + 4, :], bank[:].rearrange("p (h d) -> p h d", h=4), ACT.Copy, scale=s).then_inc(r_copied, 1)

        def res_dve(dve):
            for g in range(2):
                dve.wait_ge(qs_mm, g + 1)
                dve.tensor_tensor(sqb[:, g, :].rearrange("p (h d) -> p h d", h=4), aux[2 + g][:].rearrange("p (h d) -> p h d", h=4),
                                  EG[:, 1, 4 * g:4 * g + 4].unsqueeze(2).broadcast_to([P, 4, GD]), ALU.mult).then_inc(qs_done, 1)
            for g in range(2):
                dve.wait_ge(o_mm, g + 1)
                dve.wait_ge(qs_done, g + 1)
                dve.tensor_tensor(vb[:, 1, 4 * g:4 * g + 4, :], aux[2 + g][:].rearrange("p (h d) -> p h d", h=4),
                                  sqb[:, g, :].rearrange("p (h d) -> p h d", h=4), ALU.add)
            dve.drain()

        def merge_dve(dve):
            dve.wait_ge(r_copied, 4)
            for n in range(NT):
                o = vb[:, n]
                dve.tensor_tensor(APT[:, 0, 0:4].rearrange("p h k s -> p (h k s)"), o.rearrange("p h d -> p (h d)"), o.rearrange("p h d -> p (h d)"), ALU.mult)
                dve.drain()
                dve.tensor_reduce(hsum[:, 52 + 8 * n:60 + 8 * n], APT[:, 0, 0:4].rearrange("p h k s -> p (h k) s"), AX_X, ALU.add).then_inc(o_ss, 1)
                dve.drain()
            dve.wait_ge(o_rms, 1)
            for n in range(NT):
                o = vb[:, n]
                dve.tensor_tensor(o, o, per_head(hrms[:, 52 + 8 * n:60 + 8 * n]), ALU.mult)
                dve.drain()
                of_ = o.rearrange("p h d -> p (h d)")
                dve.tensor_tensor(of_, of_, zg[:, n, :], ALU.mult)
                dve.drain()
                dve.scalar_tensor_tensor(xn[:, n, :], xn[:, n, :], 0.5, of_, ALU.mult, ALU.add).then_inc(merged_done, 1)

        def merge_pool(pool):
            pool.wait_ge(o_ss, NT)
            pool.tensor_scalar(hsum[:, 52:68], hsum[:, 52:68], 1.0 / GD, EPS, ALU.mult, ALU.add)
            pool.drain()
            pool.tensor_tensor(hrms[:, 52:68], hsum[:, 52:68], half[:, 0:16], ALU.pow).then_inc(o_rms, 1)

        def plain_add(dve, tag):
            for g in range(2):
                u = of[tag][(g + 1) * len(of[tag]) // 2 - 1]
                dve.wait_ge(unit_done, u + 1)
                for t in range(NT):
                    b, cs = units[u]["banks"][t], slice(g * 512, (g + 1) * 512)
                    dve.tensor_tensor(x[:, t, cs], x[:, t, cs], acc[b][:], ALU.add).then_inc(acc_free[b], 1)

        def wait_added(eng, tag, g, t):
            b, n = released(of[tag][(g + 1) * len(of[tag]) // 2 - 1])[t]
            eng.wait_ge(acc_free[b], n)

        GATES = [("z", j) for j in range(4)] + [("ga", j) for j in range(4)] + [("gb", j) for j in range(4)]

        def gate_pair(q):
            return GATES[q - 1] if q >= 2 and q % 2 == 0 else None

        DSA_UNITS = {1: 6, 4: 7, 7: 8, 10: 9, 13: 10, 15: 11}

        block = ctx.enter_context(nc.Block())

        @block.sync
        def _(sp):
            xr = w["x"][0].rearrange("(t p) d -> p t d", p=P)
            for t in range(NT):
                sp.dma_start(x[:, t, :], xr[:, t, :]).then_inc(x_in, 16)
            sp.dma_start(cst[:, 0:P], consts[:, 0:P]).then_inc(id_in, 16)
            sp.dma_start(sm[:, 0:V_NARROW], small[:, 0:V_NARROW]).then_inc(gain_in, 16)
            gpos = {of["fk"][0]: ("g_mix_post", 0), of["mo"][0]: ("g_mem_post", 4), of["ff2"][0]: ("g_ff_post", 8)}
            for u in range(NU):
                if u == 2:
                    sp.dma_start(sm[:, V_NARROW:], small[:, V_NARROW:]).then_inc(small_in, 16)
                    sp.dma_start(cst[:, P:], consts[:, P:]).then_inc(cst_in, 16)
                if u == 3:
                    sp.dma_start(mem[:], w["mem"][0].rearrange("(t p) d -> p t d", p=P)).then_inc(mem_in, 16)
                if u == 5:
                    sp.dma_start(relb[:], rel).then_inc(rel_in, 16)
                if u in gpos:
                    name, n = gpos[u]
                    if n:
                        sp.wait_ge(x_done, n)
                    sp.dma_start(gpost[:], w[name].broadcast_to([P, D])).then_inc(gpost_in, 16)
                if u >= RAW_SLOTS:
                    sp.wait_ge(w_lo_done, u - RAW_SLOTS + 1)
                dst = w_raw[u % RAW_SLOTS][:].rearrange("p (c n) -> p c n", c=units[u]["src"].shape[1])
                sp.dma_start(dst, units[u]["src"]).then_inc(w_loaded[u % RAW_SLOTS], 16)
            for g in range(2):
                for t in range(NT):
                    wait_added(sp, "down", g, t)
                    cs = slice(g * 512, (g + 1) * 512)
                    sp.dma_start(out[t * P:(t + 1) * P, cs], x[:, t, cs]).then_inc(stored, 16)
            sp.wait_ge(stored, 16 * 2 * NT)

        @block.gpsimd
        def _(pool):
            rstd_pool(pool, "mix")
            rstd_pool(pool, "mem")
            pool.wait_ge(gate_ct, 4)
            pool.wait_ge(cst_in, 16)
            pool.tensor_tensor(sel_l[:], sel_a[:].unsqueeze(1).broadcast_to([104, 8, S]),
                               cst[0:104, C_SEL:C_SEL + 8].unsqueeze(2).broadcast_to([104, 8, S]), ALU.mult).then_inc(sel_done, 1)
            rstd_y_pool(pool, 0)
            rstd_y_pool(pool, 1)
            for n in ("p_out", "mpre", "p_mo", "ff", "p_ff2"):
                rstd_pool(pool, n)
            rstd_pool(pool, "mix2")
            gates2_pool(pool)
            conv_pool(pool, 0)
            conv_pool(pool, 1)
            aqk_pool(pool)
            for j in range(2, 12):
                conv_pool(pool, j)
            tok_rms_pool(pool)
            inv_pool(pool, 0)
            inv_pool(pool, 1)
            merge_pool(pool)
            rstd_pool(pool, "mlp2")

        @block.scalar
        def _(act):
            def x_piece(g, t):
                if g == 0:
                    act.wait_ge(x_in, 16 * NT)
            nt_act_stats(act, "mix", x, x_piece)
            for u in range(AHEAD):
                unit_hi(act, u)
            act.wait_ge(gain_in, 16)
            nt_act(act, "mix", h_hi)
            act_unit(act, "fq", 0)
            act_unit(act, "fq", 1)
            act.wait_ge(small_in, 16)
            act.activation(ws_hi[:], ws_raw, ACT.Copy).then_inc(ws_hi_done, 1)
            for tag in ("fk", "fv"):
                for j in range(2):
                    act_unit(act, tag, j)
            N.wait(act, gate_v)
            act.activation(gate8[:, 2, :], gate8[:, 1, :], ACT.Exp).then_inc(gate_a, 1)
            N.wait(act, gate_a)
            act.activation(gate8[:, 3, :], gate8[:, 2, :], ACT.Ln, bias=1.0).then_inc(gate_a, 1)
            act_unit(act, "cq", 0)
            act.wait_ge(mem_in, 16)
            nt_act_stats(act, "mem", mem)
            for tag, j in (("cq", 1), ("ck", 0), ("ck", 1)):
                act_unit(act, tag, j)
            nt_act(act, "mem", m_hi)
            for j in range(2):
                act_unit(act, "cv", j)

            def between(i):
                if mem_unit_at(i):
                    act_unit(act, *mem_unit_at(i))
                if i == len(FOX) // 2 + 3:
                    act.wait_ge(y_done, len(FOX) // 2)
                    for t in range(NT):
                        square(act, "y", 0, t, y[:, t, 0:512])
            attention_act(act, FOX, 0, between)
            act.wait_ge(y_done, len(FOX))
            for t in range(NT):
                square(act, "y", 1, t, y[:, t, 512:D])
            nt_act(act, "y", h_hi)
            for u in of["out"]:
                advance_hi(act, u)
            post_stats(act, "p_out", "out")
            nt_act_stats(act, "mpre", x, lambda g, t: N.wait(act, x_done))
            nt_act(act, "mpre", h_hi)
            for j in range(4):
                act_unit(act, "mq", j)
            attention_act(act, MEM, I_MEM, lambda i: None)
            nt_act(act, "memo", h_hi)
            for u in of["mo"]:
                advance_hi(act, u)
            post_stats(act, "p_mo", "mo")
            nt_act_stats(act, "ff", x, lambda g, t: N.wait(act, x_done))
            nt_act(act, "ff", h_hi)
            for j in range(16):
                advance_hi(act, of["ff1"][j])
                hid_act_relu(act, "ff1", j)
                if j >= 1:
                    hid_act_hi(act, "ff1", j - 1)
            hid_act_hi(act, "ff1", 15)
            for u in of["ff2"]:
                advance_hi(act, u)
            post_stats(act, "p_ff2", "ff2")
            nt_act_stats(act, "mix2", x, lambda g, t: N.wait(act, x_done))
            nt_act(act, "mix2", h_hi)
            act_unit(act, "akv", 0)
            act_unit(act, "akv", 1)
            act_unit(act, "iq", 0)
            act_unit(act, "iq", 1)
            ik_act(act)
            act_unit(act, "aq", 0)
            gates2_act(act)
            idx_tr_act(act)
            act_unit(act, "aq", 1)
            gates2_act_eg(act)
            for t in range(NT):
                idx_scores(act, "act", t, None)
            act_unit(act, "aq", 2)
            act_unit(act, "aq", 3)

            def qkv_tick(j):
                advance_hi(act, of["qkv"][j])
                qkv_act_in(act, j)
                if j >= 2:
                    qkv_act_tanh(act, j - 2)
            for j in range(6):
                qkv_tick(j)
            aqk_act(act)

            def between(i):
                if i in DSA_UNITS:
                    qkv_tick(DSA_UNITS[i])
            attention_act(act, DSA, I_DSA, between)
            qkv_act_tanh(act, 10)
            qkv_act_tanh(act, 11)
            act.wait_ge(qkv_done, 12)

            def gate_tick(q):
                advance_hi(act, of[GATES[q][0]][GATES[q][1]])
                if gate_pair(q):
                    gate_act(act, *gate_pair(q))
            for b in range(12):
                tok_act(act, b)
                if b % 3 == 2:
                    gate_tick(b // 3)
            for q in range(4, 7):
                gate_tick(q)
            for b in range(12):
                back_act(act, b)
                if b % 4 == 3:
                    gate_tick(7 + b // 4)
            for b in range(4):
                dt_act(act, b)
            gate_tick(10)
            gate_tick(11)
            gate_act(act, *GATES[11])
            for n in range(NT):
                inv_act(act, n)
                res_act(act, n)
            nt_act(act, "merged", h_hi)
            for u in of["out2"]:
                advance_hi(act, u)
            nt_act_stats(act, "mlp2", x, lambda g, t: wait_added(act, "out2", g, t))
            nt_act(act, "mlp2", h_hi)
            for j in range(16):
                advance_hi(act, of["up"][j])
                hid_act_relu(act, "up", j)
                if j >= 1:
                    hid_act_hi(act, "up", j - 1)
            hid_act_hi(act, "up", 15)
            for u in of["down"]:
                advance_hi(act, u)

        @block.vector
        def _(dve):
            dve.memset(half[:], -0.5).then_inc(set_done, 1)
            dve.memset(sel_a[:], 1.0)
            dve.memset(sel_r[:], 1.0)
            for u in range(AHEAD):
                unit_lo(dve, u)
            dve.wait_ge(id_in, 16)
            nt_dve_diag(dve, "mix")
            nt_dve(dve, "mix", h_hi, h_lo)
            for u in of["fq"]:
                advance_lo(dve, u)
            dve.wait_ge(ws_hi_done, 1)
            dve.tensor_tensor(ws_lo[:], ws_raw, ws_hi[:].bitcast(F32), ALU.subtract).then_inc(ws_lo_done, 1)
            for tag in ("fk", "fv"):
                for u in of[tag]:
                    advance_lo(dve, u)
            N.wait(dve, ws_mm)
            v8 = [gate8[:, j, :].rearrange("p (t h) -> p t h", t=NT) for j in range(5)]
            dve.tensor_tensor(v8[0], aux[0][:, 0:16].rearrange("p (t h) -> p t h", t=NT),
                              bc8[:, 0, :].unsqueeze(1).broadcast_to([P, NT, 8]), ALU.add)
            dve.drain()
            dve.scalar_tensor_tensor(v8[1], v8[0], -1.0, v8[0], ALU.mult, ALU.min).then_inc(gate_v, 1)
            advance_lo(dve, of["cq"][0])
            dve.wait_ge(gate_a, 2)
            dve.scalar_tensor_tensor(v8[4], v8[0], 0.0, v8[3], ALU.min, ALU.subtract).then_inc(gate_v, 1)
            dve.wait_ge(rel_in, 16)
            dve.memset(relb[0:CHUNK, :, 3 * CHUNK:4 * CHUNK], NEG).then_inc(rel_done, 1)
            advance_lo(dve, of["cq"][1])
            nt_dve_diag(dve, "mem")
            N.wait(dve, gate_tr)
            dve.tensor_tensor_scan(cum[:], sel_a[0:8, :], aux[1][0:8, 0:S], 0.0, ALU.mult, ALU.add)
            dve.drain()
            for r in (0, 64):
                dve.tensor_scalar(sel_r[r:r + 8, :], cum[:], -1.0, None, ALU.mult).then_inc(gate_ct, 1)
                dve.tensor_copy(sel_a[r + 32:r + 40, :], cum[:]).then_inc(gate_ct, 1)
            for u in of["ck"]:
                advance_lo(dve, u)
            nt_dve(dve, "mem", m_hi, m_lo)
            for u in of["cv"]:
                advance_lo(dve, u)

            def between(i):
                if mem_unit_at(i):
                    advance_lo(dve, of[mem_unit_at(i)[0]][mem_unit_at(i)[1]])
                if i == len(FOX) // 2 + 3:
                    nt_dve_diag(dve, "y", 0)
            attention_dve(dve, FOX, 0, between)
            nt_dve_diag(dve, "y", 1)
            nt_dve(dve, "y", h_hi, h_lo)
            for u in of["out"]:
                advance_lo(dve, u)
            post_add(dve, "p_out", "out", 1)
            nt_dve_diag(dve, "mpre")
            nt_dve(dve, "mpre", h_hi, h_lo)
            for u in of["mq"]:
                advance_lo(dve, u)
            attention_dve(dve, MEM, I_MEM, lambda i: None)
            nt_dve(dve, "memo", h_hi, h_lo)
            for u in of["mo"]:
                advance_lo(dve, u)
            post_add(dve, "p_mo", "mo", 2)
            nt_dve_diag(dve, "ff")
            nt_dve(dve, "ff", h_hi, h_lo)
            for j in range(16):
                advance_lo(dve, of["ff1"][j])
                hid_dve_sq(dve, "ff1", j)
                if j >= 1:
                    hid_dve_lo(dve, "ff1", j - 1)
            hid_dve_lo(dve, "ff1", 15)
            for u in of["ff2"]:
                advance_lo(dve, u)
            post_add(dve, "p_ff2", "ff2", 3)
            dve.memset(cin[:, :, :, 0:3], 0.0)
            dve.tensor_scalar(conv_h[:], sm[:, V_CONV:].rearrange("p (c k) -> p c k", k=4), 0.5, None, ALU.mult)
            dve.tensor_scalar(gq4[:], ghead[:, 2, :], 0.25, None, ALU.mult).then_inc(set2_done, 1)
            nt_dve_diag(dve, "mix2")
            nt_dve(dve, "mix2", h_hi, h_lo)
            for tag in ("akv", "iq"):
                for u in of[tag]:
                    advance_lo(dve, u)
            gates2_dve_in(dve)
            idx_rope_dve(dve)
            advance_lo(dve, of["aq"][0])
            gates2_dve(dve)
            advance_lo(dve, of["aq"][1])
            gates2_dve_sum(dve)
            for t in range(NT):
                idx_scores(dve, "dve", t, None)
            advance_lo(dve, of["aq"][2])
            advance_lo(dve, of["aq"][3])
            ticks = [0]

            def qkv_tick(j):
                advance_lo(dve, of["qkv"][j])
                if j >= 1:
                    conv_dve(dve, j - 1)
                if j >= 3:
                    qkv_dve(dve, j - 3)

            def tick():
                qkv_tick(ticks[0])
                ticks[0] += 1
            topk_dve(dve, 0, tick)
            topk_dve(dve, 1, tick)
            aqk_dve(dve, tick)

            def between(i):
                if i in DSA_UNITS:
                    qkv_tick(DSA_UNITS[i])
            attention_dve(dve, DSA, I_DSA, between)
            qkv_dve(dve, 9)
            conv_dve(dve, 11)
            qkv_dve(dve, 10)
            qkv_dve(dve, 11)

            def gate_tick(q):
                advance_lo(dve, of[GATES[q][0]][GATES[q][1]])
                if gate_pair(q):
                    gate_dve(dve, *gate_pair(q))
            for b in range(12):
                tok_dve(dve, b)
                if b % 3 == 2:
                    gate_tick(b // 3)
            ticks = [4]

            def tick():
                gate_tick(ticks[0])
                ticks[0] += 1
            tok_scale_dve(dve, tick)
            for q in range(7, 10):
                gate_tick(q)
            for b in range(4):
                dt_dve(dve, b)
            kdec_dve(dve)
            for b in range(8):
                ap_dve(dve, b)
            gate_tick(10)
            gate_tick(11)
            gate_dve(dve, *GATES[11])
            inv_dve(dve, 0)
            gate_norm_dve(dve)
            inv_dve(dve, 1)
            res_dve(dve)
            merge_dve(dve)
            nt_dve(dve, "merged", h_hi, h_lo)
            for u in of["out2"]:
                advance_lo(dve, u)
            plain_add(dve, "out2")
            nt_dve_diag(dve, "mlp2")
            nt_dve(dve, "mlp2", h_hi, h_lo)
            for j in range(16):
                advance_lo(dve, of["up"][j])
                hid_dve_sq(dve, "up", j)
                if j >= 1:
                    hid_dve_lo(dve, "up", j - 1)
            hid_dve_lo(dve, "up", 15)
            for u in of["down"]:
                advance_lo(dve, u)
            plain_add(dve, "down")

        @block.tensor
        def _(pe):
            nt_count = [0]

            def nt(n, src):
                nt_pe(pe, n, src)
                nt_count[0] += 1

            def mm(tag, *js, hi=h_hi, lo=h_lo, narrow=(), fresh=False):
                for j in js or range(len(of[tag])):
                    first = fresh and j < (2 if units[of[tag][j]]["form"] == "A" else 1)
                    unit_mm(pe, of[tag][j], hi, lo, narrow, nt_count[0] - 1 if first else None)

            pe.wait_ge(x_in, 16 * NT)
            pe.wait_ge(id_in, 16)
            nt("mix", x)
            mm("fq", fresh=True)
            mm("fk")
            pe.wait_ge(ws_lo_done, 1)
            mm("fv", narrow=[(aux[0], 0, 8)])
            mm("cq")
            pe.wait_ge(gate_v, 2)
            for t in range(NT):
                i = pe.transpose(aux[1][0:8, t * P:(t + 1) * P], gate8[:, 4, t * 8:(t + 1) * 8], ident())
            i.then_inc(gate_tr, 1)
            mm("ck")
            pe.wait_ge(gate_ct, 1)
            pe.wait_ge(mem_in, 16)
            nt("mem", mem)
            mm("cv")
            pe.wait_ge(nt_lo, KC * nt_count[0])
            pe.wait_ge(sel_done, 1)
            pe.wait_ge(cst_in, 16)

            def between(i):
                if mem_unit_at(i):
                    tag, j = mem_unit_at(i)
                    mm(tag, j, hi=m_hi, lo=m_lo)
            wait_copied(pe, "cv")
            attention_pe(pe, FOX, 0, between)
            pe.wait_ge(l_done, len(FOX))
            nt_pe(pe, "y", y, (0, 1))
            pe.wait_ge(y_done, len(FOX))
            nt_pe(pe, "y", y, (2, 3))
            nt_count[0] += 1
            mm("out", fresh=True)
            nt("mpre", x)
            mm("mq", fresh=True)
            wait_copied(pe, "mq")
            attention_pe(pe, MEM, I_MEM, lambda i: None)
            pe.wait_ge(y_done, len(FOX) + len(MEM))
            nt("memo", y)
            mm("mo", fresh=True)
            nt("ff", x)
            mm("ff1", fresh=True)
            pe.wait_ge(hid_lo_done, 16)
            mm("ff2", hi=hid_hi, lo=hid_lo)
            nt("mix2", x)
            mm("akv", fresh=True)
            mm("iq", narrow=[(aux[0], 8, 16), (aux[1], 24, 72)])
            mm("aq", 0)
            gates2_pe(pe)
            idx_tr_pe(pe)
            mm("aq", 1)
            gates2_pe_tm(pe)
            for t in range(NT):
                idx_scores(pe, "pe", t, None)
            mm("aq", 2, 3)
            mm("qkv", *range(6))
            aqk_pe(pe, None)
            pe.wait_ge(aT_copied, 5)
            wait_copied(pe, "akv")

            def between(i):
                if i in DSA_UNITS:
                    mm("qkv", DSA_UNITS[i])
            attention_pe(pe, DSA, I_DSA, between)
            pe.wait_ge(qkv_done, 12)
            pe.wait_ge(y_done, I_DSA + len(DSA))
            for b in range(12):
                tok_pe(pe, b)
                if b % 3 == 2:
                    mm("z", b // 3)
            mm("ga", 0, 1, 2)
            for b in range(12):
                back_pe(pe, b)
                if b == 3:
                    mm("ga", 3)
                if b == 7:
                    mm("gb", 0)
                if b == 11:
                    mm("gb", 1)
            for b in range(4):
                dt_pe(pe, b)
            for b in range(8):
                ap_pe(pe, b)
            mm("gb", 2, 3)
            for n in range(NT):
                inv_pe(pe, n)
                res_pe(pe, n)
            pe.wait_ge(r_copied, 10)
            pe.wait_ge(merged_done, NT)
            nt("merged", xn)
            mm("out2", fresh=True)
            nt("mlp2", x)
            mm("up", fresh=True)
            pe.wait_ge(hid_lo_done, 32)
            mm("down", hi=hid_hi, lo=hid_lo)


_STREAMED = ["x", "mem", "w_in", "w_mk", "w_mv", "w_out", "w_mq", "w_mo", "w_ff1", "w_ff2", "g_mix_post", "g_mem_post",
             "g_ff_post", "w_in_2", "w_out_2", "w_mlp_up_2", "w_mlp_down_2"]


def kernel(**inputs):
    import concourse.bacc as _bacc
    from concourse.bass_utils import run_bass_kernel_spmd as _run

    a = {name: np.asarray(v) for name, v in inputs.items()}
    nc = _bacc.Bacc("TRN2", target_bir_lowering=False, num_devices=1)
    arrays = {f"in_{name}": np.ascontiguousarray(a[name]) for name in _STREAMED}
    arrays["in_constants"] = constants()
    arrays["in_small"] = small_inputs(a)
    arrays["in_rel_rows"] = rel_rows(a["rel_bias"])
    aps = {name: nc.dram_tensor(name, v.shape, mybir.dt.from_np(v.dtype), kind="ExternalInput").ap()
           for name, v in arrays.items()}
    out = nc.dram_tensor("out_dram", (S, D), F32, kind="ExternalOutput").ap()
    build_program(nc, {name: aps[f"in_{name}"] for name in _STREAMED}, aps["in_constants"], aps["in_small"],
                  aps["in_rel_rows"], out)
    r = _run(nc, [arrays], core_ids=[0])
    return r.results[0]["out_dram"].reshape(1, S, D)
```

```python
from contextlib import ExitStack

import numpy as np
import concourse.bass as bass
from concourse import mybir

F32 = mybir.dt.float32
F32R = mybir.dt.float32r
ALU = mybir.AluOpType
ACT = mybir.ActivationFunctionType
AX_X = mybir.AxisListType.X

P = 128
S = 256
NT = S // P
D = 1024
KC = D // P
EPS = 1e-6
NEG = -1e30

FH, FD = 8, 64
DFOX = FH * FD
CHUNK, MAX_REL = 64, 128
MH, MD = 4, 256
FF = 4096
GH, GD = 8, 128
AH, AKV, AD = 8, 2, 128
IH, ID = 8, 64
TOPK = 64
ROPE_THETA = 500000.0
AR, IR = AD // 8, ID // 8

RAW_SLOTS = 3
SPLIT_SLOTS = 2
AHEAD = SPLIT_SLOTS - 1

C_ID, C_CAUSAL, C_ZERO, C_SEL, C_DMASK = 0, 128, 384, 640, 648
C_LEVEL = C_DMASK + P
LEVELS = 7
C_COS = C_LEVEL + LEVELS * P
C_SIN = C_COS + NT * AR
C_ICOS = C_SIN + NT * AR
C_ISIN = C_ICOS + NT * IR
N_CONST = C_ISIN + NT * IR

O_FQ, O_FK, O_FV, O_F, O_CQ, O_CK, O_CV = 0, 512, 1024, 1536, 1544, 2056, 2568
O_QKV, O_Z, O_GAB, O_AQ, O_AKV, O_IQ, O_IKW, O_GA, O_GB = 0, 3072, 4096, 4112, 5136, 5648, 6160, 6232, 7256


def constants():
    c = np.zeros((P, N_CONST), np.float32)
    r, f = np.arange(P)[:, None], np.arange(P)[None, :]
    c[:, C_ID:C_ID + P] = np.eye(P)
    c[:, C_CAUSAL + P:C_CAUSAL + 2 * P] = np.where(f > r, NEG, 0)
    for h in range(8):
        c[[h, 32 + h, 64 + h, 96 + h], C_SEL + h] = 1
    c[:, C_DMASK:C_DMASK + P] = np.where(f >= r, 0, NEG)
    for l in range(LEVELS):
        b = 1 << l
        c[:, C_LEVEL + l * P:C_LEVEL + (l + 1) * P] = (f // (2 * b) == r // (2 * b)) & (f % (2 * b) >= b) & (r % (2 * b) < b)
    for cc, cs, half in ((C_COS, C_SIN, AR), (C_ICOS, C_ISIN, IR)):
        inv = (np.float32(ROPE_THETA) ** (-np.arange(0, 2 * half, 2, dtype=np.float32) / np.float32(2 * half))).astype(np.float32)
        ang = np.arange(S, dtype=np.float32)[:, None] * inv[None, :]
        for t in range(NT):
            c[:, cc + t * half:cc + (t + 1) * half] = np.cos(ang[t * P:(t + 1) * P])
            c[:, cs + t * half:cs + (t + 1) * half] = np.sin(ang[t * P:(t + 1) * P])
    return c


def rel_rows(rel_bias):
    idx = np.clip(P + np.arange(P)[:, None] - np.arange(S)[None, :], -MAX_REL, MAX_REL) + MAX_REL
    return np.ascontiguousarray(np.transpose(rel_bias[0][:, idx], (1, 0, 2)))


V_GAIN, V_NARROW = 0, 8 * KC
V_BC8 = V_NARROW + KC * 96
V_HEAD = V_BC8 + 24
V_CONV = V_HEAD + 3 * P
N_SMALL = V_CONV + 24 * 4


def small_inputs(a):
    def chunks(g):
        return g.reshape(-1, P).T

    def rows(wgt, c0, n):
        return wgt[0][:, c0:c0 + n].reshape(KC, P, n).transpose(1, 0, 2)

    gains = [a["g_mem_kv"], a["g_mix_pre"], np.concatenate([a["g_fox_out"], a["g_chk_out"]], 1), a["g_mem_pre"],
             a["g_ff_pre"], a["norm_mix_g_2"], a["norm_mlp_g_2"], a["norm_mlp_g_2"]]
    narrow = np.concatenate([rows(a["w_in"], O_F, 8), rows(a["w_in_2"], O_GAB, 16), rows(a["w_in_2"], O_IKW, 72)], 2)
    vectors = [a["b_fgt"], a["a_log_2"], a["dt_bias_2"], a["q_norm_g_2"], a["k_norm_g_2"], a["gdn_norm_g_2"]]
    return np.ascontiguousarray(np.concatenate(
        [chunks(g) for g in gains] + [narrow.reshape(P, -1)] + [np.repeat(v, P, 0) for v in vectors]
        + [a["conv_w_2"][0].reshape(4, 24, P).transpose(2, 1, 0).reshape(P, -1)], 1))


def weight_units(w):
    units, of = [], {}

    def rows(name, c0, n, k0, kc):
        return w[name][0, k0 * P:(k0 + kc) * P, c0:c0 + n].rearrange("(c p) n -> p c n", p=P)

    def group(tag, form, name, c0, ncol, kchunks=KC):
        ids = []
        if form == "B":
            for c in range(c0, c0 + ncol, 256):
                ids.append(len(units))
                units.append(dict(form="B", src=rows(name, c, 256, 0, KC), banks=[None]))
        else:
            for c in range(c0, c0 + ncol, 512):
                for k in range(0, kchunks, 4):
                    ids.append(len(units))
                    units.append(dict(form="A", src=rows(name, c, 512, k, 4), k0=k, first=k == 0,
                                      last=k == kchunks - 4, banks=[None, None]))
        of[tag] = ids

    group("fq", "B", "w_in", O_FQ, 512)
    group("fk", "B", "w_in", O_FK, 512)
    group("fv", "A", "w_in", O_FV, 512)
    group("cq", "B", "w_in", O_CQ, 512)
    group("ck", "B", "w_in", O_CK, 512)
    group("cv", "A", "w_in", O_CV, 512)
    group("mk", "B", "w_mk", 0, D)
    group("mv", "A", "w_mv", 0, D)
    group("out", "A", "w_out", 0, D)
    group("mq", "B", "w_mq", 0, D)
    group("mo", "A", "w_mo", 0, D)
    group("ff1", "B", "w_ff1", 0, FF)
    group("ff2", "A", "w_ff2", 0, D, FF // P)
    group("akv", "A", "w_in_2", O_AKV, 512)
    group("iq", "A", "w_in_2", O_IQ, 512)
    group("aq", "A", "w_in_2", O_AQ, 1024)
    group("qkv", "B", "w_in_2", O_QKV, 3 * D)
    group("z", "A", "w_in_2", O_Z, D)
    group("ga", "A", "w_in_2", O_GA, D)
    group("gb", "A", "w_in_2", O_GB, D)
    group("out2", "A", "w_out_2", 0, D)
    group("up", "B", "w_mlp_up_2", 0, FF)
    group("down", "A", "w_mlp_down_2", 0, D, FF // P)
    for u in units:
        u["tiles"] = False
    for tag in ("out", "mo", "ff2", "out2", "down"):
        units[of[tag][-1]]["tiles"] = True
    bank, uses = 0, [0] * 4
    for u in units:
        if u["form"] == "B" or u["first"]:
            if u["form"] == "A" and bank % 2:
                raise ValueError("pairs of banks are aligned")
            u["banks"] = [(bank + i) % 4 for i in range(len(u["banks"]))]
            u["before"] = [uses[b] for b in u["banks"]]
            for b in u["banks"]:
                uses[b] += 1
            bank += len(u["banks"])
        else:
            u["banks"], u["before"] = units[units.index(u) - 1]["banks"], None
    return units, of


class Count:

    def __init__(self):
        self.seen = {}

    def wait(self, eng, sem, k=1):
        key = (id(eng), id(sem))
        self.seen[key] = self.seen.get(key, 0) + k
        eng.wait_ge(sem, self.seen[key])


def build_program(nc, w, consts, small, rel, out):
    units, of = weight_units(w)
    NU = len(units)
    ctx = ExitStack()
    with ctx:
        def sb(name, shape, dt=F32, at=ctx):
            return at.enter_context(nc.sbuf_tensor("s_" + name, shape, dt))

        def sem(name):
            return ctx.enter_context(nc.semaphore(name))

        w_raw = [sb(f"w_raw{i}", [P, 2048]) for i in range(RAW_SLOTS)]
        w_hi = [sb(f"w_hi{i}", [P, 2048], F32R) for i in range(SPLIT_SLOTS)]
        w_lo = [sb(f"w_lo{i}", [P, 2048], F32R) for i in range(SPLIT_SLOTS)]
        h_hi = sb("h_hi", [P, KC, S], F32R)
        h_lo = sb("h_lo", [P, KC, S], F32R)
        x = sb("x", [P, NT, D])
        xn = sb("xn", [P, NT, D])
        cst = sb("cst", [P, N_CONST])
        sm = sb("sm", [P, N_SMALL])
        gcol = sm[:, V_GAIN:V_NARROW].rearrange("p (j c) -> p j c", c=KC)
        ws_raw = sm[:, V_NARROW:V_BC8].rearrange("p (c n) -> p c n", c=KC)
        bc8 = sm[:, V_BC8:V_HEAD].rearrange("p (j h) -> p j h", h=8)
        ghead = sm[:, V_HEAD:V_CONV].rearrange("p (j d) -> p j d", d=P)
        gpost = sb("gpost", [P, D])
        ws_hi = sb("ws_hi", [P, KC, 96], F32R)
        ws_lo = sb("ws_lo", [P, KC, 96], F32R)
        stat = sb("stat", [P, 64])
        rstd = sb("rstd", [P, 64])
        nmax = sb("nmax", [P, 56])
        rsum = sb("rsum", [P, 56])
        rinv = sb("rinv", [P, 56])
        half = sb("half", [P, 32])
        junk = sb("junk", [P, 512])
        narrow = junk[:, 0:S]
        sel_l = sb("sel_l", [104, 8, S])
        sel_a = sb("sel_a", [104, S])
        sel_r = sb("sel_r", [104, S])
        cum = sb("cum", [8, S])
        gate8 = sb("gate8", [P, 8, 16])

        def softmax_buffers(at, tag):
            return (sb("L" + tag, [P, 2, S], at=at), sb("P" + tag, [P, 3, S], at=at), sb("PT" + tag, [P, 2, NT, P], at=at))

        conv_h = sb("conv_h", [P, 24, 4])
        hsum = sb("hsum", [P, 80])
        hrms = sb("hrms", [P, 80])
        gq4 = sb("gq4", [P, P])
        r1 = ExitStack()
        bufs1 = softmax_buffers(r1, "1")
        mqT = sb("mqT", [P, KC, S], at=r1)
        fqT, fkT = mqT[:, 0:4, :], mqT[:, 4:8, :]
        fv = sb("fv", [P, NT, 512], at=r1)
        cqT = sb("cqT", [P, 4, S], at=r1)
        ckT = sb("ckT", [P, 4, S], at=r1)
        cv = sb("cv", [P, NT, 512], at=r1)
        relb = sb("relb", [P, FH, S], at=r1)
        y = sb("y", [P, NT, D], at=r1)
        mem = y
        mkT = sb("mkT", [P, KC, S], at=r1)
        mv = sb("mv", [P, NT, D], at=r1)
        m_hi = sb("m_hi", [P, KC, S], F32R, at=r1)
        m_lo = sb("m_lo", [P, KC, S], F32R, at=r1)
        r1.close()
        r2 = ExitStack()
        hid_hi = sb("hid_hi", [P, FF // P, S], F32R, at=r2)
        hid_lo = sb("hid_lo", [P, FF // P, S], F32R, at=r2)
        hid_r = sb("hid_r", [P, 2, 512], at=r2)
        hid_v = sb("hid_v", [P, 2, 512], at=r2)
        r2.close()
        a0 = ExitStack()
        qkvT = sb("qkvT", [P, 24, S], at=a0)
        b0 = ExitStack()
        bufs2 = softmax_buffers(b0, "2")
        aqT = sb("aqT", [P, AH, S], at=b0)
        akT = sb("akT", [P, AKV, S], at=b0)
        av = sb("av", [P, NT, AKV * AD], at=b0)
        selb = sb("selb", [P, NT, S], at=b0)
        score = sb("score", [P, NT, S], at=b0)
        work = junk[:].rearrange("p (t s) -> p t s", t=NT)
        top8 = sb("top8", [P, NT, 8], at=b0)
        relu_i = sb("relu_i", [P, 2, S], at=b0)
        aqk = sb("aqk", [P, NT, AH + AKV, AD], at=b0)
        iqk = sb("iqk", [P, NT, IH + 2, ID], at=b0)
        iw = sb("iw", [P, NT, IH], at=b0)
        iqkT = sb("iqkT", [P, IH // 2 + 1, S], at=b0)
        rope_t = sb("rope_t", [P, 4, (AH + AKV) * AR], at=b0)
        cin = sb("cin", [P, 2, 2, 3 + S], at=b0)
        conv_t = sb("conv_t", [P, S], at=b0)
        tanh_c = sb("tanh_c", [P, 2, 512], at=b0)
        b0.close()
        b1 = ExitStack()
        khat = sb("khat", [P, NT, GH, GD], at=b1)
        kb = sb("kb", [P, NT, GH, GD], at=b1)
        qh = sb("qh", [P, NT, GH, GD], at=b1)
        vb = sb("vb", [P, NT, GH, GD], at=b1)
        kbg = sb("kbg", [P, GH, GD], at=b1)
        kdec = sb("kdec", [P, GH, GD], at=b1)
        zg = sb("zg", [P, NT, D], at=b1)
        tanh_g = sb("tanh_g", [P, 2, 512], at=b1)
        sqb = sb("sqb", [P, 2, 512], at=b1)
        b1.close()
        b2 = ExitStack()
        APT = sb("APT", [P, NT, GH, 2, P], at=b2)
        DT = sb("DT", [P, NT, GH, P], at=b2)
        b2.close()
        b3 = ExitStack()
        sb("under_APT", [P, NT * GH * 2 * P], at=b3)
        vnew = sb("vnew", [P, GH, GD], at=b3)
        S1 = sb("S1", [P, GH, GD], at=b3)
        b3.close()
        a0.close()
        a1 = ExitStack()
        khT = sb("khT", [P, NT, GH, P], at=a1)
        kbqT = sb("kbqT", [P, 2, NT, GH, P], at=a1)
        a1.close()
        a2 = ExitStack()
        Tm = sb("Tm", [P, 2, 4, P], at=a2)
        Um = sb("Um", [P, 2, 4, P], at=a2)
        Bt = sb("Bt", [P, 2, 4, P], at=a2)
        Yb = sb("Yb", [P, 2, 4, P], at=a2)
        a2.close()

        acc = [ctx.enter_context(nc.psum_tensor(f"acc{i}", [P, 512], F32)) for i in range(4)]
        aux = [ctx.enter_context(nc.psum_tensor(f"aux{i}", [P, 512], F32)) for i in range(4)]

        w_loaded = [sem(f"w_loaded{i}") for i in range(RAW_SLOTS)]
        w_hi_done, w_lo_done, unit_done = sem("w_hi_done"), sem("w_lo_done"), sem("unit_done")
        tile_done = sem("tile_done")
        acc_free = [sem(f"acc_free{i}") for i in range(4)]
        x_in, id_in, gain_in, mem_in, cst_in, small_in, rel_in, gpost_in = [sem(n) for n in (
            "x_in", "id_in", "gain_in", "mem_in", "cst_in", "small_in", "rel_in", "gpost_in")]
        ss_done, rstd_done, diag_done, nt_tr, nt_hi, nt_lo = [sem(n) for n in (
            "ss_done", "rstd_done", "diag_done", "nt_tr", "nt_hi", "nt_lo")]
        ws_hi_done, ws_lo_done, ws_mm, narrow_copied, narrow_done = [sem(n) for n in (
            "ws_hi_done", "ws_lo_done", "ws_mm", "narrow_copied", "narrow_done")]
        set_done, rel_done = sem("set_done"), sem("rel_done")
        gate_v, gate_a, gate_tr, gate_ct, sel_done = [sem(n) for n in ("gate_v", "gate_a", "gate_tr", "gate_ct", "sel_done")]
        sc_done, l_done, p_done, pt_done, ptc_done, pv_done, rinv_done, y_done = [sem(n) for n in (
            "sc_done", "l_done", "p_done", "pt_done", "ptc_done", "pv_done", "rinv_done", "y_done")]
        x_done, relu_done, hid_hi_done, hid_lo_done = [sem(n) for n in (
            "x_done", "relu_done", "hid_hi_done", "hid_lo_done")]
        stored = sem("stored")
        g2_in, g2_a, g2_g, g2_tr, g2_ct, g2_sel, g2_tm, g2_eg = [sem("g2_" + n) for n in ("in", "a", "g", "tr", "ct", "sel", "tm", "eg")]
        set2_done, ik_done, rope_i, iqT_mm, iqT_copied = [sem(n) for n in (
            "set2_done", "ik_done", "rope_i", "iqT_mm", "iqT_copied")]
        idx_mm, idx_relu, idx_acc, aqk_ss, aqk_rms, aqk_scaled, aqk_done, aT_mm, aT_copied = [sem(n) for n in (
            "idx_mm", "idx_relu", "idx_acc", "aqk_ss", "aqk_rms", "aqk_scaled", "aqk_done", "aT_mm", "aT_copied")]
        conv_done, conv2_done, tanh_done, qkv_done = [sem(n) for n in ("conv_done", "conv2_done", "tanh_done", "qkv_done")]
        gate_tanh, tok_mm, tok_copied, tok_sq, tok_ss, tok_rms, tok_done = [sem(n) for n in (
            "gate_tanh", "tok_mm", "tok_copied", "tok_sq", "tok_ss", "tok_rms", "tok_done")]
        back_mm, back_copied, dt_mm, dt_add, dt_done, kdec_done, ap_mm, ap_done = [sem(n) for n in (
            "back_mm", "back_copied", "dt_mm", "dt_add", "dt_done", "kdec_done", "ap_mm", "ap_done")]
        bt_done, u_done, t_done, y_mm, y_copied, ty_mm, yu_mm = [sem("inv_" + n) for n in (
            "bt", "u", "t", "y_mm", "y_copied", "ty_mm", "yu_mm")]
        r_mm, r_copied, qs_mm, qs_done, o_mm, o_done, o_ss, o_rms, merged_done = [sem("out_" + n) for n in (
            "r_mm", "r_copied", "qs_mm", "qs_done", "o_mm", "o_done", "o_ss", "o_rms", "merged")]

        def ident():
            return cst[:, C_ID:C_ID + P]

        N = Count()
        SS_AFTER = {"p_out": 16, "p_mo": 24, "p_ff2": 32}
        GAIN = {"mem": 0, "mix": 1, "y": 2, "mpre": 3, "memo": None, "ff": 4, "mix2": 5, "merged": None, "mlp2": 6}
        def unit_hi(act, u, q=None):
            if not q:
                act.wait_ge(w_loaded[u % RAW_SLOTS], 16 * (u // RAW_SLOTS + 1))
                if u >= SPLIT_SLOTS:
                    act.wait_ge(unit_done, u - SPLIT_SLOTS + 1)
            cs = slice(0, 2048) if q is None else slice(q * 512, (q + 1) * 512)
            act.activation(w_hi[u % SPLIT_SLOTS][:, cs], w_raw[u % RAW_SLOTS][:, cs], ACT.Copy).then_inc(
                w_hi_done, 4 if q is None else 1)

        def unit_lo(dve, u, q=None):
            dve.wait_ge(w_hi_done, 4 * u + (4 if q is None else q + 1))
            cs = slice(0, 2048) if q is None else slice(q * 512, (q + 1) * 512)
            dve.tensor_tensor(w_lo[u % SPLIT_SLOTS][:, cs], w_raw[u % RAW_SLOTS][:, cs], w_hi[u % SPLIT_SLOTS][:, cs].bitcast(F32),
                              ALU.subtract).then_inc(w_lo_done, 4 if q is None else 1)

        def narrow_mm(pe, c0, n):
            o, cs = aux[0][0:n, 0:S], slice(c0, c0 + n)
            for k in range(KC):
                pe.matmul(o, ws_hi[:, k, cs], h_hi[:, k, :], start=k == 0, stop=False)
                pe.matmul(o, ws_hi[:, k, cs], h_lo[:, k, :], start=False, stop=False)
                i = pe.matmul(o, ws_lo[:, k, cs], h_hi[:, k, :], start=False, stop=k == KC - 1)
            i.then_inc(ws_mm, 1)

        def narrow_act(act, n):
            N.wait(act, ws_mm)
            act.activation(narrow[0:n, :], aux[0][0:n, 0:S], ACT.Copy).then_inc(narrow_copied, 1)

        def narrow_tr(pe, n):
            N.wait(pe, narrow_copied)
            for t in range(NT):
                i = pe.transpose(aux[1][:, t * n:(t + 1) * n], narrow[0:n, t * P:(t + 1) * P], cst[0:n, C_ID:C_ID + n])
            i.then_inc(narrow_done, 1)

        def unit_mm(pe, u, hi, lo, fresh=None, parts=range(4)):
            def chunk_ready(k):
                if fresh is not None:
                    pe.wait_ge(nt_lo, KC * fresh + k + 1)

            q = units[u]
            def split_ready(part):
                if q["form"] == "A" or part < 2:
                    pe.wait_ge(w_lo_done, 4 * u + (part + 1 if q["form"] == "A" else 2 * part + 2))

            if q["before"] is not None and parts[0] == 0:
                for b, n in zip(q["banks"], q["before"]):
                    if n:
                        pe.wait_ge(acc_free[b], n)
            wh, wl = w_hi[u % SPLIT_SLOTS], w_lo[u % SPLIT_SLOTS]
            if q["tiles"]:
                for t in range(NT):
                    o, ts = acc[q["banks"][t]][:], slice(t * P, (t + 1) * P)
                    for kk in range(4):
                        k, cs = q["k0"] + kk, slice(kk * 512, (kk + 1) * 512)
                        if t == 0:
                            split_ready(kk)
                            chunk_ready(k)
                        pe.matmul(o, hi[:, k, ts], wh[:, cs], start=False, stop=False)
                        pe.matmul(o, hi[:, k, ts], wl[:, cs], start=False, stop=False)
                        i = pe.matmul(o, lo[:, k, ts], wh[:, cs], start=False, stop=kk == 3)
                    if t == 0:
                        i.then_inc(tile_done, 1)
            elif q["form"] == "A":
                for kk in parts:
                    split_ready(kk)
                    k = q["k0"] + kk
                    cs = slice(kk * 512, (kk + 1) * 512)
                    chunk_ready(k)
                    for t in range(NT):
                        ts = slice(t * P, (t + 1) * P)
                        o = acc[q["banks"][t]][:]
                        pe.matmul(o, hi[:, k, ts], wh[:, cs], start=q["first"] and kk == 0, stop=False)
                        pe.matmul(o, hi[:, k, ts], wl[:, cs], start=False, stop=False)
                        i = pe.matmul(o, lo[:, k, ts], wh[:, cs], start=False, stop=q["last"] and kk == 3)
            else:
                for part in parts:
                    split_ready(part)
                    m = part // 2
                    o = acc[q["banks"][0]][:, m * S:(m + 1) * S]
                    for k in range(4 * (part % 2), 4 * (part % 2) + 4):
                        cs = slice(k * 256 + m * P, k * 256 + (m + 1) * P)
                        if m == 0:
                            chunk_ready(k)
                        pe.matmul(o, wh[:, cs], hi[:, k, :], start=k == 0, stop=False)
                        pe.matmul(o, wh[:, cs], lo[:, k, :], start=False, stop=False)
                        i = pe.matmul(o, wl[:, cs], hi[:, k, :], start=False, stop=k == KC - 1)
            if parts[-1] == 3:
                i.then_inc(unit_done, 1)

        def released(u):
            q, v = units[u], u
            while units[v]["before"] is None:
                v -= 1
            return [(b, n + 1) for b, n in zip(q["banks"], units[v]["before"])]

        def wait_copied(pe, tag):
            for u in of[tag]:
                for b, n in released(u):
                    pe.wait_ge(acc_free[b], n)

        def nt_act_stats(act, n, src, ready=None):
            for t in range(NT):
                for g in range(2):
                    if ready is not None:
                        ready(g, t)
                    square(act, n, g, t, src[:, t, g * 512:(g + 1) * 512])

        def square(act, n, g, t, piece):
            c = 4 * NCOL[n] + 2 * g + t
            act.activation(junk[:], piece, ACT.Square, accum_out=stat[:, c:c + 1]).then_inc(ss_done, 1)
            N.wait(act, ss_done)

        NCOL = {"mem": 0, "mix": 1, "y": 2, "mpre": 3, "ff": 4, "mix2": 5, "mlp2": 6, "p_out": 7, "p_mo": 8, "p_ff2": 9}

        def rstd_pool(pool, n, behind=False):
            pool.wait_ge(set_done, 1)
            for t in range(NT):
                c = 4 * NCOL[n] + t
                N.wait(pool, ss_done, (3, 1)[t] if behind else 2)
                pool.tensor_tensor(stat[:, c:c + 1], stat[:, c:c + 1], stat[:, c + 2:c + 3], ALU.add)
                pool.drain()
                pool.tensor_scalar(stat[:, c:c + 1], stat[:, c:c + 1], 1.0 / D, EPS, ALU.mult, ALU.add)
                pool.drain()
                pool.tensor_tensor(rstd[:, c:c + 1], stat[:, c:c + 1], half[:, 0:1], ALU.pow).then_inc(rstd_done, 1)

        def rstd_y_pool(pool, g):
            c = 4 * NCOL["y"] + 2 * g
            N.wait(pool, ss_done, 2)
            pool.tensor_scalar(stat[:, c:c + 2], stat[:, c:c + 2], 1.0 / 512, EPS, ALU.mult, ALU.add)
            pool.drain()
            pool.tensor_tensor(rstd[:, c:c + 2], stat[:, c:c + 2], half[:, 0:2], ALU.pow).then_inc(rstd_done, 2)

        diag = xn[:, 0, 0:512].rearrange("p (j s) -> p j s", j=4)

        def nt_dve_diag(dve, n, g=0):
            for t in range(NT):
                N.wait(dve, rstd_done)
                c = 4 * NCOL[n] + 2 * g + t
                dve.tensor_scalar(diag[:, 2 * g + t, :], ident(), rstd[:, c:c + 1], None, ALU.mult).then_inc(diag_done, 1)

        def nt_pe(pe, n, src, banks=range(4)):
            for t in range(NT):
                if GAIN[n] is not None:
                    N.wait(pe, diag_done)
                for j in banks:
                    for kk in range(2):
                        k = 2 * j + kk
                        o, piece = aux[j][:, kk * S + t * P:kk * S + (t + 1) * P], src[:, t, k * P:(k + 1) * P]
                        if GAIN[n] is None:
                            i = pe.transpose(o, piece, ident())
                        else:
                            g = k // 4 if n == "y" else 0
                            i = pe.matmul(o, piece, diag[:, 2 * g + t, :], start=True, stop=True)
                    if t == NT - 1:
                        i.then_inc(nt_tr, 1)

        def nt_act(act, n, hi):
            for j in range(4):
                N.wait(act, nt_tr)
                for kk in range(2):
                    k = 2 * j + kk
                    g = 1.0 if GAIN[n] is None else gcol[:, GAIN[n], k:k + 1]
                    act.activation(hi[:, k, :], aux[j][:, kk * S:(kk + 1) * S], ACT.Copy, scale=g).then_inc(nt_hi, 1)

        def nt_dve(dve, n, hi, lo):
            for j in range(4):
                for kk in range(2):
                    k = 2 * j + kk
                    if kk == 0:
                        N.wait(dve, nt_hi, 2)
                    g = 1.0 if GAIN[n] is None else gcol[:, GAIN[n], k:k + 1]
                    dve.scalar_tensor_tensor(lo[:, k, :], aux[j][:, kk * S:(kk + 1) * S], g, hi[:, k, :].bitcast(F32),
                                             ALU.mult, ALU.subtract).then_inc(nt_lo, 1)

        def evac_b(act, u, dst, scale=1.0):
            act.wait_ge(unit_done, u + 1)
            act.activation(dst, acc[units[u]["banks"][0]][:], ACT.Copy, scale=scale).then_inc(acc_free[units[u]["banks"][0]], 1)

        def evac_a(act, u, dsts, scale=1.0):
            act.wait_ge(unit_done, u + 1)
            for t in range(NT):
                b = units[u]["banks"][t]
                act.activation(dsts[t], acc[b][:], ACT.Copy, scale=scale).then_inc(acc_free[b], 1)

        def bufs(i):
            return bufs1 if i < I_DSA else bufs2

        def at_pe_scores(pe, i, it):
            if i >= 2:
                pe.wait_ge(l_done, i - 1)
            nk = it["nk"]
            o = aux[i % 2][:, 0:nk]
            for j, (a, b) in enumerate(it["qk"]):
                m = pe.matmul(o, a, b, start=j == 0, stop=j == len(it["qk"]) - 1)
            m.then_inc(sc_done, 1)

        def at_dve_mask(dve, i, it):
            N.wait(dve, sc_done)
            if i >= 2:
                dve.wait_ge(p_done, i - 1)
            nk = it["nk"]
            dve.tensor_tensor_reduce(out=bufs(i)[0][:, i % 2, 0:nk], in0=aux[i % 2][:, 0:nk], in1=it["bias"], scale=-it["scale"],
                                     scalar=3e38, op0=ALU.add, op1=ALU.min, accum_out=nmax[:, i:i + 1]).then_inc(l_done, 1)

        def at_act_exp(act, i, it):
            N.wait(act, l_done)
            if i >= 3:
                act.wait_ge(pt_done, i - 2)
            nk = it["nk"]
            act.activation(bufs(i)[1][:, i % 3, 0:nk], bufs(i)[0][:, i % 2, 0:nk], ACT.Exp, bias=nmax[:, i:i + 1], scale=-1.0,
                           accum_out=rsum[:, i:i + 1]).then_inc(p_done, 1)

        def at_pe_tr(pe, i, it):
            N.wait(pe, p_done)
            if i >= 2:
                pe.wait_ge(y_done, i - 1)
            for b in range(it["nk"] // P):
                m = pe.transpose(aux[2 + i % 2][:, b * P:(b + 1) * P], bufs(i)[1][:, i % 3, b * P:(b + 1) * P], ident())
            m.then_inc(pt_done, 1)

        def at_dve_copy(dve, i, it):
            N.wait(dve, pt_done)
            if i >= 2:
                dve.wait_ge(pv_done, i - 1)
            nb = it["nk"] // P
            dve.tensor_copy(bufs(i)[2][:, i % 2, 0:nb, :], aux[2 + i % 2][:, 0:nb * P]).then_inc(ptc_done, 1)
            dve.wait_ge(p_done, i + 1)
            dve.reciprocal(rinv[:, i:i + 1], rsum[:, i:i + 1]).then_inc(rinv_done, 1)

        def at_pe_pv(pe, i, it):
            N.wait(pe, ptc_done)
            nb = it["nk"] // P
            dv = it["dv"]
            for b in range(nb):
                m = pe.matmul(aux[2 + i % 2][:, S:S + dv], bufs(i)[2][:, i % 2, b, :], it["v"][b], start=b == 0, stop=b == nb - 1)
            m.then_inc(pv_done, 1)

        def at_act_out(act, i, it):
            N.wait(act, pv_done)
            act.wait_ge(rinv_done, i + 1)
            act.activation(it["out"], aux[2 + i % 2][:, S:S + it["dv"]], ACT.Copy, scale=rinv[:, i:i + 1]).then_inc(y_done, 1)

        def fox_items():
            items = []
            for h in range(FH):
                r, m = 64 * (h % 2), h // 2
                for t in range(NT):
                    ts, nk = slice(t * P, (t + 1) * P), (t + 1) * P
                    items.append(dict(nk=nk, scale=1.0, dv=FD,
                                      qk=[(fqT[r:r + 64, m, ts], fkT[r:r + 64, m, 0:nk]), (sel_l[r:r + 40, h, ts], sel_r[r:r + 40, 0:nk])],
                                      bias=cst[:, C_CAUSAL + 2 * P - nk:C_CAUSAL + 2 * P],
                                      v=[fv[:, b, h * FD:(h + 1) * FD] for b in range(t + 1)],
                                      out=y[:, t, h * FD:(h + 1) * FD]))
            for h in range(FH):
                r, m = 64 * (h % 2), h // 2
                for t in range(NT):
                    ts, nk = slice(t * P, (t + 1) * P), (t + 1) * P
                    items.append(dict(nk=nk, scale=1.0, dv=FD,
                                      qk=[(cqT[r:r + 64, m, ts], ckT[r:r + 64, m, 0:nk])],
                                      bias=relb[:, h, S - nk:S],
                                      v=[cv[:, b, h * FD:(h + 1) * FD] for b in range(t + 1)],
                                      out=y[:, t, DFOX + h * FD:DFOX + (h + 1) * FD]))
            return items

        def mem_items():
            items = []
            for h in range(MH):
                for t in range(NT):
                    ts = slice(t * P, (t + 1) * P)
                    items.append(dict(nk=S, scale=1.0, dv=MD,
                                      qk=[(mqT[:, 2 * h + c, ts], mkT[:, 2 * h + c, :]) for c in range(2)],
                                      bias=cst[:, C_ZERO:C_ZERO + S],
                                      v=[mv[:, b, h * MD:(h + 1) * MD] for b in range(NT)],
                                      out=y[:, t, h * MD:(h + 1) * MD]))
            return items

        FOX, MEM = fox_items(), mem_items()
        I_MEM = len(FOX)
        I_DSA = I_MEM + len(MEM)

        def dsa_items():
            items = []
            for h in range(AH):
                kv = h // (AH // AKV)
                for t in range(NT):
                    ts, nk = slice(t * P, (t + 1) * P), (t + 1) * P
                    items.append(dict(nk=nk, scale=float(AD) ** -0.5, dv=AD, qk=[(aqT[:, h, ts], akT[:, kv, 0:nk])],
                                      bias=selb[:, t, 0:nk],
                                      v=[av[:, b, kv * AD:(kv + 1) * AD] for b in range(t + 1)],
                                      out=xn[:, t, h * AD:(h + 1) * AD]))
            return items

        DSA = dsa_items()

        TILE_FIRST = ["out", "mo", "ff2", "out2", "down"]

        def half_unit(tag, g):
            return of[tag][(g + 1) * len(of[tag]) // 2 - 1]

        def wait_piece(eng, tag, g, t):
            if g == 1 and t == 0:
                eng.wait_ge(tile_done, TILE_FIRST.index(tag) + 1)
            else:
                eng.wait_ge(unit_done, half_unit(tag, g) + 1)

        def post_stats(act, n, tag, g):
            for t in range(NT):
                wait_piece(act, tag, g, t)
                square(act, n, g, t, acc[units[half_unit(tag, g)]["banks"][t]][:])

        def post_gain(dve, n, tag, n_load, g, t):
            dve.wait_ge(gpost_in, 16 * n_load)
            wait_piece(dve, tag, g, t)
            dve.wait_ge(ss_done, SS_AFTER[n] - 3 + 2 * g + t)
            b, cs = units[half_unit(tag, g)]["banks"][t], slice(g * 512, (g + 1) * 512)
            dve.tensor_tensor(xn[:, t, cs], acc[b][:], gpost[:, cs], ALU.mult).then_inc(acc_free[b], 1)

        def post_add(dve, n, tag, n_load):
            for t in range(NT):
                post_gain(dve, n, tag, n_load, 1, t)
                N.wait(dve, rstd_done)
                dve.drain()
                for g in range(2):
                    c, cs = 4 * NCOL[n] + t, slice(g * 512, (g + 1) * 512)
                    dve.scalar_tensor_tensor(x[:, t, cs], xn[:, t, cs], rstd[:, c:c + 1], x[:, t, cs],
                                             ALU.mult, ALU.add).then_inc(x_done, 1)

        def wait_read(eng, u):
            for b, n in released(u):
                eng.wait_ge(acc_free[b], n)

        HB = {"ff1": 0, "up": 16}

        def hid_act_relu(act, tag, j):
            u = of[tag][j]
            act.wait_ge(unit_done, u + 1)
            if j >= 2:
                wait_read(act, u - 2)
            act.activation(hid_r[:, j % 2, :], acc[units[u]["banks"][0]][:], ACT.Relu).then_inc(relu_done, 1)

        def hid_dve_sq(dve, tag, j):
            u = of[tag][j]
            N.wait(dve, relu_done)
            if j >= 2:
                dve.wait_ge(hid_lo_done, HB[tag] + j - 1)
            b = units[u]["banks"][0]
            dve.scalar_tensor_tensor(hid_v[:, j % 2, :], acc[b][:], 0.0, hid_r[:, j % 2, :], ALU.max, ALU.mult).then_inc(acc_free[b], 1)

        def hid_act_hi(act, tag, j):
            wait_read(act, of[tag][j])
            act.activation(hid_hi[:, 2 * j:2 * j + 2, :], hid_v[:, j % 2, :], ACT.Copy).then_inc(hid_hi_done, 1)

        def hid_dve_lo(dve, tag, j):
            N.wait(dve, hid_hi_done)
            dve.tensor_tensor(hid_lo[:, 2 * j:2 * j + 2, :], hid_v[:, j % 2, :], hid_hi[:, 2 * j:2 * j + 2, :].bitcast(F32),
                              ALU.subtract).then_inc(hid_lo_done, 1)

        def advance_hi(act, u, q=None):
            if u + AHEAD < NU:
                unit_hi(act, u + AHEAD, q)

        def advance_lo(dve, u, q=None):
            if u + AHEAD < NU:
                unit_lo(dve, u + AHEAD, q)

        EVAC_B = {"fq": (fqT, 0.125), "fk": (fkT, 1.0), "cq": (cqT, 0.125), "ck": (ckT, 1.0), "mk": (mkT, 1.0), "mq": (mqT, 0.0625)}
        EVAC_A = {"fv": fv, "cv": cv}

        def act_unit(act, tag, j):
            advance_hi(act, of[tag][j])
            evacuate(act, tag, j)

        def act_group(act, tag):
            for j in range(len(of[tag])):
                advance_hi(act, of[tag][j])
                if j:
                    evacuate(act, tag, j - 1)
            evacuate(act, tag, len(of[tag]) - 1)

        def evacuate(act, tag, j):
            u = of[tag][j]
            if tag in EVAC_B:
                dst, scale = EVAC_B[tag]
                evac_b(act, u, dst[:, 2 * j:2 * j + 2, :], scale)
            elif tag in EVAC_A and units[u]["last"]:
                evac_a(act, u, [EVAC_A[tag][:, t, :] for t in range(NT)])
            elif tag == "mv" and units[u]["last"]:
                g = j // 2
                evac_a(act, u, [mv[:, t, g * 512:(g + 1) * 512] for t in range(NT)])
            elif tag == "iq" and units[u]["last"]:
                evac_a(act, u, [iqk[:, t, 0:IH, :].rearrange("p h d -> p (h d)") for t in range(NT)])
            elif tag == "aq" and units[u]["last"]:
                g = j // 2
                evac_a(act, u, [aqk[:, t, 4 * g:4 * g + 4, :].rearrange("p h d -> p (h d)") for t in range(NT)])
            elif tag == "akv" and units[u]["last"]:
                act.wait_ge(unit_done, u + 1)
                for t in range(NT):
                    b = units[u]["banks"][t]
                    act.activation(aqk[:, t, AH:, :].rearrange("p h d -> p (h d)"), acc[b][:, 0:AKV * AD], ACT.Copy)
                    act.activation(av[:, t, :], acc[b][:, AKV * AD:], ACT.Copy).then_inc(acc_free[b], 1)

        def attention_pe(pe, items, i0, between):
            for i in range(len(items) + 3):
                if i < len(items):
                    at_pe_scores(pe, i0 + i, items[i])
                if 2 <= i <= len(items) + 1:
                    at_pe_tr(pe, i0 + i - 2, items[i - 2])
                if i >= 3:
                    at_pe_pv(pe, i0 + i - 3, items[i - 3])
                between(i)

        def attention_act(act, items, i0, between):
            for i in range(len(items) + 3):
                if i < len(items):
                    at_act_exp(act, i0 + i, items[i])
                if i >= 3:
                    at_act_out(act, i0 + i - 3, items[i - 3])
                between(i)

        def attention_dve(dve, items, i0, between):
            for i in range(len(items) + 2):
                if i < len(items):
                    at_dve_mask(dve, i0 + i, items[i])
                if i >= 2:
                    at_dve_copy(dve, i0 + i - 2, items[i - 2])
                between(i)

        MEMU = [("mk", j) for j in range(4)] + [("mv", j) for j in range(4)]


        def both(ap, n=NT):
            return ap.unsqueeze(1).broadcast_to([ap.shape[0], n] + list(ap.shape[1:]))

        g16 = [gate8[:, j, :].rearrange("p (t h) -> p t h", t=NT) for j in range(8)]
        BETA, EG, A_EXP = g16[7], g16[5], gate8[:, 3, 0:8]

        def gates2_act(act):
            N.wait(act, g2_in)
            act.activation(gate8[:, 2, :], gate8[:, 1, :], ACT.Exp).then_inc(g2_a, 1)
            act.activation(A_EXP, bc8[:, 1, :], ACT.Exp).then_inc(g2_a, 1)
            act.activation(g16[6], aux[1][:, 0:2 * 88].rearrange("p (t c) -> p t c", t=NT)[:, :, 8:16], ACT.Tanh, scale=0.5).then_inc(g2_a, 1)
            act.wait_ge(g2_a, 1)
            act.activation(gate8[:, 4, :], gate8[:, 2, :], ACT.Ln, bias=1.0).then_inc(g2_a, 1)

        def gates2_dve_in(dve):
            N.wait(dve, narrow_done)
            dve.tensor_tensor(g16[0], aux[1][:, 0:2 * 88].rearrange("p (t c) -> p t c", t=NT)[:, :, 0:8], both(bc8[:, 2, :]), ALU.add)
            dve.drain()
            dve.scalar_tensor_tensor(g16[1], g16[0], -1.0, g16[0], ALU.mult, ALU.min).then_inc(g2_in, 1)

        def gates2_dve(dve):
            dve.wait_ge(g2_a, 4)
            dve.tensor_scalar(BETA, g16[6], 0.5, 0.5, ALU.mult, ALU.add)
            dve.scalar_tensor_tensor(g16[1], g16[0], 0.0, g16[4], ALU.max, ALU.add)
            dve.drain()
            dve.scalar_tensor_tensor(g16[2], g16[1], -1.0, both(A_EXP), ALU.mult, ALU.mult).then_inc(g2_g, 1)

        def gates2_pe(pe):
            pe.wait_ge(g2_g, 1)
            for t in range(NT):
                i = pe.transpose(aux[3][0:8, t * P:(t + 1) * P], gate8[:, 2, t * 8:(t + 1) * 8], ident())
            i.then_inc(g2_tr, 1)

        def gates2_dve_sum(dve):
            dve.wait_ge(g2_tr, 1)
            for t in range(NT):
                ts = slice(t * P, (t + 1) * P)
                dve.tensor_tensor_scan(cum[:, ts], sel_a[0:8, ts], aux[3][0:8, ts], 0.0, ALU.mult, ALU.add)
            dve.drain()
            dve.tensor_copy(sel_r[0:8, :], cum[:]).then_inc(g2_ct, 1)
            dve.tensor_scalar(sel_a[32:40, :], cum[:], -1.0, None, ALU.mult).then_inc(g2_ct, 1)

        def gates2_pool(pool):
            pool.wait_ge(g2_ct, 2)
            pool.tensor_tensor(sel_l[0:40], both(sel_a[0:40, :], 8),
                               cst[0:40, C_SEL:C_SEL + 8].unsqueeze(2).broadcast_to([40, 8, S]), ALU.mult).then_inc(g2_sel, 1)

        def gates2_pe_tm(pe):
            pe.wait_ge(g2_ct, 2)
            for t in range(NT):
                i = pe.transpose(aux[3][:, t * 8:(t + 1) * 8], cum[:, t * P:(t + 1) * P], cst[0:8, C_ID:C_ID + 8])
            i.then_inc(g2_tm, 1)

        def gates2_act_eg(act):
            act.wait_ge(g2_tm, 1)
            act.activation(gate8[:, 5, :], aux[3][:, 0:16], ACT.Exp).then_inc(g2_eg, 1)

        def rope(dve, v, heads, n, c_cos, c_sin, t):
            cos, sin = [cst[:, c + t * n:c + (t + 1) * n].unsqueeze(1).broadcast_to([P, heads, n]) for c in (c_cos, c_sin)]
            tmp = [rope_t[:, j, 0:heads * n].rearrange("p (h d) -> p h d", h=heads) for j in range(4)]
            x1, x2 = v[:, :, 0:n], v[:, :, n:2 * n]
            dve.tensor_tensor(tmp[0], x1, cos, ALU.mult)
            dve.tensor_tensor(tmp[1], x2, sin, ALU.mult)
            dve.tensor_tensor(tmp[2], x2, cos, ALU.mult)
            dve.tensor_tensor(tmp[3], x1, sin, ALU.mult)
            dve.drain()
            dve.tensor_tensor(x1, tmp[0], tmp[1], ALU.subtract)
            return dve.tensor_tensor(x2, tmp[2], tmp[3], ALU.add)

        def ik_act(act):
            act.wait_ge(narrow_done, 2)
            act.wait_ge(g2_in, 1)
            for t in range(NT):
                c = t * 88 + 16
                act.activation(iqk[:, t, IH:IH + 2, :], both(aux[1][:, c:c + ID]), ACT.Copy).then_inc(ik_done, 1)
                act.activation(iw[:, t, :], aux[1][:, c + ID:c + ID + IH], ACT.Copy, scale=float(IH * ID) ** -0.5).then_inc(ik_done, 1)

        def idx_rope_dve(dve):
            wait_copied(dve, "iq")
            dve.wait_ge(ik_done, 2 * NT)
            for t in range(NT):
                if t:
                    dve.wait_ge(rope_i, t)
                rope(dve, iqk[:, t], IH + 2, IR, C_ICOS, C_ISIN, t).then_inc(rope_i, 1)

        def idx_tr_pe(pe):
            pe.wait_ge(rope_i, NT)
            pe.wait_ge(g2_in, 1)
            pe.wait_ge(g2_a, 4)
            pe.wait_ge(ik_done, 2 * NT)
            for j in range(IH // 2 + 1):
                for t in range(NT):
                    i = pe.transpose(aux[j // 2][:, (j % 2) * S + t * P:(j % 2) * S + (t + 1) * P],
                                     iqk[:, t, 2 * j:2 * j + 2, :].rearrange("p h d -> p (h d)"), ident())
                if j % 2 or j == IH // 2:
                    i.then_inc(iqT_mm, 1)

        def idx_tr_act(act):
            for b in range(3):
                act.wait_ge(iqT_mm, b + 1)
                n = 2 if b < 2 else 1
                act.activation(iqkT[:, 2 * b:2 * b + n, :], aux[b][:, 0:n * S], ACT.Copy).then_inc(iqT_copied, 1)

        def idx_scores(eng, which, between):
            for j in range(NT * IH):
                t, h = j // IH, j % IH
                nk = (t + 1) * P
                r = 64 * (h % 2)
                if which == "pe":
                    pe = eng
                    pe.wait_ge(iqT_copied, 3)
                    if j >= 2:
                        pe.wait_ge(idx_relu, j - 1)
                    pe.matmul(aux[h % 2][:, 0:nk], iqkT[r:r + 64, h // 2, t * P:(t + 1) * P], iqkT[r:r + 64, IH // 2, 0:nk],
                              start=True, stop=True).then_inc(idx_mm, 1)
                elif which == "act":
                    act = eng
                    act.wait_ge(idx_mm, j + 1)
                    if j >= 2:
                        act.wait_ge(idx_acc, j - 1)
                    act.activation(relu_i[:, h % 2, 0:nk], aux[h % 2][:, 0:nk], ACT.Relu).then_inc(idx_relu, 1)
                else:
                    dve = eng
                    dve.wait_ge(idx_relu, j + 1)
                    if h == 0:
                        dve.tensor_scalar(score[:, t, 0:nk], relu_i[:, 0, 0:nk], iw[:, t, 0:1], None, ALU.mult).then_inc(idx_acc, 1)
                    else:
                        dve.wait_ge(idx_acc, j)
                        dve.scalar_tensor_tensor(score[:, t, 0:nk], relu_i[:, h % 2, 0:nk], iw[:, t, h:h + 1], score[:, t, 0:nk],
                                                 ALU.mult, ALU.add).then_inc(idx_acc, 1)
                between(j)

        def topk_dve(dve, tick):
            sc, wk, sl = [[v[:, t, 0:(t + 1) * P] for t in range(NT)] for v in (score, work, selb)]
            dve.wait_ge(idx_acc, IH * NT)
            for t in range(NT):
                nk = (t + 1) * P
                dve.tensor_tensor(sc[t], sc[t], cst[:, C_CAUSAL + 2 * P - nk:C_CAUSAL + 2 * P], ALU.add)
            for r in range(TOPK // 8):
                src = sc if r == 0 else wk
                dve.drain()
                for t in range(NT):
                    dve.max(top8[:, t], src[t])
                dve.drain()
                for t in range(NT):
                    dve.match_replace(wk[t], top8[:, t], src[t], NEG)
                if r % 2:
                    tick()
            dve.drain()
            for t in range(NT):
                dve.tensor_tensor(wk[t], wk[t], sc[t], ALU.is_equal)
            dve.drain()
            for t in range(NT):
                dve.tensor_scalar(sl[t], wk[t], NEG, None, ALU.mult)
            dve.drain()

        def aqk_dve(dve, tick):
            for t in range(NT):
                dve.wait_ge(aqk_scaled, 10 * (t + 1))
                dve.tensor_tensor(aqk[:, t, 0:AH], aqk[:, t, 0:AH], both(ghead[:, 0, :], AH), ALU.mult)
                dve.tensor_tensor(aqk[:, t, AH:], aqk[:, t, AH:], both(ghead[:, 1, :], AKV), ALU.mult)
                dve.drain()
                rope(dve, aqk[:, t], AH + AKV, AR, C_COS, C_SIN, t).then_inc(aqk_done, 1)
                dve.drain()
                tick()

        def aqk_act_squares(act, t):
            if t == 0:
                wait_copied(act, "akv")
                wait_copied(act, "aq")
                act.wait_ge(idx_acc, NT * IH)
            for h in range(AH + AKV):
                i = t * (AH + AKV) + h
                if i >= 4:
                    act.wait_ge(aqk_ss, i - 3)
                act.activation(relu_i[:, i // 2 % 2, (i % 2) * P:(i % 2 + 1) * P], aqk[:, t, h, :], ACT.Square,
                               accum_out=hsum[:, i:i + 1]).then_inc(aqk_ss, 1)

        def aqk_act_scale(act, t):
            act.wait_ge(aqk_rms, 1)
            for h in range(AH + AKV):
                c = 10 * t + h
                act.activation(aqk[:, t, h, :], aqk[:, t, h, :], ACT.Copy, scale=hrms[:, c:c + 1]).then_inc(aqk_scaled, 1)

        def aqk_pool(pool):
            pool.wait_ge(aqk_ss, NT * (AH + AKV))
            pool.tensor_scalar(hsum[:, 0:20], hsum[:, 0:20], 1.0 / AD, EPS, ALU.mult, ALU.add)
            pool.drain()
            pool.tensor_tensor(hrms[:, 0:20], hsum[:, 0:20], half[:, 0:20], ALU.pow).then_inc(aqk_rms, 1)

        def aqk_pe(pe, tick):
            for j in range(5):
                if j == 0:
                    pe.wait_ge(aqk_done, NT)
                    pe.wait_ge(idx_relu, NT * IH)
                    pe.wait_ge(g2_eg, 1)
                if j == 4:
                    pe.wait_ge(aT_copied, 1)
                for hh in range(2):
                    for t in range(NT):
                        i = pe.transpose(aux[j % 4][:, hh * S + t * P:hh * S + (t + 1) * P], aqk[:, t, 2 * j + hh, :], ident())
                i.then_inc(aT_mm, 1)

        def aqk_act(act):
            for j in range(5):
                act.wait_ge(aT_mm, j + 1)
                dst = aqT[:, 2 * j:2 * j + 2, :] if j < 4 else akT[:, 0:2, :]
                act.activation(dst, aux[j % 4][:], ACT.Copy).then_inc(aT_copied, 1)

        def qkv_act_in(act, j):
            u = of["qkv"][j]
            act.wait_ge(unit_done, u + 1)
            act.wait_ge(set2_done, 1)
            if j >= 2:
                act.wait_ge(conv_done, j - 1)
                act.wait_ge(conv2_done, j - 1)
            b = units[u]["banks"][0]
            act.activation(cin[:, j % 2, :, 3:3 + S], acc[b][:].rearrange("p (m s) -> p m s", m=2), ACT.Copy).then_inc(acc_free[b], 1)

        def conv_pool(pool, j):
            wait_read(pool, of["qkv"][j])
            pool.wait_ge(set2_done, 1)
            c = 2 * j + 1
            for tap in range(4):
                tw, src, dst = conv_h[:, c, tap:tap + 1], cin[:, j % 2, 1, tap:tap + S], qkvT[:, c, :]
                if tap:
                    pool.drain()
                pool.tensor_scalar(conv_t[:] if tap else dst, src, tw, None, ALU.mult)
                if tap:
                    pool.drain()
                    i = pool.tensor_tensor(dst, dst, conv_t[:], ALU.add)
            i.then_inc(conv_done, 1)

        def conv_dve(dve, j):
            wait_read(dve, of["qkv"][j])
            c = 2 * j
            for tap in range(4):
                tw, src, dst = conv_h[:, c, tap:tap + 1], cin[:, j % 2, 0, tap:tap + S], qkvT[:, c, :]
                if tap == 0:
                    i = dve.tensor_scalar(dst, src, tw, None, ALU.mult)
                else:
                    dve.drain()
                    i = dve.scalar_tensor_tensor(dst, src, tw, dst, ALU.mult, ALU.add)
            i.then_inc(conv2_done, 1)

        def qkv_act_tanh(act, j):
            act.wait_ge(conv_done, j + 1)
            act.wait_ge(conv2_done, j + 1)
            if j >= 2:
                act.wait_ge(qkv_done, j - 1)
            act.activation(tanh_c[:, j % 2, :], qkvT[:, 2 * j:2 * j + 2, :].rearrange("p m s -> p (m s)"), ACT.Tanh).then_inc(tanh_done, 1)

        def qkv_dve(dve, j):
            dve.wait_ge(tanh_done, j + 1)
            v = qkvT[:, 2 * j:2 * j + 2, :].rearrange("p m s -> p (m s)")
            dve.scalar_tensor_tensor(v, tanh_c[:, j % 2, :], 1.0, v, ALU.add, ALU.mult).then_inc(qkv_done, 1)

        def gate_act(act, tag, j):
            u = of[tag][j]
            act.wait_ge(unit_done, u + 1)
            base = {"z": 0, "ga": 4, "gb": 8}[tag] + (j // 2) * 2
            for t in range(NT):
                n = base + t
                if n >= 2:
                    wait_read(act, u - 2)
                act.activation(tanh_g[:, n % 2, :], acc[units[u]["banks"][t]][:], ACT.Tanh, scale=0.5).then_inc(gate_tanh, 1)

        def gate_dve(dve, tag, j):
            u = of[tag][j]
            g = j // 2
            cs = slice(g * 512, (g + 1) * 512)
            base = {"z": 0, "ga": 4, "gb": 8}[tag] + 2 * g
            for t in range(NT):
                n, b = base + t, units[u]["banks"][t]
                dve.wait_ge(gate_tanh, n + 1)
                th = tanh_g[:, n % 2, :]
                if tag == "z":
                    i = dve.scalar_tensor_tensor(zg[:, t, cs], th, 1.0, acc[b][:], ALU.add, ALU.mult)
                elif tag == "ga":
                    i = dve.scalar_tensor_tensor(zg[:, t, cs], th, 1.0, zg[:, t, cs], ALU.add, ALU.mult)
                else:
                    i = dve.scalar_tensor_tensor(xn[:, t, cs], th, 1.0, xn[:, t, cs], ALU.add, ALU.mult)
                i.then_inc(acc_free[b], 1)

        def gate_norm_dve(dve, t):
            v = zg[:, t, :].rearrange("p (h d) -> p h d", d=GD)
            dve.tensor_tensor(v, v, both(gq4[:], GH), ALU.mult)

        TOK = [(kind, n, g) for kind in (1, 0, 2) for n in range(NT) for g in range(2)]

        squares = kdec[:].rearrange("p (j h) d -> p j (h d)", j=2)

        def tok_pe(pe, b):
            kind, n, g = TOK[b]
            pe.wait_ge(qkv_done, {1: 8, 0: 8, 2: 12}[kind])
            if b >= 4:
                pe.wait_ge(tok_copied, b - 3)
            for hh in range(4):
                i = pe.transpose(aux[b % 4][:, hh * P:(hh + 1) * P], qkvT[:, kind * 8 + 4 * g + hh, n * P:(n + 1) * P], ident())
            i.then_inc(tok_mm, 1)

        def tok_act(act, b):
            kind, n, g = TOK[b]
            act.wait_ge(tok_mm, b + 1)
            if kind < 2:
                if b >= 2:
                    act.wait_ge(tok_ss, b - 1)
                act.activation(squares[:, b % 2, :], aux[b % 4][:], ACT.Square).then_inc(tok_sq, 1)
            dst = {1: khat, 0: qh, 2: vb}[kind][:, n, 4 * g:4 * g + 4, :]
            act.activation(dst, aux[b % 4][:].rearrange("p (h d) -> p h d", h=4), ACT.Copy).then_inc(tok_copied, 1)

        def tok_dve(dve, b):
            kind, n, g = TOK[b]
            if kind < 2:
                dve.wait_ge(tok_sq, b + 1)
                c = 20 + (0 if kind == 1 else 16) + 8 * n + 4 * g
                dve.tensor_reduce(hsum[:, c:c + 4], squares[:, b % 2, :].rearrange("p (h d) -> p h d", d=GD), AX_X, ALU.add).then_inc(tok_ss, 1)

        def tok_rms_pool(pool):
            pool.wait_ge(tok_ss, 8)
            pool.tensor_scalar(hsum[:, 20:52], hsum[:, 20:52], EPS, None, ALU.add)
            pool.drain()
            pool.tensor_tensor(hrms[:, 20:52], hsum[:, 20:52], half[:], ALU.pow)
            pool.drain()
            pool.tensor_scalar(hrms[:, 36:52], hrms[:, 36:52], float(GD) ** -0.5, None, ALU.mult).then_inc(tok_rms, 1)

        def per_head(ap):
            return ap.unsqueeze(2).broadcast_to([P, GH, GD])

        def tok_scale_dve(dve, tick):
            dve.wait_ge(tok_rms, 1)
            dve.wait_ge(tok_copied, 12)
            dve.wait_ge(g2_eg, 1)
            for n in range(NT):
                dve.tensor_tensor(khat[:, n], khat[:, n], per_head(hrms[:, 20 + 8 * n:28 + 8 * n]), ALU.mult).then_inc(tok_done, 1)
                dve.tensor_tensor(qh[:, n], qh[:, n], per_head(hrms[:, 36 + 8 * n:44 + 8 * n]), ALU.mult).then_inc(tok_done, 1)
                dve.wait_ge(tok_done, 5 * n + 1)
                dve.tensor_tensor(kb[:, n], khat[:, n], per_head(BETA[:, n, :]), ALU.mult).then_inc(tok_done, 1)
                tick()
                dve.tensor_tensor(vb[:, n], vb[:, n], per_head(BETA[:, n, :]), ALU.mult).then_inc(tok_done, 1)
                dve.wait_ge(tok_done, 5 * n + 3)
                if n:
                    dve.tensor_tensor(kbg[:], kb[:, n], per_head(EG[:, n, :]), ALU.mult).then_inc(tok_done, 1)
                else:
                    dve.engine_nop().then_inc(tok_done, 1)
                    tick()

        BACK = [(kind, n, g) for kind in range(3) for n in range(NT) for g in range(2)]

        def back_pe(pe, b):
            kind, n, g = BACK[b]
            pe.wait_ge(tok_done, 5 * n + (1, 3, 2)[kind])
            if b >= 4:
                pe.wait_ge(back_copied, b - 3)
            src = (khat, kb, qh)[kind]
            for hh in range(4):
                i = pe.transpose(aux[b % 4][:, hh * P:(hh + 1) * P], src[:, n, 4 * g + hh, :], ident())
            i.then_inc(back_mm, 1)

        def back_act(act, b):
            kind, n, g = BACK[b]
            act.wait_ge(back_mm, b + 1)
            dst = khT[:, n, 4 * g:4 * g + 4, :] if kind == 0 else kbqT[:, kind - 1, n, 4 * g:4 * g + 4, :]
            act.activation(dst, aux[b % 4][:].rearrange("p (h s) -> p h s", h=4), ACT.Copy).then_inc(back_copied, 1)

        def dt_pe(pe, b):
            n, g = b // 2, b % 2
            if b == 0:
                pe.wait_ge(back_copied, 12)
                pe.wait_ge(g2_sel, 1)
            for hh in range(4):
                ts = slice(n * P, (n + 1) * P)
                i = pe.matmul(aux[b][:, hh * P:(hh + 1) * P], sel_l[0:40, 4 * g + hh, ts], sel_r[0:40, ts], start=True, stop=True)
            i.then_inc(dt_mm, 1)

        def dt_dve(dve, b):
            n, g = b // 2, b % 2
            dve.wait_ge(dt_mm, b + 1)
            dve.tensor_tensor(DT[:, n, 4 * g:4 * g + 4, :], aux[b][:].rearrange("p (h s) -> p h s", h=4),
                              both(cst[:, C_DMASK:C_DMASK + P], 4), ALU.add).then_inc(dt_add, 1)

        def dt_act(act, b):
            n, g = b // 2, b % 2
            act.wait_ge(dt_add, b + 1)
            v = DT[:, n, 4 * g:4 * g + 4, :]
            act.activation(v, v, ACT.Exp).then_inc(dt_done, 1)

        def kdec_dve(dve):
            dve.wait_ge(dt_done, 2)
            dve.tensor_tensor(kdec[:], khat[:, 0], DT[:, 0, :, P - 1:P].broadcast_to([P, GH, GD]), ALU.mult).then_inc(kdec_done, 1)
            dve.wait_ge(kdec_done, 1)

        def ap_pe(pe, b):
            n, h = b // 4, 2 * (b % 4)
            if b < 4:
                pe.wait_ge(dt_add, b + 1)
            else:
                pe.wait_ge(ap_done, b - 3)
            for hh in range(2):
                i = pe.matmul(aux[b % 4][:, hh * S:(hh + 1) * S], khT[:, n, h + hh, :], kbqT[:, :, n, h + hh, :], start=True, stop=True)
            i.then_inc(ap_mm, 1)

        def ap_dve(dve, b):
            n, h = b // 4, 2 * (b % 4)
            dve.wait_ge(ap_mm, b + 1)
            dve.wait_ge(dt_done, 2 * n + 1 + (b % 4) // 2)
            for hh in range(2):
                i = dve.tensor_tensor(APT[:, n, h + hh], aux[b % 4][:, hh * S:(hh + 1) * S].rearrange("p (k s) -> p k s", k=2),
                                      both(DT[:, n, h + hh, :]), ALU.mult)
            i.then_inc(ap_done, 1)

        def level(l):
            return both(cst[:, C_LEVEL + l * P:C_LEVEL + (l + 1) * P], 4)

        def inv_banks(n, g):
            free = (0, 1) if units[of["gb"][2]]["banks"][0] else (2, 3)
            return (acc[free[0]], acc[free[1]]) if g else (aux[2], aux[3])

        def inv_pool(pool, n, between):
            for l in range(LEVELS):
                between(l)
                for g in range(2):
                    if l == 0:
                        pool.wait_ge(ap_done, 8)
                        if n:
                            pool.wait_ge(y_mm, (LEVELS * n - 1) * 2 + g + 1)
                    elif l == 1:
                        pool.wait_ge(u_done, 2 * LEVELS * n + g + 1)
                    else:
                        pool.wait_ge(y_mm, 2 * (LEVELS * n + l - 1) + g + 1)
                    pool.tensor_tensor(Bt[:, g], APT[:, n, 4 * g:4 * g + 4, 0, :], level(l), ALU.mult).then_inc(bt_done, 1)

        def inv_pe(pe, n, between):
            for l in range(LEVELS):
                e = LEVELS * n + l
                for g in range(2):
                    if l == 0:
                        pe.wait_ge(u_done, 2 * e + g + 1)
                        if n:
                            pe.wait_ge(r_copied, 6)
                        for hh in range(4):
                            i = pe.transpose(aux[g][:, hh * P:(hh + 1) * P], Um[:, g, hh, :], ident())
                    else:
                        pe.wait_ge(bt_done, 2 * e + g + 1)
                        if l == 1:
                            pe.wait_ge(y_copied, 2 * (e - 1) + g + 1)
                        else:
                            pe.wait_ge(t_done, 2 * ((LEVELS - 2) * n + l - 2) + g + 1)
                        for hh in range(4):
                            i = pe.matmul(aux[g][:, hh * P:(hh + 1) * P], Bt[:, g, hh, :], Tm[:, g, hh, :], start=True, stop=True)
                    i.then_inc(y_mm, 1)
                if l == 0:
                    continue
                between(2 * (l - 1))
                for g in range(2):
                    pe.wait_ge(y_copied, 2 * e + g + 1)
                    ty, yu = inv_banks(n, g)
                    pe.wait_ge(u_done, 2 * (e - 1) + g + 1)
                    if n == 0 and l == 1 and g:
                        for b, count in released(of["gb"][1]):
                            pe.wait_ge(acc_free[b], count)
                    if l < LEVELS - 1:
                        for hh in range(4):
                            i = pe.matmul(ty[:, hh * P:(hh + 1) * P], Um[:, g, hh, :], Yb[:, g, hh, :], start=True, stop=True)
                        i.then_inc(ty_mm, 1)
                    for hh in range(4):
                        i = pe.matmul(yu[:, hh * P:(hh + 1) * P], Yb[:, g, hh, :], Um[:, g, hh, :], start=True, stop=True)
                    i.then_inc(yu_mm, 1)
                between(2 * (l - 1) + 1)

        def inv_act(act, n, between):
            for l in range(LEVELS):
                between(l)
                e = LEVELS * n + l
                for g in range(2):
                    act.wait_ge(y_mm, 2 * e + g + 1)
                    dst = Tm if l == 0 else Yb
                    act.activation(dst[:, g], aux[g][:].rearrange("p (h s) -> p h s", h=4), ACT.Copy).then_inc(y_copied, 1)

        def inv_dve(dve, n, between):
            for l in range(LEVELS):
                between(l)
                e = LEVELS * n + l
                for g in range(2):
                    if l == 0:
                        dve.wait_ge(bt_done, 2 * e + g + 1)
                        if n:
                            dve.wait_ge(r_copied, 2)
                        dve.tensor_tensor(Um[:, g], both(cst[:, C_ID:C_ID + P], 4), Bt[:, g], ALU.subtract).then_inc(u_done, 1)
                        continue
                    if l < LEVELS - 1:
                        dve.wait_ge(ty_mm, 2 * ((LEVELS - 2) * n + l - 1) + g + 1)
                        dve.tensor_tensor(Tm[:, g], Tm[:, g], inv_banks(n, g)[0][:].rearrange("p (h s) -> p h s", h=4), ALU.subtract).then_inc(t_done, 1)
                    dve.wait_ge(yu_mm, 2 * ((LEVELS - 1) * n + l - 1) + g + 1)
                    dve.tensor_tensor(Um[:, g], Um[:, g], inv_banks(n, g)[1][:].rearrange("p (h s) -> p h s", h=4), ALU.subtract).then_inc(u_done, 1)

        wTn = kbqT[:, 1, 0]

        def heads(pe, bank, g, f):
            for hh in range(4):
                parts = f(4 * g + hh, hh)
                for j, (a, b) in enumerate(parts):
                    i = pe.matmul(bank[:, hh * P:(hh + 1) * P], a, b, start=j == 0, stop=j == len(parts) - 1)
            return i

        def res_pe(pe, n):
            base = 6 * n
            pe.wait_ge(u_done, 2 * LEVELS * (n + 1))
            if n == 0:
                pe.wait_ge(kdec_done, 1)
                for g in range(2):
                    heads(pe, aux[g], g, lambda h, hh: [(Um[:, g, hh, :], vb[:, 0, h, :])]).then_inc(r_mm, 1)
                for g in range(2):
                    pe.wait_ge(r_copied, g + 1)
                    heads(pe, aux[2 + g], g, lambda h, hh: [(APT[:, 0, h, 1, :], vnew[:, h, :])]).then_inc(r_mm, 1)
                for g in range(2):
                    heads(pe, aux[g], g, lambda h, hh: [(kdec[:, h, :], vnew[:, h, :])]).then_inc(r_mm, 1)
            else:
                for g in range(2):
                    heads(pe, aux[g], g, lambda h, hh: [(kbg[:, h, :], Um[:, g, hh, :])]).then_inc(r_mm, 1)
                for g in range(2):
                    heads(pe, aux[2 + g], g, lambda h, hh: [(kbqT[:, 1, 1, h, :], S1[:, h, :])]).then_inc(qs_mm, 1)
                for g in range(2):
                    pe.wait_ge(r_copied, base + g + 1)
                    heads(pe, aux[g], g, lambda h, hh: [(Um[:, g, hh, :], vb[:, 1, h, :]), (wTn[:, h, :], S1[:, h, :])]).then_inc(r_mm, 1)
                for g in range(2):
                    pe.wait_ge(r_copied, base + 2 + g + 1)
                    pe.wait_ge(qs_done, g + 1)
                    heads(pe, aux[2 + g], g, lambda h, hh: [(APT[:, 1, h, 1, :], vnew[:, h, :])]).then_inc(o_mm, 1)

        def res_act(act, n):
            dst = [(vnew, 1.0), (vb[:, 0], 1.0), (S1, 1.0)] if n == 0 else [(wTn, -1.0), (vnew, 1.0)]
            base = 6 * n
            for k, (d, s) in enumerate(dst):
                for g in range(2):
                    act.wait_ge(r_mm, base + 2 * k + g + 1)
                    bank = aux[g] if n or k != 1 else aux[2 + g]
                    act.activation(d[:, 4 * g:4 * g + 4, :], bank[:].rearrange("p (h d) -> p h d", h=4), ACT.Copy, scale=s).then_inc(r_copied, 1)

        def res_dve(dve):
            for g in range(2):
                dve.wait_ge(qs_mm, g + 1)
                dve.tensor_tensor(sqb[:, g, :].rearrange("p (h d) -> p h d", h=4), aux[2 + g][:].rearrange("p (h d) -> p h d", h=4),
                                  EG[:, 1, 4 * g:4 * g + 4].unsqueeze(2).broadcast_to([P, 4, GD]), ALU.mult).then_inc(qs_done, 1)
            for g in range(2):
                dve.wait_ge(o_mm, g + 1)
                dve.wait_ge(qs_done, g + 1)
                dve.tensor_tensor(vb[:, 1, 4 * g:4 * g + 4, :], aux[2 + g][:].rearrange("p (h d) -> p h d", h=4),
                                  sqb[:, g, :].rearrange("p (h d) -> p h d", h=4), ALU.add).then_inc(o_done, 1)

        def merge_act(act, n, g):
            if n == 0:
                act.wait_ge(r_copied, 3 + g)
            else:
                act.wait_ge(o_done, g + 1)
            if 8 * n + 4 * g:
                act.wait_ge(o_ss, 8 * n + 4 * g)
            for hh in range(4):
                c = 52 + 8 * n + 4 * g + hh
                act.activation(junk[:, hh * P:(hh + 1) * P], vb[:, n, 4 * g + hh, :], ACT.Square,
                               accum_out=hsum[:, c:c + 1]).then_inc(o_ss, 1)

        def merge_pool(pool, n, g):
            c = 52 + 8 * n + 4 * g
            pool.wait_ge(o_ss, 8 * n + 4 * (g + 1))
            pool.tensor_scalar(hsum[:, c:c + 4], hsum[:, c:c + 4], 1.0 / GD, EPS, ALU.mult, ALU.add)
            pool.drain()
            pool.tensor_tensor(hrms[:, c:c + 4], hsum[:, c:c + 4], half[:, 0:4], ALU.pow).then_inc(o_rms, 1)

        def merge_dve(dve, n, g):
            dve.wait_ge(o_rms, 2 * n + g + 1)
            dve.drain()
            for hh in range(4):
                h = 4 * g + hh
                o, c = vb[:, n, h, :], 52 + 8 * n + h
                dve.scalar_tensor_tensor(o, o, hrms[:, c:c + 1], zg[:, n, h * GD:(h + 1) * GD], ALU.mult, ALU.mult)
            dve.drain()
            cs = slice(g * 512, (g + 1) * 512)
            dve.scalar_tensor_tensor(xn[:, n, cs], xn[:, n, cs], 0.5, vb[:, n, 4 * g:4 * g + 4, :].rearrange("p h d -> p (h d)"),
                                     ALU.mult, ALU.add).then_inc(merged_done, 1)

        def plain_add(dve, tag, g):
            for t in range(NT):
                wait_piece(dve, tag, g, t)
                b, cs = units[half_unit(tag, g)]["banks"][t], slice(g * 512, (g + 1) * 512)
                dve.tensor_tensor(x[:, t, cs], x[:, t, cs], acc[b][:], ALU.add).then_inc(acc_free[b], 1)

        def wait_added(eng, tag, g, t):
            b, n = released(of[tag][(g + 1) * len(of[tag]) // 2 - 1])[t]
            eng.wait_ge(acc_free[b], n)

        GATES = [("z", j) for j in range(4)] + [("ga", j) for j in range(4)] + [("gb", j) for j in range(4)]

        def gate_pair(q):
            return GATES[q - 1] if q >= 2 and q % 2 == 0 else None

        def dsa_parts(i):
            return [(6 + q // 4, q % 4) for q in range(3 * i // 2, 3 * (i + 1) // 2) if q < 6 * 4]

        block = ctx.enter_context(nc.Block())

        @block.sync
        def _(sp):
            xr = w["x"][0].rearrange("(t p) d -> p t d", p=P)
            for t in range(NT):
                sp.dma_start(x[:, t, :], xr[:, t, :]).then_inc(x_in, 16)
            sp.dma_start(cst[:, 0:P], consts[:, 0:P]).then_inc(id_in, 16)
            sp.dma_start(sm[:, 0:V_NARROW], small[:, 0:V_NARROW]).then_inc(gain_in, 16)
            gpos = {of["fk"][0]: ("g_mix_post", 0), of["mo"][0]: ("g_mem_post", 4), of["ff2"][0]: ("g_ff_post", 8)}
            for u in range(NU):
                if u == 2:
                    sp.dma_start(sm[:, V_NARROW:], small[:, V_NARROW:]).then_inc(small_in, 16)
                    sp.dma_start(cst[:, P:], consts[:, P:]).then_inc(cst_in, 16)
                if u == 3:
                    sp.dma_start(mem[:], w["mem"][0].rearrange("(t p) d -> p t d", p=P)).then_inc(mem_in, 16)
                if u == 5:
                    sp.dma_start(relb[:], rel).then_inc(rel_in, 16)
                if u in gpos:
                    name, n = gpos[u]
                    if n:
                        sp.wait_ge(x_done, n)
                    sp.dma_start(gpost[:], w[name].broadcast_to([P, D])).then_inc(gpost_in, 16)
                if u >= RAW_SLOTS:
                    sp.wait_ge(w_lo_done, 4 * (u - RAW_SLOTS + 1))
                dst = w_raw[u % RAW_SLOTS][:].rearrange("p (c n) -> p c n", c=units[u]["src"].shape[1])
                sp.dma_start(dst, units[u]["src"]).then_inc(w_loaded[u % RAW_SLOTS], 16)
            for g in range(2):
                for t in range(NT):
                    wait_added(sp, "down", g, t)
                    cs = slice(g * 512, (g + 1) * 512)
                    sp.dma_start(out[t * P:(t + 1) * P, cs], x[:, t, cs]).then_inc(stored, 16)
            sp.wait_ge(stored, 16 * 2 * NT)

        @block.gpsimd
        def _(pool):
            rstd_pool(pool, "mix")
            rstd_pool(pool, "mem")
            pool.wait_ge(gate_ct, 4)
            pool.wait_ge(cst_in, 16)
            pool.tensor_tensor(sel_l[:], sel_a[:].unsqueeze(1).broadcast_to([104, 8, S]),
                               cst[0:104, C_SEL:C_SEL + 8].unsqueeze(2).broadcast_to([104, 8, S]), ALU.mult).then_inc(sel_done, 1)
            rstd_y_pool(pool, 0)
            rstd_y_pool(pool, 1)
            for n in ("p_out", "mpre", "p_mo", "ff", "p_ff2"):
                rstd_pool(pool, n, behind=n.startswith("p_"))
            rstd_pool(pool, "mix2")
            gates2_pool(pool)
            conv_pool(pool, 0)
            conv_pool(pool, 1)
            aqk_pool(pool)
            for j in range(2, 12):
                conv_pool(pool, j)
            tok_rms_pool(pool)
            inv_pool(pool, 0, lambda l: None)
            inv_pool(pool, 1, lambda l: merge_pool(pool, 0, l - 3) if l in (3, 4) else None)
            merge_pool(pool, 1, 0)
            merge_pool(pool, 1, 1)
            rstd_pool(pool, "mlp2")

        @block.scalar
        def _(act):
            def x_piece(g, t):
                if g == 0:
                    act.wait_ge(x_in, 16 * NT)
            nt_act_stats(act, "mix", x, x_piece)
            for u in range(AHEAD):
                unit_hi(act, u)
            act.wait_ge(gain_in, 16)
            nt_act(act, "mix", h_hi)
            act_group(act, "fq")
            act.wait_ge(small_in, 16)
            act.activation(ws_hi[:], ws_raw, ACT.Copy).then_inc(ws_hi_done, 1)
            act_group(act, "fk")
            narrow_act(act, 8)
            act_unit(act, "fv", 0)
            act_unit(act, "fv", 1)
            advance_hi(act, of["cq"][0])
            N.wait(act, gate_v)
            act.activation(gate8[:, 2, :], gate8[:, 1, :], ACT.Exp).then_inc(gate_a, 1)
            N.wait(act, gate_a)
            act.activation(gate8[:, 3, :], gate8[:, 2, :], ACT.Ln, bias=1.0).then_inc(gate_a, 1)
            evacuate(act, "cq", 0)
            advance_hi(act, of["cq"][1])
            act.wait_ge(mem_in, 16)
            nt_act_stats(act, "mem", mem)
            evacuate(act, "cq", 1)
            act_group(act, "ck")
            nt_act(act, "mem", m_hi)
            for j in range(2):
                act_unit(act, "cv", j)

            def between(i):
                if i // 4 < len(MEMU):
                    tag, j = MEMU[i // 4]
                    advance_hi(act, of[tag][j], i % 4)
                if i % 4 == 0 and i:
                    evacuate(act, *MEMU[i // 4 - 1])
                if i == len(FOX) // 2 + 3:
                    act.wait_ge(y_done, len(FOX) // 2)
                    for t in range(NT):
                        square(act, "y", 0, t, y[:, t, 0:512])
            attention_act(act, FOX, 0, between)
            act.wait_ge(y_done, len(FOX))
            for t in range(NT):
                square(act, "y", 1, t, y[:, t, 512:D])
            nt_act(act, "y", h_hi)
            for u in of["out"]:
                if u == of["out"][-1]:
                    post_stats(act, "p_out", "out", 0)
                advance_hi(act, u)
            post_stats(act, "p_out", "out", 1)
            nt_act_stats(act, "mpre", x, lambda g, t: N.wait(act, x_done))
            nt_act(act, "mpre", h_hi)
            act_group(act, "mq")
            attention_act(act, MEM, I_MEM, lambda i: None)
            nt_act(act, "memo", h_hi)
            for u in of["mo"]:
                if u == of["mo"][-1]:
                    post_stats(act, "p_mo", "mo", 0)
                advance_hi(act, u)
            post_stats(act, "p_mo", "mo", 1)
            nt_act_stats(act, "ff", x, lambda g, t: N.wait(act, x_done))
            nt_act(act, "ff", h_hi)
            for j in range(16 + 2):
                if j < 16:
                    advance_hi(act, of["ff1"][j])
                if 1 <= j <= 16:
                    hid_act_relu(act, "ff1", j - 1)
                if j >= 2:
                    hid_act_hi(act, "ff1", j - 2)
            for u in of["ff2"]:
                if u == of["ff2"][-1]:
                    post_stats(act, "p_ff2", "ff2", 0)
                advance_hi(act, u)
            post_stats(act, "p_ff2", "ff2", 1)
            nt_act_stats(act, "mix2", x, lambda g, t: N.wait(act, x_done))
            nt_act(act, "mix2", h_hi)
            act_unit(act, "akv", 0)
            act_unit(act, "akv", 1)
            narrow_act(act, 88)
            act_unit(act, "iq", 0)
            act_unit(act, "iq", 1)
            ik_act(act)
            act_unit(act, "aq", 0)
            gates2_act(act)
            idx_tr_act(act)
            act_unit(act, "aq", 1)
            gates2_act_eg(act)

            def between(j):
                if j % 2:
                    advance_hi(act, of["aq"][2 + j // 8], j // 2 % 4)
            idx_scores(act, "act", between)
            evacuate(act, "aq", 3)

            def qkv_tick(j):
                advance_hi(act, of["qkv"][j])
                qkv_act_in(act, j)
                if j >= 2:
                    qkv_act_tanh(act, j - 2)
            for j in range(6):
                qkv_tick(j)
                if j in (0, 1):
                    aqk_act_squares(act, j)
                if j in (3, 4):
                    aqk_act_scale(act, j - 3)
            aqk_act(act)

            def between(i):
                for j, q in dsa_parts(i):
                    advance_hi(act, of["qkv"][j], q)
                    if j > 6 and q == 0:
                        qkv_act_in(act, j - 1)
                    if j > 6 and q == 2:
                        qkv_act_tanh(act, j - 3)
            attention_act(act, DSA, I_DSA, between)
            qkv_act_in(act, 11)
            qkv_act_tanh(act, 9)

            def gate_tick(q):
                advance_hi(act, of[GATES[q][0]][GATES[q][1]])
                if gate_pair(q):
                    gate_act(act, *gate_pair(q))
            for b in range(12):
                tok_act(act, b)
                if b == 7:
                    act.wait_ge(qkv_done, 12)
                if b % 3 == 2:
                    gate_tick(b // 3)
                if b in (2, 5):
                    qkv_act_tanh(act, 10 + b // 3)
            for q in range(4, 7):
                gate_tick(q)
            for b in range(12):
                back_act(act, b)
                if b % 4 == 3:
                    gate_tick(7 + b // 4)
            for b in range(4):
                dt_act(act, b)

            def between(l):
                if l == 1:
                    gate_tick(10)
                if l == 3:
                    gate_tick(11)
                if l == 5:
                    gate_act(act, *GATES[11])
            inv_act(act, 0, between)
            res_act(act, 0)

            def between(l):
                if l in (1, 2):
                    merge_act(act, 0, l - 1)
            inv_act(act, 1, between)
            res_act(act, 1)
            for g in range(2):
                merge_act(act, 1, g)
            nt_act(act, "merged", h_hi)
            for u in of["out2"]:
                advance_hi(act, u)
            nt_act_stats(act, "mlp2", x, lambda g, t: wait_added(act, "out2", g, t))
            nt_act(act, "mlp2", h_hi)
            for j in range(16 + 2):
                if j < 16:
                    advance_hi(act, of["up"][j])
                if 1 <= j <= 16:
                    hid_act_relu(act, "up", j - 1)
                if j >= 2:
                    hid_act_hi(act, "up", j - 2)
            for u in of["down"]:
                advance_hi(act, u)

        @block.vector
        def _(dve):
            dve.memset(half[:], -0.5).then_inc(set_done, 1)
            dve.memset(sel_a[:], 1.0)
            dve.memset(sel_r[:], 1.0)
            dve.wait_ge(id_in, 16)
            nt_dve_diag(dve, "mix")
            for u in range(AHEAD):
                unit_lo(dve, u)
            nt_dve(dve, "mix", h_hi, h_lo)
            for u in of["fq"]:
                advance_lo(dve, u)
            dve.wait_ge(ws_hi_done, 1)
            dve.tensor_tensor(ws_lo[:], ws_raw, ws_hi[:].bitcast(F32), ALU.subtract).then_inc(ws_lo_done, 1)
            for tag in ("fk", "fv"):
                for u in of[tag]:
                    advance_lo(dve, u)
            N.wait(dve, narrow_done)
            v8 = [gate8[:, j, :].rearrange("p (t h) -> p t h", t=NT) for j in range(5)]
            dve.tensor_tensor(v8[0], aux[1][:, 0:16].rearrange("p (t h) -> p t h", t=NT),
                              bc8[:, 0, :].unsqueeze(1).broadcast_to([P, NT, 8]), ALU.add)
            dve.drain()
            dve.scalar_tensor_tensor(v8[1], v8[0], -1.0, v8[0], ALU.mult, ALU.min).then_inc(gate_v, 1)
            advance_lo(dve, of["cq"][0])
            dve.wait_ge(gate_a, 2)
            dve.scalar_tensor_tensor(v8[4], v8[0], 0.0, v8[3], ALU.min, ALU.subtract).then_inc(gate_v, 1)
            dve.wait_ge(rel_in, 16)
            dve.memset(relb[0:CHUNK, :, 3 * CHUNK:4 * CHUNK], NEG).then_inc(rel_done, 1)
            advance_lo(dve, of["cq"][1])
            nt_dve_diag(dve, "mem")
            advance_lo(dve, of["ck"][0])
            N.wait(dve, gate_tr)
            dve.tensor_tensor_scan(cum[:], sel_a[0:8, :], aux[2][0:8, 0:S], 0.0, ALU.mult, ALU.add)
            dve.drain()
            for r in (0, 64):
                dve.tensor_scalar(sel_r[r:r + 8, :], cum[:], -1.0, None, ALU.mult).then_inc(gate_ct, 1)
                dve.tensor_copy(sel_a[r + 32:r + 40, :], cum[:]).then_inc(gate_ct, 1)
            advance_lo(dve, of["ck"][1])
            nt_dve(dve, "mem", m_hi, m_lo)
            for u in of["cv"]:
                advance_lo(dve, u)

            def between(i):
                if 1 <= i <= 4 * len(MEMU):
                    tag, j = MEMU[(i - 1) // 4]
                    advance_lo(dve, of[tag][j], (i - 1) % 4)
                if i == len(FOX) // 2 + 3:
                    nt_dve_diag(dve, "y", 0)
            attention_dve(dve, FOX, 0, between)
            nt_dve_diag(dve, "y", 1)
            nt_dve(dve, "y", h_hi, h_lo)
            for u in of["out"]:
                if u == of["out"][-1]:
                    for t in range(NT):
                        post_gain(dve, "p_out", "out", 1, 0, t)
                advance_lo(dve, u)
            post_add(dve, "p_out", "out", 1)
            nt_dve_diag(dve, "mpre")
            nt_dve(dve, "mpre", h_hi, h_lo)
            for u in of["mq"]:
                advance_lo(dve, u)
            attention_dve(dve, MEM, I_MEM, lambda i: None)
            nt_dve(dve, "memo", h_hi, h_lo)
            for u in of["mo"]:
                if u == of["mo"][-1]:
                    for t in range(NT):
                        post_gain(dve, "p_mo", "mo", 2, 0, t)
                advance_lo(dve, u)
            post_add(dve, "p_mo", "mo", 2)
            nt_dve_diag(dve, "ff")
            nt_dve(dve, "ff", h_hi, h_lo)
            for j in range(16 + 2):
                if j < 16:
                    advance_lo(dve, of["ff1"][j])
                if 1 <= j <= 16:
                    hid_dve_sq(dve, "ff1", j - 1)
                if j >= 2:
                    hid_dve_lo(dve, "ff1", j - 2)
            for u in of["ff2"]:
                if u == of["ff2"][-1]:
                    for t in range(NT):
                        post_gain(dve, "p_ff2", "ff2", 3, 0, t)
                advance_lo(dve, u)
            post_add(dve, "p_ff2", "ff2", 3)
            dve.memset(cin[:, :, :, 0:3], 0.0)
            dve.tensor_scalar(conv_h[:], sm[:, V_CONV:].rearrange("p (c k) -> p c k", k=4), 0.5, None, ALU.mult)
            dve.tensor_scalar(gq4[:], ghead[:, 2, :], 0.25, None, ALU.mult).then_inc(set2_done, 1)
            nt_dve_diag(dve, "mix2")
            nt_dve(dve, "mix2", h_hi, h_lo)
            advance_lo(dve, of["akv"][0])
            advance_lo(dve, of["akv"][1])
            advance_lo(dve, of["iq"][0])
            gates2_dve_in(dve)
            advance_lo(dve, of["iq"][1])
            idx_rope_dve(dve)
            advance_lo(dve, of["aq"][0])
            gates2_dve(dve)
            advance_lo(dve, of["aq"][1])
            gates2_dve_sum(dve)

            def between(j):
                if j % 2 == 0 and j or j == NT * IH - 1:
                    q = (j - 1) // 2
                    advance_lo(dve, of["aq"][2 + q // 4], q % 4)
            idx_scores(dve, "dve", between)
            ticks = [0]

            def qkv_tick(j):
                advance_lo(dve, of["qkv"][j])
                if j >= 1:
                    conv_dve(dve, j - 1)
                if j >= 3:
                    qkv_dve(dve, j - 3)

            def tick():
                qkv_tick(ticks[0])
                ticks[0] += 1
            topk_dve(dve, tick)
            aqk_dve(dve, tick)

            def between(i):
                for j, q in dsa_parts(i - 1) if i else []:
                    advance_lo(dve, of["qkv"][j], q)
                    if q == 1:
                        conv_dve(dve, j - 1)
                    if q == 3:
                        qkv_dve(dve, j - 3)
            attention_dve(dve, DSA, I_DSA, between)
            qkv_dve(dve, 9)
            conv_dve(dve, 11)

            def gate_tick(q):
                advance_lo(dve, of[GATES[q][0]][GATES[q][1]])
                if gate_pair(q):
                    gate_dve(dve, *gate_pair(q))
            for b in range(12):
                tok_dve(dve, b)
                if b % 3 == 2:
                    gate_tick(b // 3)
                if b in (2, 5):
                    qkv_dve(dve, 10 + b // 3)
            ticks = [4]

            def tick():
                gate_tick(ticks[0])
                ticks[0] += 1
            tok_scale_dve(dve, tick)
            for q in range(7, 10):
                gate_tick(q)
            for b in range(4):
                dt_dve(dve, b)
            kdec_dve(dve)
            for b in range(8):
                ap_dve(dve, b)

            def between(l):
                if l == 1:
                    gate_tick(10)
                if l == 3:
                    gate_tick(11)
                if l == 5:
                    gate_dve(dve, *GATES[11])
            inv_dve(dve, 0, between)

            def between(l):
                if l in (1, 2):
                    gate_norm_dve(dve, l - 1)
                if l in (4, 5):
                    merge_dve(dve, 0, l - 4)
            inv_dve(dve, 1, between)
            res_dve(dve)
            for g in range(2):
                merge_dve(dve, 1, g)
            nt_dve(dve, "merged", h_hi, h_lo)
            for u in of["out2"]:
                if u == of["out2"][-1]:
                    plain_add(dve, "out2", 0)
                advance_lo(dve, u)
            plain_add(dve, "out2", 1)
            nt_dve_diag(dve, "mlp2")
            nt_dve(dve, "mlp2", h_hi, h_lo)
            for j in range(16 + 2):
                if j < 16:
                    advance_lo(dve, of["up"][j])
                if 1 <= j <= 16:
                    hid_dve_sq(dve, "up", j - 1)
                if j >= 2:
                    hid_dve_lo(dve, "up", j - 2)
            for u in of["down"]:
                if u == of["down"][-1]:
                    plain_add(dve, "down", 0)
                advance_lo(dve, u)
            plain_add(dve, "down", 1)

        @block.tensor
        def _(pe):
            nt_count = [0]

            def nt(n, src):
                nt_pe(pe, n, src)
                nt_count[0] += 1

            def mm(tag, *js, hi=h_hi, lo=h_lo, fresh=False, parts=range(4)):
                for j in js or range(len(of[tag])):
                    first = fresh and j < (2 if units[of[tag][j]]["form"] == "A" else 1)
                    unit_mm(pe, of[tag][j], hi, lo, nt_count[0] - 1 if first else None, parts)

            def hidden_mm(tag, base):
                for j in range(len(of[tag])):
                    if j < len(of[tag]) // 2:
                        pe.wait_ge(hid_lo_done, base + 2 * j + 2)
                    mm(tag, j, hi=hid_hi, lo=hid_lo)

            pe.wait_ge(x_in, 16 * NT)
            pe.wait_ge(id_in, 16)
            nt("mix", x)
            mm("fq", fresh=True)
            mm("fk")
            pe.wait_ge(ws_lo_done, 1)
            narrow_mm(pe, 0, 8)
            mm("fv", 0)
            narrow_tr(pe, 8)
            mm("fv", 1)
            mm("cq")
            mm("ck", 0)
            pe.wait_ge(gate_v, 2)
            for t in range(NT):
                i = pe.transpose(aux[2][0:8, t * P:(t + 1) * P], gate8[:, 4, t * 8:(t + 1) * 8], ident())
            i.then_inc(gate_tr, 1)
            mm("ck", 1)
            pe.wait_ge(gate_ct, 1)
            pe.wait_ge(mem_in, 16)
            nt("mem", mem)
            mm("cv")
            pe.wait_ge(nt_lo, KC * nt_count[0])
            pe.wait_ge(sel_done, 1)
            pe.wait_ge(cst_in, 16)

            def between(i):
                if i // 4 < len(MEMU):
                    tag, j = MEMU[i // 4]
                    mm(tag, j, hi=m_hi, lo=m_lo, parts=[i % 4])
            wait_copied(pe, "cv")
            attention_pe(pe, FOX, 0, between)
            pe.wait_ge(l_done, len(FOX))
            nt_pe(pe, "y", y, (0, 1))
            pe.wait_ge(y_done, len(FOX))
            nt_pe(pe, "y", y, (2, 3))
            nt_count[0] += 1
            mm("out", fresh=True)
            nt("mpre", x)
            mm("mq", fresh=True)
            wait_copied(pe, "mq")
            attention_pe(pe, MEM, I_MEM, lambda i: None)
            pe.wait_ge(y_done, len(FOX) + len(MEM))
            nt("memo", y)
            mm("mo", fresh=True)
            nt("ff", x)
            mm("ff1", fresh=True)
            hidden_mm("ff2", 0)
            nt("mix2", x)
            mm("akv", fresh=True)
            narrow_mm(pe, 8, 88)
            mm("iq", 0)
            narrow_tr(pe, 88)
            mm("iq", 1)
            mm("aq", 0)
            gates2_pe(pe)
            idx_tr_pe(pe)
            mm("aq", 1)
            gates2_pe_tm(pe)

            def between(j):
                if j % 2:
                    mm("aq", 2 + j // 8, parts=[j // 2 % 4])
            idx_scores(pe, "pe", between)
            mm("qkv", *range(6))
            aqk_pe(pe, None)
            pe.wait_ge(aT_copied, 5)
            wait_copied(pe, "akv")

            def between(i):
                for j, q in dsa_parts(i):
                    mm("qkv", j, parts=[q])
            attention_pe(pe, DSA, I_DSA, between)
            pe.wait_ge(y_done, I_DSA + len(DSA))
            for b in range(12):
                tok_pe(pe, b)
                if b % 3 == 2:
                    mm("z", b // 3)
            mm("ga", 0, 1, 2)
            for b in range(12):
                back_pe(pe, b)
                if b == 3:
                    mm("ga", 3)
                if b == 7:
                    mm("gb", 0)
                if b == 11:
                    mm("gb", 1)
            for b in range(4):
                dt_pe(pe, b)
            for b in range(8):
                ap_pe(pe, b)

            def between(slot):
                if slot < 8:
                    mm("gb", 2 + slot // 4, parts=[slot % 4])
            inv_pe(pe, 0, between)
            res_pe(pe, 0)
            wait_copied(pe, "gb")
            inv_pe(pe, 1, lambda slot: None)
            res_pe(pe, 1)
            pe.wait_ge(r_copied, 10)
            for g in range(2):
                pe.wait_ge(merged_done, NT + g + 1)
                nt_pe(pe, "merged", xn, (2 * g, 2 * g + 1))
            nt_count[0] += 1
            mm("out2", fresh=True)
            nt("mlp2", x)
            mm("up", fresh=True)
            hidden_mm("down", 16)


_STREAMED = ["x", "mem", "w_in", "w_mk", "w_mv", "w_out", "w_mq", "w_mo", "w_ff1", "w_ff2", "g_mix_post", "g_mem_post",
             "g_ff_post", "w_in_2", "w_out_2", "w_mlp_up_2", "w_mlp_down_2"]


def kernel(**inputs):
    import concourse.bacc as _bacc
    from concourse.bass_utils import run_bass_kernel_spmd as _run

    a = {name: np.asarray(v) for name, v in inputs.items()}
    nc = _bacc.Bacc("TRN2", target_bir_lowering=False, num_devices=1)
    arrays = {f"in_{name}": np.ascontiguousarray(a[name]) for name in _STREAMED}
    arrays["in_constants"] = constants()
    arrays["in_small"] = small_inputs(a)
    arrays["in_rel_rows"] = rel_rows(a["rel_bias"])
    aps = {name: nc.dram_tensor(name, v.shape, mybir.dt.from_np(v.dtype), kind="ExternalInput").ap()
           for name, v in arrays.items()}
    out = nc.dram_tensor("out_dram", (S, D), F32, kind="ExternalOutput").ap()
    build_program(nc, {name: aps[f"in_{name}"] for name in _STREAMED}, aps["in_constants"], aps["in_small"],
                  aps["in_rel_rows"], out)
    r = _run(nc, [arrays], core_ids=[0])
    return r.results[0]["out_dram"].reshape(1, S, D)
```
